# Optimizing a Trainium2 kernel written in Bass

```python
import functools
import jax, jax.numpy as jnp
from jax import lax
import numpy as np
import math

D_MODEL = 1024
BATCH = 1
SEQ = 512
DEPTH = 1

HEAD_DIM = 64
GROUP_WIDTH = D_MODEL // 4
MIX_WIDTH = 4 * GROUP_WIDTH
N_GROUP_HEADS = GROUP_WIDTH // HEAD_DIM
SHORT_CONV_K = 3
DSWA_CONFIGS = ((128, 1), (512, 4), (2048, 16))
POOL_WINDOWS = (2, 4, 8, 16)
POOL_GROUP = GROUP_WIDTH // len(POOL_WINDOWS)
ROPE_THETA = 500000.0
ROPE_DIM = HEAD_DIM // 4
Q_BLOCK = 128
MEM_LEN = 256
XA_HEADS = 4
XA_HEAD_DIM = D_MODEL // XA_HEADS
D_FF = ((8 * D_MODEL // 3 + 127) // 128) * 128
FFN_CONV_K = 3
RMS_EPS = 1e-6
NEG_INF = -1e30
FORGET_BIAS_INIT = 3.0
N_IN = 3 * GROUP_WIDTH + 3 * GROUP_WIDTH + 3 * GROUP_WIDTH + N_GROUP_HEADS + GROUP_WIDTH


def rms_norm(t, g):
    tf = t.astype(jnp.float32)
    y = tf * lax.rsqrt(jnp.mean(tf * tf, axis=-1, keepdims=True) + RMS_EPS)
    return (y * g.astype(jnp.float32)).astype(t.dtype)

def causal_depthwise_conv(t, w):
    K, C = w.shape
    return lax.conv_general_dilated(
        t, w.astype(t.dtype)[:, None, :], window_strides=(1,), padding=((K - 1, 0),),
        dimension_numbers=("NWC", "WIO", "NWC"), feature_group_count=C)

def to_heads(t):
    B, S, W = t.shape
    return t.reshape(B, S, W // HEAD_DIM, HEAD_DIM).transpose(0, 2, 1, 3)

def from_heads(t):
    B, H, S, dh = t.shape
    return t.transpose(0, 2, 1, 3).reshape(B, S, H * dh)

def rope_tables(positions):
    inv_freq = ROPE_THETA ** (-jnp.arange(0, ROPE_DIM, 2, dtype=jnp.float32) / ROPE_DIM)
    ang = positions.astype(jnp.float32)[:, None, :, None] * inv_freq
    return jnp.cos(ang), jnp.sin(ang)

def apply_partial_rope(t, cos, sin):
    tf = t.astype(jnp.float32)
    r1, r2 = jnp.split(tf[..., :ROPE_DIM], 2, axis=-1)
    rot = jnp.concatenate([r1 * cos - r2 * sin, r2 * cos + r1 * sin], axis=-1)
    return jnp.concatenate([rot, tf[..., ROPE_DIM:]], axis=-1).astype(t.dtype)

def short_conv_mixer(p, w_conv):
    h, b_gate, c_gate = jnp.split(p, 3, axis=-1)
    return b_gate * causal_depthwise_conv(c_gate * h, w_conv)

def dilated_attention(q, k, v):
    B, H, S, dh = q.shape
    nb = S // Q_BLOCK
    qb = q.reshape(B, H, nb, Q_BLOCK, dh).transpose(2, 0, 1, 3, 4)
    kf = k.astype(jnp.float32)
    vf = v.astype(jnp.float32)
    scale = dh ** -0.5

    def block(args):
        i, qi = args
        t = i * Q_BLOCK + jnp.arange(Q_BLOCK)
        qs = qi.astype(jnp.float32) * scale
        scores, values = [], []
        for window, dil in DSWA_CONFIGS:
            idx = t[:, None] - dil * jnp.arange(window // dil + 1)[None, :]
            idxc = jnp.maximum(idx, 0)
            kg = kf[:, :, idxc]
            s = jnp.einsum("bhqd,bhqnd->bhqn", qs, kg)
            scores.append(jnp.where(idx >= 0, s, NEG_INF))
            values.append(vf[:, :, idxc])
        m = functools.reduce(jnp.maximum, [s.max(axis=-1, keepdims=True) for s in scores])
        num, den = 0.0, 0.0
        for s, vg in zip(scores, values):
            e = jnp.exp(s - m)
            num = num + jnp.einsum("bhqn,bhqnd->bhqd", e, vg)
            den = den + e.sum(axis=-1, keepdims=True)
        return num / den

    o = lax.map(block, (jnp.arange(nb), qb))
    return o.transpose(1, 2, 0, 3, 4).reshape(B, H, S, dh).astype(q.dtype)

def dilated_mixer(p, cos, sin):
    q, k, v = [to_heads(t) for t in jnp.split(p, 3, axis=-1)]
    q = apply_partial_rope(q, cos, sin)
    k = apply_partial_rope(k, cos, sin)
    return from_heads(dilated_attention(q, k, v))

def forgetting_attention(q, k, v, c):
    B, H, S, dh = q.shape
    nb = S // Q_BLOCK
    qb = q.reshape(B, H, nb, Q_BLOCK, dh).transpose(2, 0, 1, 3, 4)
    cb = c.reshape(B, H, nb, Q_BLOCK).transpose(2, 0, 1, 3)
    kf = k.astype(jnp.float32)
    vf = v.astype(jnp.float32)
    kpos = jnp.arange(S)
    scale = dh ** -0.5

    def block(args):
        i, qi, ci = args
        t = i * Q_BLOCK + jnp.arange(Q_BLOCK)
        s = jnp.einsum("bhqd,bhkd->bhqk", qi.astype(jnp.float32) * scale, kf)
        s = s + ci[..., None] - c[:, :, None, :]
        s = jnp.where(kpos[None, :] <= t[:, None], s, NEG_INF)
        return jnp.einsum("bhqk,bhkd->bhqd", jax.nn.softmax(s, axis=-1), vf)

    o = lax.map(block, (jnp.arange(nb), qb, cb))
    return o.transpose(1, 2, 0, 3, 4).reshape(B, H, S, dh).astype(q.dtype)

def forgetting_mixer(p, b_f):
    G = GROUP_WIDTH
    q, k, v = to_heads(p[..., :G]), to_heads(p[..., G:2 * G]), to_heads(p[..., 2 * G:3 * G])
    logf = jax.nn.log_sigmoid(p[..., 3 * G:].astype(jnp.float32) + b_f.astype(jnp.float32))
    c = jnp.cumsum(logf, axis=1).transpose(0, 2, 1)
    return from_heads(forgetting_attention(q, k, v, c))

def pool_mixer(p, w_pool, scale):
    B, S, _ = p.shape
    pf = p.astype(jnp.float32).reshape(B, S, len(POOL_WINDOWS), POOL_GROUP)
    cs = jnp.cumsum(pf, axis=1)
    cs0 = jnp.concatenate([jnp.zeros_like(cs[:, :1]), cs], axis=1)
    t = jnp.arange(S)
    outs = []
    for g, w in enumerate(POOL_WINDOWS):
        upper = cs0[:, 1:, g]
        lower = cs0[:, jnp.maximum(t + 1 - w, 0), g]
        cnt = jnp.minimum(t + 1, w).astype(jnp.float32)[None, :, None]
        outs.append((upper - lower) / cnt - pf[:, :, g])
    z = jnp.stack(outs, axis=2)
    y = jnp.einsum("bsgc,gcd->bsgd", z, w_pool.astype(jnp.float32)).reshape(B, S, GROUP_WIDTH)
    return (y * scale.astype(jnp.float32)).astype(p.dtype)

def memory_cross_attention(xn, memn, w_q, w_kv, w_o):
    B, S, D = xn.shape
    M = memn.shape[1]
    q = (xn @ w_q).reshape(B, S, XA_HEADS, XA_HEAD_DIM)
    k, v = jnp.split(memn @ w_kv, 2, axis=-1)
    k = k.reshape(B, M, XA_HEADS, XA_HEAD_DIM)
    v = v.reshape(B, M, XA_HEADS, XA_HEAD_DIM)
    s = jnp.einsum("bshd,bmhd->bhsm", q.astype(jnp.float32), k.astype(jnp.float32)) * XA_HEAD_DIM ** -0.5
    o = jnp.einsum("bhsm,bmhd->bshd", jax.nn.softmax(s, axis=-1), v.astype(jnp.float32))
    return o.reshape(B, S, D).astype(xn.dtype) @ w_o

def conv_ffn(xn, w_up, w_conv, w_down):
    u = causal_depthwise_conv(xn @ w_up, w_conv)
    a, g = jnp.split(u, 2, axis=-1)
    return (a * jax.nn.silu(g)) @ w_down

def first_inputs(seed: int = 0) -> dict:
    key = jax.random.key(seed)
    ks = jax.random.split(key, 24)
    f32 = jnp.float32
    nrm = lambda k, shape, s: jax.random.normal(k, shape, f32) * s
    L, D, G = DEPTH, D_MODEL, GROUP_WIDTH
    x = jax.random.normal(ks[0], (BATCH, SEQ, D), f32)
    mem = jax.random.normal(ks[1], (BATCH, MEM_LEN, D), f32)
    offset = jax.random.randint(ks[2], (BATCH, 1), 0, 1024, dtype=jnp.int32)
    positions = (jnp.arange(SEQ, dtype=jnp.int32)[None, :] + offset).astype(jnp.int32)
    return {
        "x": x,
        "mem": mem,
        "positions": positions,
        "g_mix": 1.0 + nrm(ks[3], (L, D), 0.02),
        "w_in": nrm(ks[4], (L, D, N_IN), D ** -0.5),
        "b_forget": FORGET_BIAS_INIT + nrm(ks[5], (L, N_GROUP_HEADS), 0.1),
        "w_sconv": nrm(ks[6], (L, SHORT_CONV_K, G), SHORT_CONV_K ** -0.5),
        "w_pool": nrm(ks[7], (L, len(POOL_WINDOWS), POOL_GROUP, POOL_GROUP), POOL_GROUP ** -0.5),
        "pool_scale": 1.0 + nrm(ks[8], (L, G), 0.02),
        "w_out": nrm(ks[9], (L, MIX_WIDTH, D), MIX_WIDTH ** -0.5),
        "g_xa": 1.0 + nrm(ks[10], (L, D), 0.02),
        "g_mem": 1.0 + nrm(ks[11], (L, D), 0.02),
        "w_xq": nrm(ks[12], (L, D, D), D ** -0.5),
        "w_xkv": nrm(ks[13], (L, D, 2 * D), D ** -0.5),
        "w_xo": nrm(ks[14], (L, D, D), D ** -0.5),
        "g_ffn": 1.0 + nrm(ks[15], (L, D), 0.02),
        "w_up": nrm(ks[16], (L, D, 2 * D_FF), D ** -0.5),
        "w_ffconv": nrm(ks[17], (L, FFN_CONV_K, 2 * D_FF), FFN_CONV_K ** -0.5),
        "w_down": nrm(ks[18], (L, D_FF, D), D_FF ** -0.5),
        "g_final": 1.0 + nrm(ks[19], (D,), 0.02),
    }

def first_block(x, mem, positions, g_mix, w_in, b_forget, w_sconv, w_pool, pool_scale, w_out,
              g_xa, g_mem, w_xq, w_xkv, w_xo, g_ffn, w_up, w_ffconv, w_down, g_final):
    G = GROUP_WIDTH
    cos, sin = rope_tables(positions)
    h = x
    for l in range(DEPTH):
        xn = rms_norm(h, g_mix[l])
        proj = xn @ w_in[l]
        pa, pb, pc, pd = jnp.split(proj, [3 * G, 6 * G, 9 * G + N_GROUP_HEADS], axis=-1)
        ya = short_conv_mixer(pa, w_sconv[l])
        yb = dilated_mixer(pb, cos, sin)
        yc = forgetting_mixer(pc, b_forget[l])
        yd = pool_mixer(pd, w_pool[l], pool_scale[l])
        h = h + jnp.concatenate([ya, yb, yc, yd], axis=-1) @ w_out[l]
        h = h + memory_cross_attention(rms_norm(h, g_xa[l]), rms_norm(mem, g_mem[l]),
                                       w_xq[l], w_xkv[l], w_xo[l])
        h = h + conv_ffn(rms_norm(h, g_ffn[l]), w_up[l], w_ffconv[l], w_down[l])
    return rms_norm(h, g_final)


DEPTH_2 = 2

N_A = DEPTH_2 // 2
N_B = DEPTH_2 - N_A
CHUNK = 128
D_GATE = D_MODEL
N_GROUPS = 8
GROUP_DIM = D_GATE // N_GROUPS
N_HEADS = 8
V_DIM = 2 * HEAD_DIM
QK_WIDTH = N_HEADS * 2 * HEAD_DIM
V_WIDTH = N_HEADS * V_DIM
D_FF_2 = int(math.ceil(8 * D_MODEL / 3 / 256) * 256)
EPS = 1e-6


def _alibi_slopes(n):
    return np.array([2.0 ** (-8.0 * (i + 1) / n) for i in range(n)], dtype=np.float32)

def _lambda_init(layer_idx):
    return 0.8 - 0.6 * math.exp(-0.3 * layer_idx)

def rms_norm_2(x, g):
    xf = x.astype(jnp.float32)
    y = xf * lax.rsqrt(jnp.mean(xf * xf, axis=-1, keepdims=True) + EPS)
    return (y * g.astype(jnp.float32)).astype(x.dtype)

def layer_norm_gain(x, g):
    xf = x.astype(jnp.float32)
    mu = jnp.mean(xf, axis=-1, keepdims=True)
    var = jnp.mean(jnp.square(xf - mu), axis=-1, keepdims=True)
    return ((xf - mu) * lax.rsqrt(var + EPS) * g.astype(jnp.float32)).astype(x.dtype)

def swiglu(h, w_gu, w_down):
    gu = h @ w_gu
    g, u = jnp.split(gu, 2, axis=-1)
    return (jax.nn.silu(g) * u) @ w_down

def gmlp_mixer(h, w_in, v_gain, w_sp, b_sp, w_out):
    B, S, _ = h.shape
    uv = jax.nn.gelu(h @ w_in)
    u, v = jnp.split(uv, 2, axis=-1)
    v = layer_norm_gain(v, v_gain)
    v = v.reshape(B, S // CHUNK, CHUNK, N_GROUPS, GROUP_DIM)
    causal = jnp.tril(jnp.ones((CHUNK, CHUNK), dtype=w_sp.dtype))
    z = jnp.einsum('gts,bcsgd->bctgd', w_sp * causal, v)
    z = z + b_sp.T[None, None, :, :, None]
    return (u * z.reshape(B, S, D_GATE)) @ w_out

def shared_kv(x, g, w_kv):
    B, S, _ = x.shape
    kv = rms_norm_2(x, g) @ w_kv
    k = kv[..., :QK_WIDTH].reshape(B, S, N_HEADS, 2, HEAD_DIM).transpose(0, 2, 3, 1, 4)
    v = kv[..., QK_WIDTH:].reshape(B, S, N_HEADS, V_DIM).transpose(0, 2, 1, 3)
    return k, v

def diff_attention(h, k, v, w_q, lam_vecs, subln, w_o, lambda_init):
    B, S, _ = h.shape
    n_blk = S // Q_BLOCK
    q = (h @ w_q).reshape(B, S, N_HEADS, 2, HEAD_DIM)
    q = q.reshape(B, n_blk, Q_BLOCK, N_HEADS, 2, HEAD_DIM).transpose(1, 0, 3, 4, 2, 5)
    lf = lam_vecs.astype(jnp.float32)
    lam = jnp.exp(jnp.sum(lf[0] * lf[1])) - jnp.exp(jnp.sum(lf[2] * lf[3])) + lambda_init
    slopes = jnp.asarray(_alibi_slopes(N_HEADS))
    scale = HEAD_DIM ** -0.5
    kf = k.astype(jnp.float32)
    vf = v.astype(jnp.float32)
    key_pos = jnp.arange(S, dtype=jnp.int32)

    def block(args):
        qb, bi = args
        q_pos = bi * Q_BLOCK + jnp.arange(Q_BLOCK, dtype=jnp.int32)
        dist = (q_pos[:, None] - key_pos[None, :]).astype(jnp.float32)
        bias = -slopes[:, None, None] * dist[None]
        s = jnp.einsum('bhitd,bhisd->bhits', qb.astype(jnp.float32), kf) * scale
        s = s + bias[None, :, None]
        s = jnp.where((dist >= 0)[None, None, None], s, -jnp.inf)
        p = jax.nn.softmax(s, axis=-1)
        a = p[:, :, 0] - lam * p[:, :, 1]
        return jnp.einsum('bhts,bhsd->bhtd', a, vf)

    o = lax.map(block, (q, jnp.arange(n_blk, dtype=jnp.int32)))
    o = o.transpose(1, 0, 3, 2, 4).reshape(B, S, N_HEADS, V_DIM).astype(h.dtype)
    o = rms_norm_2(o, subln) * (1.0 - lambda_init)
    return o.reshape(B, S, V_WIDTH) @ w_o

def second_inputs(seed: int = 0) -> dict:
    key = jax.random.key(seed)
    ks = jax.random.split(key, 20)
    f32 = jnp.float32

    def w(k, shape, fan_in):
        return jax.random.normal(k, shape, f32) * (fan_in ** -0.5)

    def gain(k, shape):
        return 1.0 + 0.05 * jax.random.normal(k, shape, f32)

    return {
        "x": jax.random.normal(ks[0], (BATCH, SEQ, D_MODEL), f32),
        "a_norm": gain(ks[1], (N_A, D_MODEL)),
        "a_w_in": w(ks[2], (N_A, D_MODEL, 2 * D_GATE), D_MODEL),
        "a_v_norm": gain(ks[3], (N_A, D_GATE)),
        "a_w_sp": w(ks[4], (N_A, N_GROUPS, CHUNK, CHUNK), CHUNK),
        "a_b_sp": 1.0 + 0.1 * jax.random.normal(ks[5], (N_A, N_GROUPS, CHUNK), f32),
        "a_w_out": w(ks[6], (N_A, D_GATE, D_MODEL), D_GATE),
        "ffn_norm": gain(ks[7], (DEPTH_2, D_MODEL)),
        "ffn_w_gu": w(ks[8], (DEPTH_2, D_MODEL, 2 * D_FF_2), D_MODEL),
        "ffn_w_down": w(ks[9], (DEPTH_2, D_FF_2, D_MODEL), D_FF_2),
        "kv_norm": gain(ks[10], (D_MODEL,)),
        "kv_w": w(ks[11], (D_MODEL, QK_WIDTH + V_WIDTH), D_MODEL),
        "b_norm": gain(ks[12], (N_B, D_MODEL)),
        "b_w_q": w(ks[13], (N_B, D_MODEL, QK_WIDTH), D_MODEL),
        "b_lambda": 0.1 * jax.random.normal(ks[14], (N_B, 4, HEAD_DIM), f32),
        "b_subln": gain(ks[15], (N_B, V_DIM)),
        "b_w_o": w(ks[16], (N_B, V_WIDTH, D_MODEL), V_WIDTH),
        "final_norm": gain(ks[17], (D_MODEL,)),
    }

def second_block(x, a_norm, a_w_in, a_v_norm, a_w_sp, a_b_sp, a_w_out, ffn_norm, ffn_w_gu, ffn_w_down,
              kv_norm, kv_w, b_norm, b_w_q, b_lambda, b_subln, b_w_o, final_norm):
    k = v = None
    for l in range(DEPTH_2):
        if l < N_A:
            x = x + gmlp_mixer(rms_norm_2(x, a_norm[l]), a_w_in[l], a_v_norm[l],
                               a_w_sp[l], a_b_sp[l], a_w_out[l])
        else:
            j = l - N_A
            if j == 0:
                k, v = shared_kv(x, kv_norm, kv_w)
            x = x + diff_attention(rms_norm_2(x, b_norm[j]), k, v, b_w_q[j], b_lambda[j],
                                   b_subln[j], b_w_o[j], _lambda_init(l))
        x = x + swiglu(rms_norm_2(x, ffn_norm[l]), ffn_w_gu[l], ffn_w_down[l])
    return rms_norm_2(x, final_norm)


def setup_inputs(seed=0):
    out = dict(first_inputs(seed))
    for name, value in second_inputs(seed + 1).items():
        if name != "x":
            out[name + "_2"] = value
    return out


def reference(
    x, mem, positions, g_mix, w_in, b_forget, w_sconv, w_pool, pool_scale, w_out, g_xa, g_mem,
    w_xq, w_xkv, w_xo, g_ffn, w_up, w_ffconv, w_down, g_final, a_norm_2, a_w_in_2, a_v_norm_2,
    a_w_sp_2, a_b_sp_2, a_w_out_2, ffn_norm_2, ffn_w_gu_2, ffn_w_down_2, kv_norm_2, kv_w_2,
    b_norm_2, b_w_q_2, b_lambda_2, b_subln_2, b_w_o_2, final_norm_2,
):
    x = first_block(
        x, mem, positions, g_mix, w_in, b_forget, w_sconv, w_pool, pool_scale, w_out, g_xa,
        g_mem, w_xq, w_xkv, w_xo, g_ffn, w_up, w_ffconv, w_down, g_final,
    )
    return second_block(
        x, a_norm_2, a_w_in_2, a_v_norm_2, a_w_sp_2, a_b_sp_2, a_w_out_2, ffn_norm_2,
        ffn_w_gu_2, ffn_w_down_2, kv_norm_2, kv_w_2, b_norm_2, b_w_q_2, b_lambda_2, b_subln_2,
        b_w_o_2, final_norm_2,
    )


_drawn_inputs = setup_inputs


def setup_inputs(seed=0):
    import zlib

    import numpy as np

    out = dict(_drawn_inputs(seed))
    spreads = {}
    factors = {'b_forget': 64.0,
     'pool_scale': 5.366,
     'g_xa': 8.0,
     'g_mem': 8.0,
     'g_ffn': 3.279,
     'b_norm_2': 3.349,
     'b_lambda_2': 5.808,
     'b_subln_2': 3.457}
    for name, (base, spread) in spreads.items():
        noise = np.random.default_rng([zlib.crc32(name.encode()), seed]).standard_normal(out[name].shape)
        drawn = base * np.exp(spread * noise) if base else spread * noise
        out[name] = __import__('jax').numpy.asarray(drawn.astype(out[name].dtype))
    for name, factor in factors.items():
        out[name] = (out[name] * factor).astype(out[name].dtype)
    return out
```

```python
import math
from contextlib import ExitStack

import numpy as np

import concourse.bass as bass
from concourse import mybir

F32 = mybir.dt.float32
F32R = mybir.dt.float32r
I32 = mybir.dt.int32
ALU = mybir.AluOpType
ACT = mybir.ActivationFunctionType
AX = mybir.AxisListType

P = 128
D = 1024
S = 512
KC = D // P
M = 256
MB = M // P
TB = S // P
HD = 64
FF = 2816
FC = FF // P
G = D // 4
GC = G // P
N_FORGET = G // HD
XA_HEADS = 4
XC = D // XA_HEADS // P
N_DIFF = 8
N_SPATIAL = 8
EPS = 1e-6
MASKED = 1e30
FAR = 3.0e38
ROPE_DIM = HD // 4
ROPE_THETA = 500000.0
DILATED = ((128, 1), (512, 4), (2048, 16))
POOL_WINDOWS = (2, 4, 8, 16)
LAMBDA_INIT = 0.8 - 0.6 * math.exp(-0.3)
DIFF_SLOTS = 4
BAND = S + S - P

UNITS = (("w_in", 2 * KC + 5), ("w_out", KC), ("mem_k", KC), ("mem_v", KC), ("xq", KC), ("xo", KC),
         ("up", 2 * FC), ("down", FC), ("a_v", KC), ("a_u", KC), ("a_out", KC), ("gu0", 2 * FC), ("down0", FC),
         ("kv_v", KC), ("qk", 2 * KC), ("bo", KC), ("gu1", 2 * FC), ("down1", FC))
FIRST = {}
N_UNITS = 0
for _name, _n in UNITS:
    FIRST[_name] = N_UNITS
    N_UNITS += _n

PARAMS = (("g_mix", KC), ("g_xa", KC), ("g_mem", KC), ("g_ffn", KC), ("a_norm", KC), ("ffn_norm0", KC),
          ("kv_norm", KC), ("b_norm", KC), ("ffn_norm1", KC), ("g_first", KC), ("a_gain", KC), ("g_final", KC), ("a_v_norm", KC),
          ("b_forget", 1), ("w_sconv", 3 * GC), ("pool_scale", GC), ("w_ffconv", 3 * 2 * FC), ("b_subln", 1),
          ("eps", 1), ("inv_freq", 1), ("inv_window", GC), ("slopes", N_DIFF))
AT = {}
N_PARAMS = 0
for _name, _n in PARAMS:
    AT[_name] = N_PARAMS
    N_PARAMS += _n

CONSTS = (("ident", P), ("ones", P), ("rope_perm", P), ("causal", P), ("keep", P), ("inv_count", GC * 16),
          ("pick", 2 * N_DIFF - 1))
CAT = {}
N_CONSTS = 0
for _name, _n in CONSTS:
    CAT[_name] = N_CONSTS
    N_CONSTS += _n

TWO_PI = 2.0 * math.pi
TURN_1 = 201.0 / 32.0
TURN_2 = round((TWO_PI - TURN_1) * 2.0 ** 17) / 2.0 ** 17
TURN_3 = round((TWO_PI - TURN_1 - TURN_2) * 2.0 ** 27) / 2.0 ** 27
TURN_4 = TWO_PI - TURN_1 - TURN_2 - TURN_3
ROUNDER = 1.5 * 2.0 ** 23
PI_BELOW = 3.1415925


def bass_two_blocks(nc, weights, x_cols, mem_cols, positions, params, consts, dil_table, head_rows, alibi_table, head_picks,
                    pool_blocks, spatial, spatial_bias, lambdas, out):
    ctx = ExitStack()

    def sem(name):
        return ctx.enter_context(nc.semaphore(name))

    def stage(name, *signals):
        return {s: sem(f"{name}_{s}") for s in signals}

    def at(const, i=None, per=0):
        return const if i is None else const + i * per

    def diff_turns(engine, step, depth):
        for n in range(8):
            step(n, None, 0)
        with engine.Fori(1, N_DIFF // 2 - 1) as c:
            for n in range(8):
                step(n, c, 0)
        for n in range(8 + depth):
            step(n, None, 4 * N_DIFF - 8)

    def live(n, c, base):
        return n < 8 and (n >= 0 or c is not None or base > 0)

    def qk_due(n, c, base):
        return n % 2 == 0 and (0 < n < 8 or c is not None or base > 0 and n == 0) and (base == 0 or n == 0)

    with ctx:
        def sb(name, shape, dt=F32, where=ctx):
            return where.enter_context(nc.sbuf_tensor(name, shape, dt))

        x = sb("x", [P, KC, S])
        xg_hi = sb("xg_hi", [P, KC, S], F32R)
        xg_lo = sb("xg_lo", [P, KC, S], F32R)
        w_raw = sb("w_raw", [P, 2, D])
        w_hi = sb("w_hi", [P, 2, D], F32R)
        w_lo = sb("w_lo", [P, 2, D], F32R)
        par = sb("par", [P, N_PARAMS])
        con = sb("con", [P, N_CONSTS])
        r_cols = sb("r_cols", [P, S])
        r_rows = sb("r_rows", [P, TB])
        rms_rows = sb("rms_rows", [P, TB])
        squares = sb("squares", [P, 2, S])
        square_sum = sb("square_sum", [P, S])
        lam_in = sb("lam_in", [P, 4 * HD])
        lam_dot = sb("lam_dot", [P, 2])
        lam_exp = sb("lam_exp", [P, 2])
        lam = sb("lam", [P, 1])
        subln = sb("subln", [P, 1])

        m_ctx = ExitStack()
        mix = dict(
            hi=sb("mix_hi", [P, KC, S], F32R, m_ctx), lo=sb("mix_lo", [P, KC, S], F32R, m_ctx),
            proj=sb("proj", [P, 17, S], F32, m_ctx), v=sb("mix_v", [P, TB, 2 * G], F32, m_ctx),
            dil=sb("dil", [P, BAND], F32, m_ctx),
            c_rows=sb("c_rows", [P, S], F32, m_ctx), nci=sb("nci", [P, TB, N_FORGET], F32, m_ctx))
        m_top = ExitStack()
        rope = dict(
            pos=sb("pos", [P, S], I32, m_top), ang=sb("ang", [P, S], F32, m_top),
            turns=sb("turns", [P, S], F32, m_top), red=sb("red", [P, S], F32, m_top),
            cos=sb("cos", [P, S], F32, m_top), sin=sb("sin", [P, S], F32, m_top),
            prod=sb("rope_prod", [P, S], F32, m_top), heads=sb("heads", [P, N_FORGET * P], F32, m_top),
            g1=sb("gate_a", [P, S], F32, m_top), g2=sb("gate_b", [P, S], F32, m_top),
            g3=sb("gate_c", [P, S], F32, m_top), g4=sb("gate_d", [P, S], F32, m_top),
            pad=sb("pad", [P, S + 16], F32, m_top), win=sb("win", [P, S + 16], F32, m_top),
            win2=sb("win2", [P, S + 16], F32, m_top), z=sb("pooled", [P, GC, S], F32, m_top),
            pool_w=sb("pool_w", [P, GC, P], F32, m_top))
        m_top.close()

        def attention_buffers(tag, where, q_cols, k_cols, v_cols, n_e, s_cols, turned):
            names = {}
            for set_ in range(2):
                for part, cols in (("q", q_cols), ("k", k_cols), ("v", v_cols)):
                    for half in ("hi", "lo"):
                        names[f"{part}{half}{set_}"] = sb(f"{tag}_{part}_{half}{set_}", [P, cols], F32R, where)
            names["pt_hi"] = sb(f"{tag}_pt_hi", [P, 2, turned], F32R, where)
            names["pt_lo"] = sb(f"{tag}_pt_lo", [P, 2, turned], F32R, where)
            names["e"] = sb(f"{tag}_e", [P, n_e, s_cols], F32, where)
            names["least"] = sb(f"{tag}_least", [P, n_e], F32, where)
            names["sums"] = sb(f"{tag}_sums", [P, n_e], F32, where)
            names["inv"] = sb(f"{tag}_inv", [P, n_e], F32, where)
            return names

        at1 = attention_buffers("at1", m_ctx, S, S, S, 3, S, S)
        m_ctx.close()
        c_ctx = ExitStack()
        xa = dict(
            hi=sb("xa_hi", [P, KC, S], F32R, c_ctx), lo=sb("xa_lo", [P, KC, S], F32R, c_ctx),
            q=sb("xa_q", [P, KC, S], F32, c_ctx), k=sb("xa_k", [P, KC, M], F32, c_ctx),
            v=sb("xa_v", [P, MB, D], F32, c_ctx), r_cols=sb("mem_r_cols", [P, M], F32, c_ctx),
            r_rows=sb("mem_r_rows", [P, MB], F32, c_ctx))
        c_top = ExitStack()
        memory = dict(
            x=sb("mem_x", [P, KC, M], F32, c_top), hi=sb("mem_hi", [P, KC, M], F32R, c_top),
            lo=sb("mem_lo", [P, KC, M], F32R, c_top), sq=sb("mem_sq", [P, 2, M], F32, c_top),
            acc=sb("mem_acc", [P, M], F32, c_top), rms=sb("mem_rms", [P, M], F32, c_top),
            rms_rows=sb("mem_rms_rows", [P, MB], F32, c_top))
        c_top.close()
        at2 = attention_buffers("at2", c_ctx, XC * S, XC * M, MB * XC * P, 3, M, M)
        c_ctx.close()
        f_ctx = ExitStack()
        ffn = dict(
            hi=sb("hid_hi", [P, FC, S], F32R, f_ctx), lo=sb("hid_lo", [P, FC, S], F32R, f_ctx),
            ua=sb("up_a", [P, S + 2], F32, f_ctx), ug=sb("up_g", [P, S + 2], F32, f_ctx),
            ta=sb("conv_a", [P, S], F32, f_ctx), tg=sb("conv_g", [P, S], F32, f_ctx),
            gate=sb("gate", [P, S], F32, f_ctx), h=sb("hid", [P, S], F32, f_ctx))
        f_ctx.close()
        g_ctx = ExitStack()
        sg = dict(
            hi=sb("sg_hi", [P, KC, S], F32R, g_ctx), lo=sb("sg_lo", [P, KC, S], F32R, g_ctx),
            u=sb("sg_u", [P, KC, S], F32, g_ctx), v=sb("sg_v", [P, TB, D], F32, g_ctx),
            v_hi=sb("sg_v_hi", [P, TB, D], F32R, g_ctx), v_lo=sb("sg_v_lo", [P, TB, D], F32R, g_ctx),
            v_sum=sb("sg_v_sum", [P, TB, 2], F32, g_ctx), mean=sb("sg_mean", [P, TB], F32, g_ctx),
            v_sq=sb("sg_v_sq", [P, TB], F32, g_ctx), std=sb("sg_std", [P, TB], F32, g_ctx),
            r=sb("sg_r", [P, TB], F32, g_ctx), z=sb("sg_z", [P, S], F32, g_ctx),
            w=sb("sp_w", [P, N_SPATIAL * P], F32, g_ctx), w_hi=sb("sp_w_hi", [P, N_SPATIAL * P], F32R, g_ctx),
            w_lo=sb("sp_w_lo", [P, N_SPATIAL * P], F32R, g_ctx), b=sb("sp_b", [P, N_SPATIAL, P], F32, g_ctx))
        first = dict(
            r=sb("first_r", [P, S], F32, g_ctx), r_rows=sb("first_r_rows", [P, TB], F32, g_ctx),
            sums=sb("first_sums", [P, S], F32, g_ctx), sums_rows=sb("first_sums_rows", [P, TB], F32, g_ctx))
        g_ctx.close()
        d_ctx = ExitStack()
        da = dict(
            v=sb("da_v", [P, TB, D], F32, d_ctx), o=sb("da_o", [P, KC, S], F32, d_ctx),
            xb_hi=sb("xb_hi", [P, KC, S], F32R, d_ctx), xb_lo=sb("xb_lo", [P, KC, S], F32R, d_ctx),
            alibi=sb("alibi", [P, BAND], F32, d_ctx), bias=sb("da_bias", [P, 2, BAND], F32, d_ctx),
            zero=sb("da_zero", [P, 1], F32, d_ctx), k=squares[:, 0, :], q=squares[:, 1, :])
        at3 = attention_buffers("at3", d_ctx, S, S, S, 2 * DIFF_SLOTS, S, S)
        at3["second"] = sb("at3_second", [P, 2 * DIFF_SLOTS], F32, d_ctx)
        da["picks"] = at3["e"][0:N_DIFF, 0:N_DIFF * P // S, :].rearrange("p a n -> p (a n)")
        da["rms"] = at3["e"][0:N_DIFF, N_DIFF * P // S, :]
        d_ctx.close()
        o_ctx = ExitStack()
        result = sb("result", [P, KC, S], F32, o_ctx)
        o_ctx.close()

        ps = ctx.enter_context(nc.psum_tensor("ps", [P, 8, S], F32))

        ident = con[:, CAT["ident"]:CAT["ident"] + P]
        ones = con[:, CAT["ones"]:CAT["ones"] + P]
        causal = con[:, CAT["causal"]:CAT["causal"] + P]

        def column(name, c=0, rows=slice(0, P)):
            return par[rows, bass.ds(AT[name] + c, 1)]

        loads = stage("loaded", "input", "con", "early", "tables", "mem", "spatial", "alibi")
        N_EARLY, N_TABLES = 2, 3
        w_loaded = [sem("weights_loaded_0"), sem("weights_loaded_1")]
        w_hi_ready = sem("weights_hi_ready")
        w_ready = sem("weights_ready")
        used = sem("units_used")
        x_ready = sem("x_ready")
        xg_hi_ready = sem("xg_hi_ready")
        xg_ready = sem("xg_ready")
        sq_ready = sem("squares_ready")
        summed = sem("squares_summed")
        sums_ready = sem("square_sums_ready")
        rms_ready = sem("rms_ready")
        r_ready = sem("r_ready")
        rows_sums_ready = sem("row_square_sums_ready")
        rows_rms_ready = sem("row_rms_ready")
        rows_ready = sem("r_rows_ready")
        w_in = stage("w_in", "evacuated", "v_ready")
        gate = stage("gate", "steps", "abs", "exp", "c", "turned", "rows")
        rot = stage("rope", "steps", "trig", "swapped", "prod", "prod_cos", "done")
        small = stage("mixer", "steps", "conv", "pooled", "product", "hi")
        mix_ready = sem("mix_ready")
        a1 = stage("at1", "staged_hi", "staged", "scores", "least", "exps", "inv", "probs", "turned", "pt_hi", "pt",
                   "pv", "out_hi", "bias", "bias_steps")
        a2 = stage("at2", "staged_hi", "staged", "scores", "least", "exps", "inv", "probs", "turned", "pt_hi", "pt",
                   "pv", "out_hi", "out")
        a3 = stage("at3", "staged_hi", "staged", "v_staged", "scores", "least", "exps", "inv", "second", "weighed", "probs",
                   "turned", "pt_hi", "pt", "pv", "out", "bias", "sq", "summed", "rms", "spread", "normed", "out_hi",
                   "out_lo")
        lams = stage("lambda", "dots", "exps", "done")
        mem = stage("mem", "hi", "lo", "sq", "summed", "sums", "rms", "r", "k_ready", "v_ready")
        xqs = stage("xq", "ready")
        ffn_stages = {"up": stage("up", "scaled", "tapped", "steps", "gated", "product", "hid_hi", "hid", "zero"),
                      "gu0": stage("gu0", "scaled", "gated", "product", "hid_hi", "hid"),
                      "gu1": stage("gu1", "scaled", "gated", "product", "hid_hi", "hid")}
        a_in = stage("a_in", "scaled", "u", "v", "steps", "v_sq", "std", "normed", "v_hi", "v_lo",
                     "w", "w_hi", "w_lo", "first", "z_done", "z", "product", "hi", "ready")
        kv = stage("kv", "v", "qk", "xb_hi", "xb", "zero")
        proj_sums = sem("residual_sums")
        RESIDUALS = ("w_out", "xo", "down", "a_out", "down0", "bo", "down1")
        finals = stage("final", "scaled", "stored")

        NORM = {"mix": 0, "xa": 1, "ffn": 2, "first": 3, "a": 4, "ffn0": 5, "kv": 6, "ffn1": 7, "final": 8}
        SPLIT = {"mix": 0, "xa": 1, "ffn": 2, "first": 3, "ffn0": 4, "kv": 5, "ffn1": 6}
        ROWS = {"mix": 0, "first": 1, "a": 2, "kv": 3}

        block = ctx.enter_context(nc.Block())

        @block.sync
        def _(sp):
            sp.dma_start(x[:], x_cols).then_inc(loads["input"], 16)
            sp.dma_start(par[:], params).then_inc(loads["input"], 16)
            for u in range(2):
                sp.dma_start(w_raw[:, u, :], weights[u]).then_inc(w_loaded[u], 16)
            with sp.Fori(1, N_UNITS // 2) as i:
                for s in range(2):
                    sp.wait_ge(w_ready, i * 2 + (s - 1))
                    sp.dma_start(w_raw[:, s, :], weights[bass.ds(i * 2 + s, 1), :, :].rearrange("u p n -> p (u n)")
                                 ).then_inc(w_loaded[s], 16)
            for u in range(N_UNITS // 2 * 2, N_UNITS):
                sp.wait_ge(w_ready, u - 1)
                sp.dma_start(w_raw[:, u % 2, :], weights[u]).then_inc(w_loaded[u % 2], 16)
            for c in range(KC):
                sp.wait_ge(finals["scaled"], c + 1)
                sp.dma_start(out[:, c, :], result[:, c, :]).then_inc(finals["stored"], 16)
            sp.wait_ge(finals["stored"], 16 * KC)

        @block.tensor
        def _(pe):
            def product(to, wh, wl, xh, xl, start, stop):
                nc.tensor.matmul(to, wh, xh, start=start, stop=False)
                nc.tensor.matmul(to, wh, xl, start=False, stop=False)
                return nc.tensor.matmul(to, wl, xh, start=False, stop=stop)

            def tile(s, k):
                return w_hi[:, s, k * P:(k + 1) * P], w_lo[:, s, k * P:(k + 1) * P]

            def panel(u, i, to, hi, lo, chunks_ready=None):
                pe.wait_ge(w_ready, at(u + 1, i, 2))
                for k in range(KC):
                    if chunks_ready is not None:
                        pe.wait_ge(xg_ready, chunks_ready + k + 1)
                    wh, wl = tile(u % 2, k)
                    mm = product(to, wh, wl, hi[:, k, :], lo[:, k, :], k == 0, k == KC - 1)
                mm.then_inc(used, 1)

            def square_sums(norm, bank, rows_bank=None, sums=square_sum):
                pe.wait_ge(summed, KC * (NORM[norm] + 1))
                nc.tensor.matmul(ps[:, bank, :], ones, sums[:], start=True, stop=True).then_inc(sums_ready, 1)
                if rows_bank is not None:
                    for b in range(TB):
                        mm = nc.tensor.matmul(ps[:, rows_bank, b:b + 1], sums[:, b * P:(b + 1) * P],
                                              ones[:, 0:1], start=True, stop=True)
                    mm.then_inc(rows_sums_ready, 1)

            def values(first, u, hi, lo, n_blocks, banks, per_unit):
                halves = 2 // per_unit
                pe.wait_ge(w_ready, u + 1)
                for kk in range(per_unit):
                    k = (u - first) * per_unit + kk
                    for b in range(n_blocks):
                        for h in range(halves):
                            cols = slice((kk * halves + h) * S, (kk * halves + h + 1) * S)
                            mm = product(ps[:, banks[b * halves + h], :],
                                         hi[:, k, b * P:(b + 1) * P], lo[:, k, b * P:(b + 1) * P],
                                         w_hi[:, u % 2, cols], w_lo[:, u % 2, cols], k == 0, k == KC - 1)
                mm.then_inc(used, 1)

            def into_residual(name, n, bank0, hi, lo, ready, chunk_ready, bank_free):
                u0 = FIRST[name]

                def unit(k, i, first, final):
                    u = u0 + k
                    pe.wait_ge(w_ready, at(u + 1, i, 2))
                    pe.wait_ge(ready, at(chunk_ready(k), i, 2))
                    kk = at(k, i, 2)
                    for j in range(KC):
                        if first and j in bank_free:
                            pe.wait_ge(*bank_free[j])
                        wh, wl = tile(u % 2, j)
                        mm = product(ps[:, (bank0 + j) % 8, :], wh, wl, hi[:, kk, :], lo[:, kk, :], first, final)
                        if final and j < KC - 1:
                            mm.then_inc(proj_sums, 1)
                    mm.then_inc(used, 1)

                unit(0, None, True, False)
                unit(1, None, False, False)
                if n > 4:
                    with pe.Fori(0, n // 2 - 2) as i:
                        unit(2, i, False, False)
                        unit(3, i, False, False)
                unit(n - 2, None, False, False)
                unit(n - 1, None, False, True)

            def hidden(name, norm, st, base):
                u0 = FIRST[name]
                panel(u0, None, ps[:, base, :], xg_hi, xg_lo, KC * SPLIT[norm])
                square_sums(norm, (base + 2) % 8)
                panel(u0 + 1, None, ps[:, base + 1, :], xg_hi, xg_lo)
                with pe.Fori(0, FC - 1) as i:
                    for s in range(2):
                        pe.wait_ge(st["scaled"], at(s + 1, i, 2))
                        panel(u0 + 2 + s, i, ps[:, base + s, :], xg_hi, xg_lo)

            def attention_turn(a, buf, n_items, s_of, t_of, pv_of):
                for m in range(n_items + 3):
                    if m < n_items:
                        s_of(m)
                    if 0 <= m - 2 < n_items:
                        t_of(m - 2)
                    if 0 <= m - 3 < n_items:
                        pv_of(m - 3)

            u0 = FIRST["w_in"]
            pe.wait_ge(loads["con"], 16)
            panel(u0, None, ps[:, 0, :], xg_hi, xg_lo, 0)
            square_sums("mix", 2, 3)
            panel(u0 + 1, None, ps[:, 1, :], xg_hi, xg_lo)
            with pe.Fori(0, 7) as i:
                for s in range(2):
                    pe.wait_ge(w_in["evacuated"], at(s + 1, i, 2))
                    panel(u0 + 2 + s, i, ps[:, s, :], xg_hi, xg_lo)
            pe.wait_ge(w_in["evacuated"], 15)
            panel(u0 + 16, None, ps[:, 0, :], xg_hi, xg_lo)
            for u in range(u0 + 17, u0 + 21):
                values(u0 + 17, u, xg_hi, xg_lo, TB, (4, 5, 6, 7), 2)
                c = u - u0 - 17
                if c >= 2:
                    pe.wait_ge(rot["prod"], c - 1)
                pe.wait_ge(w_in["evacuated"], 10 + c)
                pe.wait_ge(r_ready, 1)
                pe.wait_ge(rows_ready, 1)
                nc.tensor.matmul(ps[:, 2 + c % 2, :], con[:, CAT["rope_perm"]:CAT["rope_perm"] + P],
                                 mix["proj"][:, 9 + c, :], start=True, stop=True).then_inc(rot["swapped"], 1)
            for c in range(GC):
                pe.wait_ge(small["pooled"], c + 1)
                pe.wait_ge(loads["tables"], 16 * N_TABLES)
                pe.wait_ge(w_in["evacuated"], 17)
                nc.tensor.matmul(ps[:, c, :], rope["pool_w"][:, c, :], rope["z"][:, c, :],
                                 start=True, stop=True).then_inc(small["product"], 1)
            pe.wait_ge(gate["c"], 1)
            pe.wait_ge(rot["prod"], 4)
            for b in range(TB):
                mm = nc.tensor.matmul(ps[:, 2, b * N_FORGET:(b + 1) * N_FORGET], mix["c_rows"][0:N_FORGET, b * P:(b + 1) * P],
                                      ident[0:N_FORGET, 0:N_FORGET], start=True, stop=True)
            mm.then_inc(gate["turned"], 1)
            pe.wait_ge(loads["tables"], 16 * N_TABLES)
            pe.wait_ge(mix_ready, 4)
            for h in range(N_FORGET):
                if h >= 2:
                    pe.wait_ge(gate["rows"], h)
                nc.tensor.matmul(ps[:, h % 2, :], rope["heads"][0:N_FORGET, h * P:(h + 1) * P],
                                 mix["c_rows"][0:N_FORGET, :], start=True, stop=True).then_inc(gate["turned"], 1)
            pe.wait_ge(gate["rows"], 1 + N_FORGET)

            with pe.Fori(0, GC) as c:
                def item(n):
                    return n // 8, n % 8 // 2, n % 2

                def scores(n):
                    s, b, h = item(n)
                    rows = slice(HD * h, HD * h + HD)
                    if b == 0 and h == 0:
                        pe.wait_ge(a1["staged"], at(s + 1, c, 2))
                    if n >= 2:
                        pe.wait_ge(a1["least"], at(n - 1, c, 16))
                    w = P * (b + 1)
                    qh, ql, kh, kl = (at1[f"{p}{s}"] for p in ("qhi", "qlo", "khi", "klo"))
                    product(ps[:, n % 2, 0:w], qh[rows, b * P:(b + 1) * P], ql[rows, b * P:(b + 1) * P],
                            kh[rows, 0:w], kl[rows, 0:w], True, True).then_inc(a1["scores"], 1)

                def turn(n):
                    b = item(n)[1]
                    pe.wait_ge(a1["probs"], at(n + 1, c, 16))
                    if n >= 2:
                        pe.wait_ge(a1["pt"], at(n - 1, c, 16))
                    for j in range(b + 1):
                        mm = nc.tensor.transpose(ps[:, 2 + n % 2, j * P:(j + 1) * P],
                                                 at1["e"][:, n % 3, j * P:(j + 1) * P], ident)
                    mm.then_inc(a1["turned"], 1)

                def weigh(n):
                    s, b, h = item(n)
                    pe.wait_ge(a1["pt"], at(n + 1, c, 16))
                    if b == 0 and h == 0:
                        pe.wait_ge(mix_ready, at(3 + s, c, 2))
                    vh, vl = at1[f"vhi{s}"], at1[f"vlo{s}"]
                    for j in range(b + 1):
                        cols = slice(j * P, (j + 1) * P)
                        mm = product(ps[:, 4 + 2 * s + h, b * P:(b + 1) * P], vh[:, cols], vl[:, cols],
                                     at1["pt_hi"][:, n % 2, cols], at1["pt_lo"][:, n % 2, cols], j == 0, j == b)
                    mm.then_inc(a1["pv"], 1)

                attention_turn(a1, at1, 16, scores, turn, weigh)

            into_residual("w_out", KC, 0, mix["hi"], mix["lo"], mix_ready, lambda k: k + 1,
                          {0: (a1["pt"], 32), 4: (mix_ready, 8)})

            u0 = FIRST["mem_k"]
            done = KC * (NORM["xa"] - 1)
            pe.wait_ge(x_ready, done + KC)
            for p in range(0, KC):
                if p < 1:
                    pe.wait_ge(mem["lo"], KC)
                if p < 2:
                    panel(u0 + p, None, ps[:, p, 0:M], memory["hi"], memory["lo"])
                if p == 0:
                    pe.wait_ge(mem["summed"], KC)
                    nc.tensor.matmul(ps[:, 6, 0:M], ones, memory["acc"][:], start=True, stop=True).then_inc(mem["sums"], 1)
                    for b in range(MB):
                        mm = nc.tensor.matmul(ps[:, 7, b:b + 1], memory["acc"][:, b * P:(b + 1) * P], ones[:, 0:1],
                                              start=True, stop=True)
                    mm.then_inc(mem["sums"], 1)
            with pe.Fori(0, KC // 2 - 1) as i:
                for s in range(2):
                    pe.wait_ge(mem["k_ready"], at(s + 1, i, 2))
                    panel(u0 + 2 + s, i, ps[:, s, 0:M], memory["hi"], memory["lo"])
            u0 = FIRST["mem_v"]
            for u in range(u0, u0 + KC):
                values(u0, u, memory["hi"], memory["lo"], MB, (2, 3, 4, 5), 1)
            u0 = FIRST["xq"]
            pe.wait_ge(mem["k_ready"], KC)
            panel(u0, None, ps[:, 0, :], xg_hi, xg_lo, KC * SPLIT["xa"])
            pe.wait_ge(mem["r"], 2)
            square_sums("xa", 6)
            panel(u0 + 1, None, ps[:, 1, :], xg_hi, xg_lo)
            with pe.Fori(0, KC // 2 - 1) as i:
                for s in range(2):
                    pe.wait_ge(xqs["ready"], at(s + 1, i, 2))
                    panel(u0 + 2 + s, i, ps[:, s, :], xg_hi, xg_lo)
            pe.wait_ge(xqs["ready"], KC)
            pe.wait_ge(mem["v_ready"], 2 * MB)
            with pe.Fori(0, XA_HEADS // 2) as c:
                def item(n):
                    return n // TB, n % TB

                def scores(n):
                    s, b = item(n)
                    if b == 0:
                        pe.wait_ge(a2["staged"], at(s + 1, c, 2))
                    if n >= 2:
                        pe.wait_ge(a2["exps"], at(n - 1, c, 8))
                    qh, ql, kh, kl = (at2[f"{p}{s}"] for p in ("qhi", "qlo", "khi", "klo"))
                    for d in range(XC):
                        qc = slice(d * S + b * P, d * S + (b + 1) * P)
                        kc = slice(d * M, (d + 1) * M)
                        mm = product(ps[:, n % 2, 0:M], qh[:, qc], ql[:, qc], kh[:, kc], kl[:, kc], d == 0, d == XC - 1)
                    mm.then_inc(a2["scores"], 1)

                def turn(n):
                    pe.wait_ge(a2["probs"], at(n + 1, c, 8))
                    if n >= 2:
                        pe.wait_ge(a2["pt"], at(n - 1, c, 8))
                    for j in range(MB):
                        mm = nc.tensor.transpose(ps[:, 2 + n % 2, j * P:(j + 1) * P],
                                                 at2["e"][:, n % 3, j * P:(j + 1) * P], ident)
                    mm.then_inc(a2["turned"], 1)

                def weigh(n):
                    s, b = item(n)
                    pe.wait_ge(a2["pt"], at(n + 1, c, 8))
                    vh, vl = at2[f"vhi{s}"], at2[f"vlo{s}"]
                    for d in range(XC):
                        for j in range(MB):
                            vc = slice((j * XC + d) * P, (j * XC + d + 1) * P)
                            pc = slice(j * P, (j + 1) * P)
                            mm = product(ps[:, 4 + 2 * s + d, b * P:(b + 1) * P], vh[:, vc], vl[:, vc],
                                         at2["pt_hi"][:, n % 2, pc], at2["pt_lo"][:, n % 2, pc], j == 0, j == MB - 1)
                    mm.then_inc(a2["pv"], 1)

                attention_turn(a2, at2, 8, scores, turn, weigh)

            into_residual("xo", KC, 0, xa["hi"], xa["lo"], a2["out"], lambda k: k + 1, {0: (a2["pt"], 16), 4: (a2["out"], KC)})

            st = ffn_stages["up"]
            hidden("up", "ffn", st, 0)
            into_residual("down", FC, 2, ffn["hi"], ffn["lo"], st["hid"], lambda k: k + 1,
                          {0: (r_ready, NORM["ffn"] + 1), 6: (st["scaled"], 2 * FC - 1), 7: (st["scaled"], 2 * FC)})

            u0 = FIRST["a_v"]
            for u in range(u0, u0 + 4):
                pe.wait_ge(xg_ready, KC * SPLIT["first"] + max(4, 2 * (u - u0 + 1)))
                values(u0, u, xg_hi, xg_lo, TB, (2, 3, 4, 5), 2)
                if u == u0 + 1:
                    square_sums("first", 6, 7)
                if u == u0 + 2:
                    square_sums("a", 0, 1, first["sums"])
            pe.wait_ge(rows_rms_ready, ROWS["first"] + 1)
            pe.wait_ge(a_in["first"], 2)
            for u in range(u0 + 4, u0 + KC):
                values(u0 + 4, u, xg_hi, xg_lo, TB, (6, 7, 0, 1), 2)
            u0 = FIRST["a_u"]
            pe.wait_ge(a_in["v"], 4)
            panel(u0, None, ps[:, 2, :], xg_hi, xg_lo)
            panel(u0 + 1, None, ps[:, 3, :], xg_hi, xg_lo)
            with pe.Fori(0, KC // 2 - 1) as i:
                for s in range(2):
                    pe.wait_ge(a_in["scaled"], at(s + 1, i, 2))
                    panel(u0 + 2 + s, i, ps[:, 2 + s, :], xg_hi, xg_lo)
            pe.wait_ge(a_in["w_lo"], 1)
            for g in range(N_SPATIAL):
                if g >= 2:
                    pe.wait_ge(a_in["z"], g - 1)
                for b in range(TB):
                    if g == 0:
                        pe.wait_ge(a_in["v_lo"], b + 1)
                    mm = product(ps[:, 4 + g % 2, b * P:(b + 1) * P],
                                 sg["v_hi"][:, b, g * P:(g + 1) * P], sg["v_lo"][:, b, g * P:(g + 1) * P],
                                 sg["w_hi"][:, g * P:(g + 1) * P], sg["w_lo"][:, g * P:(g + 1) * P], True, True)
                mm.then_inc(a_in["z_done"], 1)
            into_residual("a_out", KC, 0, sg["hi"], sg["lo"], a_in["ready"], lambda k: k + 1,
                          {0: (a_in["v"], 8), 2: (a_in["scaled"], KC), 4: (a_in["z"], N_SPATIAL - 1), 5: (a_in["z"], N_SPATIAL)})

            st = ffn_stages["gu0"]
            hidden("gu0", "ffn0", st, 0)
            into_residual("down0", FC, 2, ffn["hi"], ffn["lo"], st["hid"], lambda k: k + 1,
                          {0: (r_ready, NORM["ffn0"] + 1), 6: (st["scaled"], 2 * FC - 1), 7: (st["scaled"], 2 * FC)})

            u0 = FIRST["kv_v"]
            for u in range(u0, u0 + 4):
                pe.wait_ge(xg_ready, KC * SPLIT["kv"] + max(4, 2 * (u - u0 + 1)))
                values(u0, u, xg_hi, xg_lo, TB, (2, 3, 4, 5), 2)
                if u == u0 + 1:
                    pe.wait_ge(xg_ready, KC * SPLIT["kv"] + 6)
                    square_sums("kv", 6, 7)
            pe.wait_ge(r_ready, NORM["kv"] + 1)
            pe.wait_ge(rows_ready, ROWS["kv"] + 1)
            pe.wait_ge(x_ready, KC * NORM["kv"])
            for u in range(u0 + 4, u0 + KC):
                values(u0 + 4, u, xg_hi, xg_lo, TB, (6, 7, 0, 1), 2)
            qk0 = FIRST["qk"]

            def half_panel(u, i, to, hi, lo, half):
                if half == 0:
                    pe.wait_ge(w_ready, at(u + 1, i, 4))
                for k in range(KC // 2 * half, KC // 2 * (half + 1)):
                    wh, wl = tile(u % 2, k)
                    mm = product(to, wh, wl, hi[:, k, :], lo[:, k, :], k == 0, k == KC - 1)
                if half:
                    mm.then_inc(used, 1)

            def qk_input(p):
                return (da["xb_hi"], da["xb_lo"]) if p % 2 else (xg_hi, xg_lo)

            pe.wait_ge(kv["v"], 4)
            for p in range(4):
                if p == 1:
                    pe.wait_ge(kv["xb"], KC)
                for half in range(2):
                    half_panel(qk0 + p, None, ps[:, 2 + p, :], *qk_input(p), half)
            pe.wait_ge(kv["v"], 8)
            pe.wait_ge(kv["qk"], 4)

            def diff_item(n, c, base):
                def scores(n):
                    s, b = n // TB, n % TB
                    if b == 0:
                        pe.wait_ge(a3["staged"], at(2 * (base // TB + s + 1), c, 4))
                    if c is not None or n + base >= 2:
                        pe.wait_ge(a3["least"], at(2 * (base + n - 1), c, 16))
                    w = P * (b + 1)
                    qh, ql, kh, kl = (at3[f"{p}{s % 2}"] for p in ("qhi", "qlo", "khi", "klo"))
                    block_ = slice(b * P, (b + 1) * P)
                    for k, (q_, k_) in enumerate(((qh, kh), (qh, kl), (ql, kh))):
                        for h in range(2):
                            rows = slice(HD * h, HD * h + HD)
                            mm = nc.tensor.matmul(ps[:, 2 * (n % 2) + h, 0:w], q_[rows, block_], k_[rows, 0:w],
                                                  start=k == 0, stop=k == 2)
                            if k == 2:
                                mm.then_inc(a3["scores"], 1)

                def turn(n):
                    b = n % TB
                    pe.wait_ge(a3["probs"], at(base + n + 1, c, 8))
                    if c is not None or n + base >= 2:
                        pe.wait_ge(a3["pt"], at(base + n - 1, c, 8))
                    for j in range(b + 1):
                        mm = nc.tensor.transpose(ps[:, 4 + n % 2, j * P:(j + 1) * P],
                                                 at3["e"][:, 2 * (n % DIFF_SLOTS), j * P:(j + 1) * P], ident)
                    mm.then_inc(a3["turned"], 1)

                def weigh(n):
                    s, b = n // TB, n % TB
                    pe.wait_ge(a3["pt"], at(base + n + 1, c, 8))
                    if b == 0:
                        pe.wait_ge(a3["v_staged"], at(base // TB + s + 1, c, 2))
                        pe.wait_ge(a3["out"], at(base // TB + s + 1, c, 2))
                    vh, vl = at3[f"vhi{s % 2}"], at3[f"vlo{s % 2}"]
                    for j in range(b + 1):
                        cols = slice(j * P, (j + 1) * P)
                        mm = product(ps[:, 6, b * P:(b + 1) * P], vh[:, cols], vl[:, cols],
                                     at3["pt_hi"][:, n % 2, cols], at3["pt_lo"][:, n % 2, cols], j == 0, j == b)
                    mm.then_inc(a3["pv"], 1)

                if live(n - 4, c, base):
                    turn(n - 4)
                if live(n, c, base):
                    scores(n)
                if base == 0:
                    p = 4 + n // 2
                    if n % 2 == 0:
                        pe.wait_ge(kv["qk"], at(p, c, 4))
                    half_panel(qk0 + p, c, ps[:, 7, :], *qk_input(p), n % 2)
                if live(n - 6, c, base):
                    weigh(n - 6)
                if n >= 8:
                    head_sums(n - 8)

            def head_sums(h):
                if h == 0:
                    pe.wait_ge(a3["least"], 8 * N_DIFF - 2)
                pe.wait_ge(a3["sq"], h + 1)
                pick = con[:, CAT["pick"] + N_DIFF - 1 - h:CAT["pick"] + 2 * N_DIFF - 1 - h]
                nc.tensor.matmul(ps[0:N_DIFF, 0, :], pick, squares[:, h % 2, :], start=h == 0,
                                 stop=h == N_DIFF - 1).then_inc(a3["summed"], 1)

            diff_turns(pe, diff_item, 6)
            for h in range(6, N_DIFF):
                head_sums(h)
            pe.wait_ge(a3["least"], 8 * N_DIFF)
            pe.wait_ge(loads["alibi"], 2 * 16)
            pe.wait_ge(a3["rms"], 2)
            for h in range(N_DIFF):
                if h >= 4:
                    pe.wait_ge(a3["normed"], h - 3)
                pick = da["picks"][:, h * P:(h + 1) * P]
                nc.tensor.matmul(ps[:, h % 4, :], pick, da["rms"], start=True, stop=True).then_inc(a3["spread"], 1)
            into_residual("bo", KC, 4, xg_hi, xg_lo, a3["out_lo"], lambda k: k + 1, {0: (a3["out"], N_DIFF + 1), 3: (kv["qk"], 2 * KC), 4: (a3["normed"], N_DIFF)})

            st = ffn_stages["gu1"]
            hidden("gu1", "ffn1", st, 4)
            into_residual("down1", FC, 6, ffn["hi"], ffn["lo"], st["hid"], lambda k: k + 1,
                          {0: (r_ready, NORM["ffn1"] + 1), 6: (st["scaled"], 2 * FC - 1), 7: (st["scaled"], 2 * FC)})
            pe.wait_ge(x_ready, KC * NORM["final"])
            square_sums("final", 0)

        @block.scalar
        def _(act):
            def split(u, i=None):
                if u >= N_UNITS:
                    return
                act.wait_ge(w_loaded[u % 2], at(16 * (u // 2 + 1), i, 16))
                if u >= 2:
                    act.wait_ge(used, at(u - 1, i, 2))
                nc.scalar.activation(w_hi[:, u % 2, :], w_raw[:, u % 2, :], ACT.Copy).then_inc(w_hi_ready, 1)

            def norm_input(norm, gain, finals_only=False):
                n = NORM[norm]
                for c in range(KC):
                    if n == 0:
                        act.wait_ge(loads["input"], 2 * 16)
                    else:
                        act.wait_ge(x_ready, KC * (n - 1) + c + 1)
                    if not finals_only:
                        nc.scalar.activation(xg_hi[:, c, :], x[:, c, :], ACT.Copy, scale=column(gain, c)).then_inc(xg_hi_ready, 1)
                    k = KC * n + c
                    if k >= 2:
                        act.wait_ge(summed, k - 1)
                    nc.scalar.activation(squares[:, c % 2, :], x[:, c, :], ACT.Square).then_inc(sq_ready, 1)

            def norm_rms(norm, bank=None, rows_bank=None):
                n = NORM[norm]
                if norm == "a":
                    act.wait_ge(a_in["first"], 4)
                    nc.scalar.activation(first["sums"][:], first["sums"][:], ACT.Sqrt, bias=column("eps"), scale=1.0 / D).then_inc(rms_ready, 1)
                    nc.scalar.activation(first["sums_rows"][:], first["sums_rows"][:], ACT.Sqrt, bias=column("eps"),
                                         scale=1.0 / D).then_inc(rows_rms_ready, 1)
                    return
                act.wait_ge(sums_ready, n + 1)
                if rows_bank is not None:
                    act.wait_ge(rows_sums_ready, ROWS[norm] + 1)
                nc.scalar.activation(square_sum[:], ps[:, bank, :], ACT.Sqrt, bias=column("eps"), scale=1.0 / D).then_inc(rms_ready, 1)
                if rows_bank is not None:
                    if ROWS[norm]:
                        act.wait_ge(rows_ready, ROWS[norm])
                    nc.scalar.activation(rms_rows[:], ps[:, rows_bank, 0:TB], ACT.Sqrt, bias=column("eps"),
                                         scale=1.0 / D).then_inc(rows_rms_ready, 1)

            def splits_of(name, n, skip_last=0):
                u0 = FIRST[name]
                with act.Fori(0, n // 2 - 1) as i:
                    split(u0 + 2, i)
                    split(u0 + 3, i)
                split(u0 + n)
                if not skip_last:
                    split(u0 + n + 1)

            def into_residual(name, n, norm, gain):
                splits_of(name, n, 1)
                norm_input(norm, gain, gain is None)
                split(FIRST[name] + n + 1)

            act.dma_start(con[:], consts).then_inc(loads["con"], 16)
            act.wait_ge(rot["steps"], 11)
            nc.scalar.activation(rope["sin"][:], rope["red"][:], ACT.Sin).then_inc(rot["trig"], 1)
            nc.scalar.activation(rope["cos"][:], rope["ang"][:], ACT.Sin).then_inc(rot["trig"], 1)
            split(0)
            norm_input("mix", "g_mix")
            split(1)
            norm_rms("mix", 2, 3)
            u0 = FIRST["w_in"]
            split(u0 + 2)
            act.wait_ge(lams["dots"], 4)
            nc.scalar.activation(lam_exp[:], lam_dot[:], ACT.Exp).then_inc(lams["exps"], 1)
            with act.Fori(0, 4) as i:
                split(u0 + 3, i)
                split(u0 + 4, i)
            act.wait_ge(w_in["evacuated"], 1)
            nc.scalar.activation(rope["g1"][0:N_FORGET, :], mix["proj"][0:N_FORGET, 0, :], ACT.Abs,
                                 bias=column("b_forget", 0, slice(0, N_FORGET))).then_inc(gate["abs"], 1)
            act.wait_ge(gate["abs"], 1)
            nc.scalar.activation(rope["g2"][0:N_FORGET, :], rope["g1"][0:N_FORGET, :], ACT.Exp, scale=-1.0).then_inc(gate["exp"], 1)
            with act.Fori(0, 5) as i:
                split(u0 + 11, i)
                split(u0 + 12, i)
            for c in range(GC):
                act.wait_ge(small["conv"], c + 1)
                nc.scalar.activation(mix["hi"][:, c, :], mix["proj"][:, 1 + c, :], ACT.Copy).then_inc(small["hi"], 1)
            for c in range(GC):
                act.wait_ge(small["product"], c + 1)
                nc.scalar.activation(mix["hi"][:, GC + c, :], ps[:, c, :], ACT.Copy, scale=column("pool_scale", c)).then_inc(small["hi"], 1)
            split(u0 + 21)
            split(u0 + 22)
            act.wait_ge(gate["turned"], 1)
            nc.scalar.activation(mix["nci"][:].rearrange("p b h -> p (b h)"), ps[:, 2, 0:TB * N_FORGET], ACT.Copy,
                                 scale=-1.0).then_inc(gate["rows"], 1)
            act.wait_ge(mix_ready, 4)
            for h in range(N_FORGET):
                act.wait_ge(gate["turned"], h + 2)
                nc.scalar.activation(mix["proj"][:, 1 + h, :], ps[:, h % 2, :], ACT.Copy).then_inc(gate["rows"], 1)

            def exps_and_turned(a, buf, n_items, exp, hi, extra=None):
                for m in range(n_items + 4):
                    if m < n_items:
                        exp(m)
                    if 0 <= m - 2 < n_items:
                        hi(m - 2)
                    if extra is not None:
                        extra(m - 4)

            act.wait_ge(rot["done"], 4)
            act.wait_ge(w_in["evacuated"], 17)
            act.wait_ge(w_in["v_ready"], TB)
            with act.Fori(0, GC) as c:
                for s in range(2):
                    parts = ((f"qhi{s}", mix["proj"][:, bass.ds(9 + 4 * s + c, 1), :], -HD ** -0.5),
                             (f"khi{s}", mix["proj"][:, bass.ds(11 + 4 * s + c, 1), :], 1.0),
                             (f"vhi{s}", mix["v"][:, :, bass.ds(G * s + c * P, P)], 1.0))
                    for name, src, scale in parts:
                        to = at1[name][:].rearrange("p (a n) -> p a n", a=src.shape[1])
                        nc.scalar.activation(to, src, ACT.Copy, scale=scale).then_inc(a1["staged_hi"], 1)

                def exp(n):
                    act.wait_ge(a1["least"], at(n + 1, c, 16))
                    w = P * (n % 8 // 2 + 1)
                    nc.scalar.activation(at1["e"][:, n % 3, 0:w], at1["e"][:, n % 3, 0:w], ACT.Exp, scale=-1.0,
                                         bias=at1["least"][:, n % 3:n % 3 + 1],
                                         accum_out=at1["sums"][:, n % 3:n % 3 + 1]).then_inc(a1["exps"], 1)

                def hi(n):
                    act.wait_ge(a1["turned"], at(n + 1, c, 16))
                    if n >= 2:
                        act.wait_ge(a1["pv"], at(n - 1, c, 16))
                    w = P * (n % 8 // 2 + 1)
                    nc.scalar.activation(at1["pt_hi"][:, n % 2, 0:w], ps[:, 2 + n % 2, 0:w], ACT.Copy).then_inc(a1["pt_hi"], 1)

                def outputs(n):
                    if n not in (7, 15):
                        return
                    s = n // 8
                    act.wait_ge(a1["pv"], at(n + 1, c, 16))
                    for h in range(2):
                        rows = slice(HD * h, HD * h + HD)
                        nc.scalar.activation(mix["hi"][rows, bass.ds(4 + s + c * 2, 1), :].rearrange("p a n -> p (a n)"),
                                             ps[rows, 4 + 2 * s + h, :], ACT.Copy).then_inc(a1["out_hi"], 1)

                exps_and_turned(a1, at1, 16, exp, hi, outputs)

            act.wait_ge(mix_ready, 8)
            act.wait_ge(a1["pt"], 32)
            act.dma_start(memory["x"][:], mem_cols).then_inc(loads["mem"], 16)
            u0 = FIRST["w_out"]
            split(u0 + 2)
            act.wait_ge(loads["mem"], 16)
            for c in range(KC):
                nc.scalar.activation(memory["hi"][:, c, :], memory["x"][:, c, :], ACT.Copy, scale=column("g_mem", c)).then_inc(mem["hi"], 1)
                if c >= 2:
                    act.wait_ge(mem["summed"], c - 1)
                nc.scalar.activation(memory["sq"][:, c % 2, :], memory["x"][:, c, :], ACT.Square).then_inc(mem["sq"], 1)
            for u in range(u0 + 3, u0 + KC + 1):
                split(u)
            norm_input("xa", "g_xa")
            split(u0 + KC + 1)
            act.wait_ge(mem["sums"], 2)
            nc.scalar.activation(memory["rms"][:], ps[:, 6, 0:M], ACT.Sqrt, bias=column("eps"), scale=1.0 / D).then_inc(mem["rms"], 1)
            nc.scalar.activation(memory["rms_rows"][:], ps[:, 7, 0:MB], ACT.Sqrt, bias=column("eps"), scale=1.0 / D).then_inc(mem["rms"], 1)
            splits_of("mem_k", KC)
            splits_of("mem_v", KC)
            act.wait_ge(used, FIRST["mem_v"] + KC)
            act.wait_ge(mem["r"], 2)
            for b in range(MB):
                for h in range(2):
                    nc.scalar.activation(xa["v"][:, b, h * S:(h + 1) * S], ps[:, 2 + 2 * b + h, :], ACT.Copy,
                                         scale=xa["r_rows"][:, b:b + 1]).then_inc(mem["v_ready"], 1)
            norm_rms("xa", 6)
            splits_of("xq", KC)
            act.wait_ge(xqs["ready"], KC)
            act.wait_ge(mem["v_ready"], 2 * MB)
            with act.Fori(0, XA_HEADS // 2) as c:
                for s in range(2):
                    parts = ((f"qhi{s}", xa["q"][:, bass.ds(c * (2 * XC) + XC * s, XC), :], -(XC * P) ** -0.5),
                             (f"khi{s}", xa["k"][:, bass.ds(c * (2 * XC) + XC * s, XC), :], 1.0),
                             (f"vhi{s}", xa["v"][:, :, bass.ds(c * (2 * XC * P) + XC * P * s, XC * P)], 1.0))
                    for name, src, scale in parts:
                        to = at2[name][:].rearrange("p (a n) -> p a n", a=src.shape[1])
                        nc.scalar.activation(to, src, ACT.Copy, scale=scale).then_inc(a2["staged_hi"], 1)

                def exp(n):
                    if n >= 3:
                        act.wait_ge(a2["turned"], at(n - 2, c, 8))
                    act.wait_ge(a2["least"], at(n + 1, c, 8))
                    nc.scalar.activation(at2["e"][:, n % 3, :], ps[:, n % 2, 0:M], ACT.Exp, scale=-1.0,
                                         bias=at2["least"][:, n % 3:n % 3 + 1],
                                         accum_out=at2["sums"][:, n % 3:n % 3 + 1]).then_inc(a2["exps"], 1)

                def hi(n):
                    act.wait_ge(a2["turned"], at(n + 1, c, 8))
                    if n >= 2:
                        act.wait_ge(a2["pv"], at(n - 1, c, 8))
                    nc.scalar.activation(at2["pt_hi"][:, n % 2, :], ps[:, 2 + n % 2, 0:M], ACT.Copy).then_inc(a2["pt_hi"], 1)

                def outputs(n):
                    if n not in (TB - 1, 2 * TB - 1):
                        return
                    s = n // TB
                    act.wait_ge(a2["pv"], at(n + 1, c, 8))
                    for d in range(XC):
                        nc.scalar.activation(xa["hi"][:, bass.ds(c * (2 * XC) + XC * s + d, 1), :].rearrange("p a n -> p (a n)"),
                                             ps[:, 4 + 2 * s + d, :], ACT.Copy).then_inc(a2["out_hi"], 1)

                exps_and_turned(a2, at2, 8, exp, hi, outputs)
            into_residual("xo", KC, "ffn", "g_ffn")

            st = ffn_stages["up"]
            norm_rms("ffn", 2)

            def conv_gate(i, done):
                act.wait_ge(st["steps"], at(4 * done + 4, i, 4))
                nc.scalar.activation(ffn["gate"][:], ffn["tg"][:], ACT.Silu).then_inc(st["gated"], 1)

            def conv_hidden(i, done):
                act.wait_ge(st["product"], at(done + 1, i, 1))
                nc.scalar.activation(ffn["hi"][:, bass.ds(at(done, i, 1), 1), :].rearrange("p a n -> p (a n)"), ffn["h"][:],
                                     ACT.Copy).then_inc(st["hid_hi"], 1)

            def conv_turn(i, first):
                u = FIRST["up"]
                if not first:
                    conv_gate(i, -1)
                for s, (src, to) in enumerate(((ffn["ua"], ffn["ta"]), (ffn["ug"], ffn["tg"]))):
                    split(u + 2 + s, i)
                    if s == 0 and not first:
                        act.wait_ge(st["product"], at(0, i, 1))
                    act.wait_ge(st["scaled"], at(s + 1, i, 2))
                    nc.scalar.activation(to[:], src[:, 2:S + 2], ACT.Copy,
                                         scale=column("w_ffconv", at(2 * 2 * FC + s * FC, i, 1))).then_inc(st["tapped"], 1)
                    if s == 0 and not first:
                        conv_hidden(i, -1)

            conv_turn(None, True)
            with act.Fori(1, FC) as i:
                conv_turn(i, False)
            conv_gate(None, FC - 1)
            conv_hidden(None, FC - 1)
            act.wait_ge(st["hid"], FC)
            act.dma_start(sg["w"][:], spatial).then_inc(loads["spatial"], 16)
            act.dma_start(sg["b"][:].rearrange("p g t -> p (g t)"), spatial_bias).then_inc(loads["spatial"], 16)
            into_residual("down", FC, "first", "a_gain")

            u0 = FIRST["a_v"]
            for c in range(KC):
                k = KC * NORM["a"] + c
                act.wait_ge(summed, k - 1)
                nc.scalar.activation(squares[:, c % 2, :], x[:, c, :], ACT.Square, scale=column("g_first", c)).then_inc(sq_ready, 1)
                if c == KC // 2:
                    split(u0 + 2)
            split(u0 + 3)
            norm_rms("first", 6, 7)
            split(u0 + 4)
            norm_rms("a")
            split(u0 + 5)
            for h in range(2):
                if h:
                    for u in range(u0 + 6, u0 + KC + 2):
                        split(u)
                act.wait_ge(used, u0 + 4 * h + 4)
                act.wait_ge(rows_ready, ROWS["a"] + 1)
                for b in range(TB):
                    bank = ((2, 3, 4, 5), (6, 7, 0, 1))[h][b]
                    nc.scalar.activation(sg["v"][:, b, h * S:(h + 1) * S], ps[:, bank, :], ACT.Gelu_apprx_tanh,
                                         scale=r_rows[:, b:b + 1], accum_out=sg["v_sum"][:, b, h:h + 1]).then_inc(a_in["v"], 1)
            u0 = FIRST["a_u"]

            def gate_panel(s, i):
                act.wait_ge(a_in["scaled"], at(s + 1, i, 2))
                ut = sg["u"][:, bass.ds(at(s, i, 2), 1), :].rearrange("p a n -> p (a n)")
                nc.scalar.activation(ut, ut, ACT.Gelu_apprx_tanh).then_inc(a_in["u"], 1)
                split(u0 + 2 + s, i)

            for b in range(TB):
                act.wait_ge(a_in["steps"], 2)
                nc.scalar.activation(sg["hi"][:, 2 * b:2 * b + 2, :], sg["v"][:, b, :].rearrange("p (a n) -> p a n", a=2),
                                     ACT.Square, bias=sg["mean"][:, b:b + 1], accum_out=sg["v_sq"][:, b:b + 1]).then_inc(a_in["v_sq"], 1)
            gate_panel(0, None)
            act.wait_ge(a_in["v_sq"], TB)
            nc.scalar.activation(sg["std"][:], sg["v_sq"][:], ACT.Sqrt, bias=column("eps"), scale=1.0 / D).then_inc(a_in["std"], 1)
            act.wait_ge(a_in["w"], 1)
            nc.scalar.activation(sg["w_hi"][:], sg["w"][:], ACT.Copy).then_inc(a_in["w_hi"], 1)
            gate_panel(1, None)
            for b in range(TB):
                act.wait_ge(a_in["normed"], b + 1)
                nc.scalar.activation(sg["v_hi"][:, b, :], sg["v"][:, b, :], ACT.Copy).then_inc(a_in["v_hi"], 1)
            with act.Fori(1, KC // 2) as i:
                for s in range(2):
                    gate_panel(s, i)
            for g in range(N_SPATIAL):
                act.wait_ge(a_in["product"], g + 1)
                nc.scalar.activation(sg["hi"][:, g, :], sg["u"][:, g, :], ACT.Copy).then_inc(a_in["hi"], 1)
            into_residual("a_out", KC, "ffn0", "ffn_norm0")

            def swiglu(name, norm, base):
                st = ffn_stages[name]
                norm_rms(norm, (base + 2) % 8)
                with act.Fori(0, FC) as i:
                    act.wait_ge(st["scaled"], at(1, i, 2))
                    nc.scalar.activation(ffn["gate"][:], ffn["tg"][:], ACT.Silu).then_inc(st["gated"], 1)
                    split(FIRST[name] + 2, i)
                    split(FIRST[name] + 3, i)
                    act.wait_ge(st["product"], at(1, i, 1))
                    nc.scalar.activation(ffn["hi"][:, bass.ds(at(0, i, 1), 1), :].rearrange("p a n -> p (a n)"), ffn["h"][:],
                                         ACT.Copy).then_inc(st["hid_hi"], 1)

            swiglu("gu0", "ffn0", 0)
            into_residual("down0", FC, "kv", "kv_norm")

            act.dma_start(da["alibi"][:], alibi_table).then_inc(loads["alibi"], 16)
            u0 = FIRST["kv_v"]
            split(u0 + 2)
            norm_rms("kv", 6, 7)
            for h in range(2):
                for u in range(u0 + 4 * h + (h == 0), u0 + 4 * h + 4):
                    split(u + 2)
                    if h:
                        for c in range(2 * (u - u0 - 4), 2 * (u - u0 - 4) + 2):
                            nc.scalar.activation(da["xb_hi"][:, c, :], x[:, c, :], ACT.Copy,
                                                 scale=column("b_norm", c)).then_inc(kv["xb_hi"], 1)
                act.wait_ge(used, u0 + 4 * h + 4)
                act.wait_ge(rows_ready, ROWS["kv"] + 1)
                for b in range(TB):
                    bank = ((2, 3, 4, 5), (6, 7, 0, 1))[h][b]
                    nc.scalar.activation(da["v"][:, b, h * S:(h + 1) * S], ps[:, bank, :], ACT.Copy,
                                         scale=r_rows[:, b:b + 1]).then_inc(kv["v"], 1)
            qk0 = FIRST["qk"]
            for p in range(4):
                split(qk0 + p + 2)

            def diff_item(n, c, base):
                def hi(n):
                    act.wait_ge(a3["turned"], at(base + n + 1, c, 8))
                    if c is not None or n + base >= 2:
                        act.wait_ge(a3["pv"], at(base + n - 1, c, 8))
                    w = P * (n % TB + 1)
                    nc.scalar.activation(at3["pt_hi"][:, n % 2, 0:w], ps[:, 4 + n % 2, 0:w], ACT.Copy).then_inc(a3["pt_hi"], 1)

                def exp(n):
                    w = P * (n % TB + 1)
                    for h in range(2):
                        k = 2 * (n % DIFF_SLOTS) + h
                        act.wait_ge(a3["least"], at(2 * (base + n) + h + 1, c, 16))
                        nc.scalar.activation(at3["e"][:, k, 0:w], at3["e"][:, k, 0:w], ACT.Exp, scale=-1.0,
                                             bias=at3["least"][:, k:k + 1], accum_out=at3["sums"][:, k:k + 1]).then_inc(a3["exps"], 1)

                def second(n):
                    act.wait_ge(a3["second"], at(base + n + 1, c, 8))
                    w = P * (n % TB + 1)
                    k = 2 * (n % DIFF_SLOTS) + 1
                    nc.scalar.activation(at3["e"][:, k, 0:w], at3["e"][:, k, 0:w], ACT.Copy,
                                         scale=at3["second"][:, k:k + 1]).then_inc(a3["weighed"], 1)

                def output(n):
                    s = n // TB
                    act.wait_ge(a3["pv"], at(base + n + 1, c, 8))
                    h = bass.ds(at(base // TB + s, c, 2), 1)
                    nc.scalar.activation(da["o"][:, h, :].rearrange("p a n -> p (a n)"), ps[:, 6, :],
                                         ACT.Copy).then_inc(a3["out"], 1)

                if live(n - 5, c, base):
                    hi(n - 5)
                if n % TB == 2 and live(n - 7, c, base):
                    output(n - 7)
                if live(n - 1, c, base):
                    exp(n - 1)
                if live(n - 2, c, base):
                    second(n - 2)
                if qk_due(n, c, base):
                    split_qk(n, c, base)
                if n >= 8:
                    head_square(n - 8)

            def split_qk(n, c, base):
                u = qk0 + 3 + (base + n) // 2 + 2
                act.wait_ge(w_loaded[u % 2], at(16 * (u // 2 + 1), c, 32))
                act.wait_ge(used, at(u - 1, c, 4))
                nc.scalar.activation(w_hi[:, u % 2, :], w_raw[:, u % 2, :], ACT.Copy).then_inc(w_hi_ready, 1)

            def head_square(h):
                if h == 0:
                    act.wait_ge(a3["staged"], 2 * N_DIFF)
                act.wait_ge(a3["out"], h + 2)
                if h >= 2:
                    act.wait_ge(a3["summed"], h - 1)
                nc.scalar.activation(squares[:, h % 2, :], da["o"][:, h, :], ACT.Square).then_inc(a3["sq"], 1)

            act.sem_inc(a3["out"], 1)
            diff_turns(act, diff_item, 7)
            act.wait_ge(a3["turned"], 4 * N_DIFF)
            act.dma_start(da["picks"], head_picks).then_inc(loads["alibi"], 16)
            head_square(N_DIFF - 1)
            act.wait_ge(a3["summed"], N_DIFF)
            nc.scalar.activation(da["rms"], ps[0:N_DIFF, 0, :], ACT.Sqrt, bias=column("eps", 0, slice(0, N_DIFF)),
                                 scale=1.0 / P).then_inc(a3["rms"], 1)
            for h in range(N_DIFF):
                act.wait_ge(a3["normed"], h + 1)
                nc.scalar.activation(xg_hi[:, h, :], da["o"][:, h, :], ACT.Copy).then_inc(a3["out_hi"], 1)
            into_residual("bo", KC, "ffn1", "ffn_norm1")
            swiglu("gu1", "ffn1", 4)
            into_residual("down1", FC, "final", None)
            norm_rms("final", 0)

        @block.vector
        def _(dve):
            def split(u, i=None):
                if u >= N_UNITS:
                    return
                dve.wait_ge(w_hi_ready, at(u + 1, i, 2))
                nc.vector.tensor_tensor(w_lo[:, u % 2, :], w_raw[:, u % 2, :], w_hi[:, u % 2, :].bitcast(F32),
                                        ALU.subtract).then_inc(w_ready, 1)

            def gained(norm, gain, c):
                dve.wait_ge(xg_hi_ready, KC * SPLIT[norm] + c + 1)
                nc.vector.scalar_tensor_tensor(out=xg_lo[:, c, :], in0=x[:, c, :], scalar=column(gain, c),
                                               in1=xg_hi[:, c, :].bitcast(F32), op0=ALU.mult,
                                               op1=ALU.subtract).then_inc(xg_ready, 1)

            def norm_r(norm, rows=False):
                n = NORM[norm]
                dve.wait_ge(rms_ready, n + 1)
                nc.vector.reciprocal(r_cols[:], square_sum[:]).then_inc(r_ready, 1)
                if rows:
                    dve.wait_ge(rows_rms_ready, ROWS[norm] + 1)
                    nc.vector.reciprocal(r_rows[:], rms_rows[:]).then_inc(rows_ready, 1)
                dve.wait_ge(r_ready, n + 1)

            def scaled(to, bank, signal, cols=S, r=None):
                return nc.vector.tensor_tensor(to, ps[:, bank, 0:cols], r_cols[:] if r is None else r,
                                               ALU.mult).then_inc(signal, 1)

            def chunk(t, c):
                return t[:, bass.ds(c, 1), :].rearrange("p a n -> p (a n)")

            def splits_of(name, n, skip_last=0):
                u0 = FIRST[name]
                with dve.Fori(0, n // 2 - 1) as i:
                    split(u0 + 2, i)
                    split(u0 + 3, i)
                split(u0 + n)
                if not skip_last:
                    split(u0 + n + 1)

            def into_residual(name, n, norm, gain, bank0, final_splits=True):
                if final_splits:
                    splits_of(name, n, 1)
                done = KC * (NORM[norm] - 1)
                for j in range(KC + 1):
                    if j < KC:
                        if j < KC - 1:
                            dve.wait_ge(proj_sums, (KC - 1) * RESIDUALS.index(name) + j + 1)
                        else:
                            dve.wait_ge(used, FIRST[name] + n)
                        nc.vector.tensor_tensor(x[:, j, :], ps[:, (bank0 + j) % 8, :], x[:, j, :],
                                                ALU.add).then_inc(x_ready, 1)
                    if j and gain is not None:
                        gained(norm, gain, j - 1)
                split(FIRST[name] + n + 1)

            counted = [0]

            def step(ins, s):
                counted[0] += 1
                ins.then_inc(s, 1)
                dve.wait_ge(s, counted[0])

            dve.wait_ge(loads["early"], 16 * N_EARLY)
            dve.wait_ge(loads["input"], 2 * 16)
            ang, turns, red = rope["ang"][:], rope["turns"][:], rope["red"][:]
            step(nc.vector.tensor_copy(ang, rope["pos"][:]), rot["steps"])
            step(nc.vector.tensor_scalar(ang, ang, column("inv_freq"), None, ALU.mult), rot["steps"])
            step(nc.vector.tensor_scalar(turns, ang, 1.0 / TWO_PI, ROUNDER, ALU.mult, ALU.add), rot["steps"])
            step(nc.vector.tensor_scalar(turns, turns, -ROUNDER, None, ALU.add), rot["steps"])
            for part, src in ((TURN_1, ang), (TURN_2, red), (TURN_3, red), (TURN_4, red)):
                step(nc.vector.scalar_tensor_tensor(out=red, in0=turns, scalar=-part, in1=src, op0=ALU.mult,
                                                    op1=ALU.add), rot["steps"])
            step(nc.vector.tensor_scalar(red, red, PI_BELOW, -PI_BELOW, ALU.min, ALU.max), rot["steps"])
            step(nc.vector.scalar_tensor_tensor(out=ang, in0=red, scalar=-1.0, in1=red, op0=ALU.mult, op1=ALU.max), rot["steps"])
            step(nc.vector.tensor_scalar(ang, ang, -1.0, math.pi / 2, ALU.mult, ALU.add), rot["steps"])
            split(0)
            for c in range(KC):
                if c == 0:
                    dve.wait_ge(loads["input"], 2 * 16)
                gained("mix", "g_mix", c)
            split(1)
            dve.wait_ge(loads["early"], 16 * N_EARLY)
            for h in range(2):
                a, b = (lam_in[:, (2 * h + k) * HD:(2 * h + k + 1) * HD] for k in range(2))
                nc.vector.tensor_tensor_reduce(a, a, b, 1.0, 0.0, ALU.mult, ALU.add, lam_dot[:, h:h + 1]).then_inc(lams["dots"], 1)
            nc.vector.tensor_tensor(par[:, AT["a_gain"]:AT["a_gain"] + KC], par[:, AT["g_first"]:AT["g_first"] + KC],
                                    par[:, AT["a_norm"]:AT["a_norm"] + KC], ALU.mult).then_inc(lams["dots"], 1)
            nc.vector.tensor_scalar(subln[:], column("b_subln"), 1.0 - LAMBDA_INIT, None, ALU.mult).then_inc(lams["dots"], 1)
            norm_r("mix", True)
            u0 = FIRST["w_in"]
            dve.wait_ge(used, u0 + 1)
            scaled(mix["proj"][:, 0, :], 0, w_in["evacuated"])
            split(u0 + 2)
            with dve.Fori(0, 4) as i:
                for s in range(2):
                    dve.wait_ge(used, at(u0 + 2 + s, i, 2))
                    scaled(chunk(mix["proj"], at(1 + s, i, 2)), 1 - s, w_in["evacuated"])
                    split(u0 + 3 + s, i)
            dve.wait_ge(lams["exps"], 1)
            nc.vector.tensor_scalar(lam[:], lam_exp[:, 0:1], lam_exp[:, 1:2], LAMBDA_INIT, ALU.subtract,
                                    ALU.add).then_inc(lams["done"], 1)

            counted[0] = 0
            g1, g2, g3, g4 = (t[0:N_FORGET, :] for t in (rope["g1"], rope["g2"], rope["g3"], rope["g4"]))

            def gate_steps(p):
                if p == 0:
                    step(nc.vector.tensor_scalar(g3, g2, 2.0, None, ALU.add), gate["steps"])
                    step(nc.vector.reciprocal(g1, g3), gate["steps"])
                if p == 1:
                    step(nc.vector.tensor_tensor(g3, g2, g1, ALU.mult), gate["steps"])
                    step(nc.vector.tensor_tensor(g4, g3, g3, ALU.mult), gate["steps"])
                if p == 2:
                    step(nc.vector.tensor_scalar(g1, g4, 1.0 / 15, None, ALU.mult), gate["steps"])
                if 2 <= p < 5:
                    for k in (13 - 4 * (p - 2), 11 - 4 * (p - 2)):
                        step(nc.vector.scalar_tensor_tensor(out=g1, in0=g1, scalar=1.0 / k, in1=g4, op0=ALU.add,
                                                            op1=ALU.mult), gate["steps"])
                if p == 5:
                    step(nc.vector.scalar_tensor_tensor(out=g1, in0=g1, scalar=1.0, in1=g3, op0=ALU.add, op1=ALU.mult),
                         gate["steps"])
                    step(nc.vector.tensor_scalar(g2, mix["proj"][0:N_FORGET, 0, :], column("b_forget", 0, slice(0, N_FORGET)),
                                                 0.0, ALU.add, ALU.min), gate["steps"])
                if p == 6:
                    step(nc.vector.scalar_tensor_tensor(out=g2, in0=g1, scalar=-2.0, in1=g2, op0=ALU.mult, op1=ALU.add),
                         gate["steps"])
                    step(nc.vector.memset(g3, 1.0), gate["steps"])
                if p == 7:
                    nc.vector.tensor_tensor_scan(mix["c_rows"][0:N_FORGET, :], g3, g2, 0.0, ALU.mult, ALU.add).then_inc(gate["c"], 1)

            dve.wait_ge(gate["exp"], 1)
            for p in range(8):
                dve.wait_ge(used, u0 + 10 + p)
                scaled(mix["proj"][:, 9 + p, :], 1 - p % 2, w_in["evacuated"])
                split(u0 + 11 + p)
                gate_steps(p)
            split(u0 + 19)
            dve.wait_ge(rot["trig"], 2)
            for c in range(4):
                if c == 1:
                    split(u0 + 20)
                pc = mix["proj"][:, 9 + c, :]
                dve.wait_ge(rot["swapped"], c + 1)
                if c:
                    dve.wait_ge(rot["done"], c)
                nc.vector.tensor_tensor(rope["prod"][:], ps[:, 2 + c % 2, :], rope["sin"][:], ALU.mult).then_inc(rot["prod"], 1)
                nc.vector.tensor_tensor(pc, pc, rope["cos"][:], ALU.mult).then_inc(rot["prod_cos"], 1)
                dve.wait_ge(rot["prod_cos"], c + 1)
                dve.wait_ge(rot["prod"], c + 1)
                nc.vector.tensor_tensor(pc, pc, rope["prod"][:], ALU.add).then_inc(rot["done"], 1)
            for c in range(GC):
                dve.wait_ge(small["hi"], c + 1)
                nc.vector.tensor_tensor(mix["lo"][:, c, :], mix["proj"][:, 1 + c, :], mix["hi"][:, c, :].bitcast(F32),
                                        ALU.subtract).then_inc(mix_ready, 1)
            for c in range(GC):
                dve.wait_ge(small["hi"], GC + c + 1)
                nc.vector.scalar_tensor_tensor(out=mix["lo"][:, GC + c, :], in0=ps[:, c, :], scalar=column("pool_scale", c),
                                               in1=mix["hi"][:, GC + c, :].bitcast(F32), op0=ALU.mult,
                                               op1=ALU.subtract).then_inc(mix_ready, 1)
            split(u0 + 21)
            dve.wait_ge(used, u0 + 21)
            for b in range(TB):
                nc.vector.tensor_scalar(mix["v"][:, b, :], ps[:, 4 + b, :], r_rows[:, b:b + 1], None,
                                        ALU.mult).then_inc(w_in["v_ready"], 1)
            split(u0 + 22)

            def staging(a, buf, c, n_done, parts):
                for k, (name, src, scale) in enumerate(parts):
                    dve.wait_ge(a["staged_hi"], at(n_done + k + 1, c, 6))
                    n = src.shape[1]
                    hi = buf[name.replace("lo", "hi")][:].bitcast(F32).rearrange("p (a n) -> p a n", a=n)
                    lo = buf[name][:].rearrange("p (a n) -> p a n", a=n)
                    if scale is None:
                        ins = nc.vector.tensor_tensor(lo, src, hi, ALU.subtract)
                    else:
                        ins = nc.vector.scalar_tensor_tensor(out=lo, in0=src, scalar=scale, in1=hi, op0=ALU.mult,
                                                             op1=ALU.subtract)
                ins.then_inc(a["staged"], 1)

            def softmax_turn(n_items, least, probs, lo, outputs):
                for m in range(n_items + 4):
                    if m < n_items:
                        least(m)
                    if 0 <= m - 1 < n_items:
                        probs(m - 1)
                    if 0 <= m - 2 < n_items:
                        lo(m - 2)
                    outputs(m - 4)

            dve.wait_ge(loads["tables"], 16 * N_TABLES)
            dve.wait_ge(rot["done"], 4)
            dve.wait_ge(w_in["v_ready"], TB)
            with dve.Fori(0, GC) as c:
                for s in range(2):
                    staging(a1, at1, c, 3 * s, ((f"qlo{s}", mix["proj"][:, bass.ds(9 + 4 * s + c, 1), :], -HD ** -0.5),
                                                (f"klo{s}", mix["proj"][:, bass.ds(11 + 4 * s + c, 1), :], None),
                                                (f"vlo{s}", mix["v"][:, :, bass.ds(G * s + c * P, P)], None)))

                def least(n):
                    s, b = n // 8, n % 8 // 2
                    w = P * (b + 1)
                    if n >= 3:
                        dve.wait_ge(a1["turned"], at(n - 2, c, 16))
                    if s:
                        dve.wait_ge(a1["bias"], at(n - 7, c, 8))
                        bias = mix["proj"][:, 5 + n % 2, 0:w]
                    else:
                        bias = mix["dil"][:, S - P - b * P:S - P - b * P + w]
                    item = dve.to_reg(at(n + 1, c, 16))
                    dve.wait_ge(loads["tables"], 16 * N_TABLES)
                    dve.wait_ge(a1["scores"], item)
                    nc.vector.tensor_tensor_reduce(at1["e"][:, n % 3, 0:w], ps[:, n % 2, 0:w], bias, 1.0, FAR, ALU.add,
                                                   ALU.min, at1["least"][:, n % 3:n % 3 + 1]).then_inc(a1["least"], 1)

                def probs(n):
                    w = P * (n % 8 // 2 + 1)
                    k = n % 3
                    dve.wait_ge(a1["exps"], at(n + 1, c, 16))
                    nc.vector.reciprocal(at1["inv"][:, k:k + 1], at1["sums"][:, k:k + 1]).then_inc(a1["inv"], 1)
                    dve.wait_ge(a1["inv"], at(n + 1, c, 16))
                    nc.vector.tensor_scalar(at1["e"][:, k, 0:w], at1["e"][:, k, 0:w], at1["inv"][:, k:k + 1], None,
                                            ALU.mult).then_inc(a1["probs"], 1)

                def lo(n):
                    w = P * (n % 8 // 2 + 1)
                    dve.wait_ge(a1["pt_hi"], at(n + 1, c, 16))
                    nc.vector.tensor_tensor(at1["pt_lo"][:, n % 2, 0:w], ps[:, 2 + n % 2, 0:w],
                                            at1["pt_hi"][:, n % 2, 0:w].bitcast(F32), ALU.subtract).then_inc(a1["pt"], 1)

                def outputs(n):
                    if n not in (7, 15):
                        return
                    s = n // 8
                    dve.wait_ge(a1["out_hi"], at(2 * s + 2, c, 4))
                    for h in range(2):
                        rows = slice(HD * h, HD * h + HD)
                        at_ = bass.ds(4 + s + c * 2, 1)
                        ins = nc.vector.tensor_tensor(mix["lo"][rows, at_, :].rearrange("p a n -> p (a n)"),
                                                      ps[rows, 4 + 2 * s + h, :],
                                                      mix["hi"][rows, at_, :].rearrange("p a n -> p (a n)").bitcast(F32),
                                                      ALU.subtract)
                    ins.then_inc(mix_ready, 1)

                softmax_turn(16, least, probs, lo, outputs)

            u0 = FIRST["w_out"]
            split(u0 + 2)
            for c in range(KC):
                dve.wait_ge(mem["hi"], c + 1)
                nc.vector.scalar_tensor_tensor(out=memory["lo"][:, c, :], in0=memory["x"][:, c, :], scalar=column("g_mem", c),
                                               in1=memory["hi"][:, c, :].bitcast(F32), op0=ALU.mult,
                                               op1=ALU.subtract).then_inc(mem["lo"], 1)
            for u in range(u0 + 3, u0 + KC + 1):
                split(u)
            into_residual("w_out", KC, "xa", "g_xa", 0, False)
            dve.wait_ge(mem["rms"], 2)
            nc.vector.reciprocal(xa["r_cols"][:], memory["rms"][:]).then_inc(mem["r"], 1)
            nc.vector.reciprocal(xa["r_rows"][:], memory["rms_rows"][:]).then_inc(mem["r"], 1)
            dve.wait_ge(mem["r"], 2)
            u0 = FIRST["mem_k"]
            with dve.Fori(0, KC // 2) as i:
                for s in range(2):
                    dve.wait_ge(used, at(u0 + 1 + s, i, 2))
                    scaled(chunk(xa["k"], at(s, i, 2)), s, mem["k_ready"], M, xa["r_cols"][:])
                    split(u0 + 2 + s, i)
            splits_of("mem_v", KC)
            norm_r("xa")
            u0 = FIRST["xq"]
            with dve.Fori(0, KC // 2) as i:
                for s in range(2):
                    dve.wait_ge(used, at(u0 + 1 + s, i, 2))
                    scaled(chunk(xa["q"], at(s, i, 2)), s, xqs["ready"])
                    split(u0 + 2 + s, i)
            dve.wait_ge(xqs["ready"], KC)
            with dve.Fori(0, XA_HEADS // 2) as c:
                for s in range(2):
                    staging(a2, at2, c, 3 * s,
                            ((f"qlo{s}", xa["q"][:, bass.ds(c * (2 * XC) + XC * s, XC), :], -(XC * P) ** -0.5),
                             (f"klo{s}", xa["k"][:, bass.ds(c * (2 * XC) + XC * s, XC), :], None),
                             (f"vlo{s}", xa["v"][:, :, bass.ds(c * (2 * XC * P) + XC * P * s, XC * P)], None)))

                def least(n):
                    dve.wait_ge(a2["scores"], at(n + 1, c, 8))
                    nc.vector.tensor_reduce(at2["least"][:, n % 3:n % 3 + 1], ps[:, n % 2, 0:M], AX.X, ALU.min).then_inc(a2["least"], 1)

                def probs(n):
                    k = n % 3
                    dve.wait_ge(a2["exps"], at(n + 1, c, 8))
                    nc.vector.reciprocal(at2["inv"][:, k:k + 1], at2["sums"][:, k:k + 1]).then_inc(a2["inv"], 1)
                    dve.wait_ge(a2["inv"], at(n + 1, c, 8))
                    nc.vector.tensor_scalar(at2["e"][:, k, :], at2["e"][:, k, :], at2["inv"][:, k:k + 1], None,
                                            ALU.mult).then_inc(a2["probs"], 1)

                def lo(n):
                    dve.wait_ge(a2["pt_hi"], at(n + 1, c, 8))
                    nc.vector.tensor_tensor(at2["pt_lo"][:, n % 2, :], ps[:, 2 + n % 2, 0:M],
                                            at2["pt_hi"][:, n % 2, :].bitcast(F32), ALU.subtract).then_inc(a2["pt"], 1)

                def outputs(n):
                    if n not in (TB - 1, 2 * TB - 1):
                        return
                    s = n // TB
                    for d in range(XC):
                        dve.wait_ge(a2["out_hi"], at(XC * s + d + 1, c, 2 * XC))
                        at_ = c * (2 * XC) + XC * s + d
                        nc.vector.tensor_tensor(chunk(xa["lo"], at_), ps[:, 4 + 2 * s + d, :],
                                                chunk(xa["hi"], at_).bitcast(F32), ALU.subtract).then_inc(a2["out"], 1)

                softmax_turn(8, least, probs, lo, outputs)
            into_residual("xo", KC, "ffn", "g_ffn", 0)

            st = ffn_stages["up"]
            nc.vector.memset(ffn["ua"][:, 0:2], 0.0).then_inc(st["zero"], 1)
            nc.vector.memset(ffn["ug"][:, 0:2], 0.0).then_inc(st["zero"], 1)
            norm_r("ffn")
            dve.wait_ge(st["zero"], 2)
            def conv_product(i, done):
                dve.wait_ge(st["gated"], at(done + 1, i, 1))
                nc.vector.tensor_tensor(ffn["h"][:], ffn["ta"][:], ffn["gate"][:], ALU.mult).then_inc(st["product"], 1)

            def conv_lo(i, done):
                dve.wait_ge(st["hid_hi"], at(done + 1, i, 1))
                nc.vector.tensor_tensor(chunk(ffn["lo"], at(done, i, 1)), ffn["h"][:],
                                        chunk(ffn["hi"], at(done, i, 1)).bitcast(F32), ALU.subtract).then_inc(st["hid"], 1)

            def conv_taps(i, s, src, to):
                dve.wait_ge(st["tapped"], at(s + 1, i, 2))
                dve.wait_ge(st["scaled"], at(s + 1, i, 2))
                for k in (1, 0):
                    nc.vector.scalar_tensor_tensor(out=to[:], in0=src[:, k:S + k],
                                                   scalar=column("w_ffconv", at(k * 2 * FC + s * FC, i, 1)),
                                                   in1=to[:], op0=ALU.mult, op1=ALU.add).then_inc(st["steps"], 1)
                    dve.wait_ge(st["steps"], at(2 * s + 2 - k, i, 4))

            def conv_turn(i, first):
                u = FIRST["up"]
                dve.wait_ge(used, at(u + 1, i, 2))
                scaled(ffn["ua"][:, 2:S + 2], 0, st["scaled"])
                split(u + 2, i)
                if not first:
                    conv_product(i, -1)
                dve.wait_ge(used, at(u + 2, i, 2))
                scaled(ffn["ug"][:, 2:S + 2], 1, st["scaled"])
                split(u + 3, i)
                conv_taps(i, 0, ffn["ua"], ffn["ta"])
                if not first:
                    conv_lo(i, -1)
                conv_taps(i, 1, ffn["ug"], ffn["tg"])

            conv_turn(None, True)
            with dve.Fori(1, FC) as i:
                conv_turn(i, False)
            conv_product(None, FC - 1)
            conv_lo(None, FC - 1)
            into_residual("down", FC, "first", "a_gain", 2)

            dve.wait_ge(loads["spatial"], 2 * 16)
            for g in range(N_SPATIAL):
                wg = sg["w"][:, g * P:(g + 1) * P]
                ins = nc.vector.tensor_tensor(wg, wg, con[:, CAT["keep"]:CAT["keep"] + P], ALU.mult)
            ins.then_inc(a_in["w"], 1)
            u0 = FIRST["a_v"]
            split(u0 + 2)
            split(u0 + 3)
            dve.wait_ge(rms_ready, NORM["first"] + 1)
            nc.vector.reciprocal(first["r"][:], square_sum[:]).then_inc(r_ready, 1)
            dve.wait_ge(rows_rms_ready, ROWS["first"] + 1)
            nc.vector.reciprocal(first["r_rows"][:], rms_rows[:]).then_inc(rows_ready, 1)
            dve.wait_ge(r_ready, NORM["first"] + 1)
            dve.wait_ge(rows_ready, ROWS["first"] + 1)
            dve.wait_ge(sums_ready, NORM["a"] + 1)
            dve.wait_ge(rows_sums_ready, ROWS["a"] + 1)
            for k, (src, to, to_rows) in enumerate(((ps[:, 0, :], first["sums"], first["sums_rows"]),
                                                    (first["sums"][:], first["sums"], first["sums_rows"]))):
                if k:
                    dve.wait_ge(a_in["first"], 2 * k)
                nc.vector.tensor_tensor(to[:], src, first["r"][:], ALU.mult).then_inc(a_in["first"], 1)
                nc.vector.tensor_tensor(to_rows[:], to_rows[:] if k else ps[:, 1, 0:TB], first["r_rows"][:],
                                        ALU.mult).then_inc(a_in["first"], 1)
            split(u0 + 4)
            dve.wait_ge(rms_ready, NORM["a"] + 1)
            nc.vector.reciprocal(first["sums"][:], first["sums"][:]).then_inc(a_in["first"], 1)
            dve.wait_ge(rows_rms_ready, ROWS["a"] + 1)
            nc.vector.reciprocal(first["sums_rows"][:], first["sums_rows"][:]).then_inc(a_in["first"], 1)
            dve.wait_ge(a_in["first"], 6)
            nc.vector.tensor_tensor(r_cols[:], first["sums"][:], first["r"][:], ALU.mult).then_inc(r_ready, 1)
            nc.vector.tensor_tensor(r_rows[:], first["sums_rows"][:], first["r_rows"][:], ALU.mult).then_inc(rows_ready, 1)
            dve.wait_ge(r_ready, NORM["a"] + 1)
            for u in range(u0 + 5, u0 + KC + 2):
                split(u)
            dve.wait_ge(a_in["v"], 2 * TB)
            nc.vector.tensor_tensor(sg["mean"][:], sg["v_sum"][:, :, 0], sg["v_sum"][:, :, 1], ALU.add).then_inc(a_in["steps"], 1)
            dve.wait_ge(a_in["steps"], 1)
            nc.vector.tensor_scalar(sg["mean"][:], sg["mean"][:], -1.0 / D, None, ALU.mult).then_inc(a_in["steps"], 1)
            u0 = FIRST["a_u"]

            def gate_panel(s, i):
                dve.wait_ge(used, at(u0 + 1 + s, i, 2))
                scaled(chunk(sg["u"], at(s, i, 2)), 2 + s, a_in["scaled"])
                split(u0 + 2 + s, i)

            gate_panel(0, None)
            dve.wait_ge(a_in["std"], 1)
            nc.vector.reciprocal(sg["r"][:], sg["std"][:]).then_inc(a_in["steps"], 1)
            gate_panel(1, None)
            dve.wait_ge(a_in["steps"], 3)
            for b in range(TB + 1):
                if b < TB:
                    nc.vector.tensor_scalar(sg["v"][:, b, :], sg["v"][:, b, :], sg["mean"][:, b:b + 1], sg["r"][:, b:b + 1], ALU.add,
                                            ALU.mult).then_inc(a_in["normed"], 1)
                if b:
                    dve.wait_ge(a_in["v_hi"], b)
                    nc.vector.tensor_tensor(sg["v_lo"][:, b - 1, :], sg["v"][:, b - 1, :], sg["v_hi"][:, b - 1, :].bitcast(F32),
                                            ALU.subtract).then_inc(a_in["v_lo"], 1)
            dve.wait_ge(a_in["w_hi"], 1)
            nc.vector.tensor_tensor(sg["w_lo"][:], sg["w"][:], sg["w_hi"][:].bitcast(F32), ALU.subtract).then_inc(a_in["w_lo"], 1)
            with dve.Fori(1, KC // 2) as i:
                for s in range(2):
                    gate_panel(s, i)
            dve.wait_ge(loads["spatial"], 2 * 16)
            dve.wait_ge(a_in["u"], KC)
            for g in range(N_SPATIAL + 1):
                if g < N_SPATIAL:
                    dve.wait_ge(a_in["z_done"], g + 1)
                    if g:
                        dve.wait_ge(a_in["product"], g)
                    nc.vector.scalar_tensor_tensor(
                        out=sg["z"][:].rearrange("p (b t) -> p b t", b=TB),
                        in0=ps[:, 4 + g % 2, :].rearrange("p (b t) -> p b t", b=TB), scalar=column("a_v_norm", g),
                        in1=sg["b"][:, g, :].unsqueeze(1).to_broadcast([P, TB, P]), op0=ALU.mult, op1=ALU.add).then_inc(a_in["z"], 1)
                    dve.wait_ge(a_in["z"], g + 1)
                    nc.vector.tensor_tensor(sg["u"][:, g, :], sg["u"][:, g, :], sg["z"][:], ALU.mult).then_inc(a_in["product"], 1)
                if g:
                    dve.wait_ge(a_in["hi"], g)
                    nc.vector.tensor_tensor(sg["lo"][:, g - 1, :], sg["u"][:, g - 1, :], sg["hi"][:, g - 1, :].bitcast(F32),
                                            ALU.subtract).then_inc(a_in["ready"], 1)
            for c in range(KC):
                nc.vector.scalar_tensor_tensor(out=x[:, c, :], in0=x[:, c, :], scalar=column("g_first", c), in1=first["r"][:],
                                               op0=ALU.mult, op1=ALU.mult).then_inc(x_ready, 1)
            dve.wait_ge(x_ready, KC * NORM["a"])
            into_residual("a_out", KC, "ffn0", "ffn_norm0", 0)

            def swiglu(name, norm, base):
                st = ffn_stages[name]
                norm_r(norm)
                u0 = FIRST[name]
                with dve.Fori(0, FC) as i:
                    for s, to in enumerate((ffn["tg"], ffn["ta"])):
                        dve.wait_ge(used, at(u0 + 1 + s, i, 2))
                        scaled(to[:], base + s, st["scaled"])
                        split(u0 + 2 + s, i)
                    dve.wait_ge(st["gated"], at(1, i, 1))
                    dve.wait_ge(st["scaled"], at(2, i, 2))
                    nc.vector.tensor_tensor(ffn["h"][:], ffn["ta"][:], ffn["gate"][:], ALU.mult).then_inc(st["product"], 1)
                    dve.wait_ge(st["hid_hi"], at(1, i, 1))
                    nc.vector.tensor_tensor(chunk(ffn["lo"], at(0, i, 1)), ffn["h"][:], chunk(ffn["hi"], at(0, i, 1)).bitcast(F32),
                                            ALU.subtract).then_inc(st["hid"], 1)

            swiglu("gu0", "ffn0", 0)
            into_residual("down0", FC, "kv", "kv_norm", 2)

            nc.vector.memset(da["zero"][:], 0.0).then_inc(kv["zero"], 1)
            u0 = FIRST["kv_v"]
            split(u0 + 2)
            norm_r("kv", True)
            for u in range(u0 + 1, u0 + KC):
                split(u + 2)
                for c in range(2 * (u - u0 - 4), 2 * (u - u0 - 4) + 2):
                    if c >= 0:
                        dve.wait_ge(kv["xb_hi"], c + 1)
                        nc.vector.scalar_tensor_tensor(out=da["xb_lo"][:, c, :], in0=x[:, c, :], scalar=column("b_norm", c),
                                                       in1=da["xb_hi"][:, c, :].bitcast(F32), op0=ALU.mult,
                                                       op1=ALU.subtract).then_inc(kv["xb"], 1)
            qk0 = FIRST["qk"]

            def panel_out(p, i, bank):
                dve.wait_ge(used, at(qk0 + p + 1, i, 4))
                if p >= 2:
                    dve.wait_ge(a3["staged"], at(p - 1, i, 4))
                if p % 2:
                    nc.vector.scalar_tensor_tensor(out=da["q"], in0=ps[:, bank, :], scalar=-HD ** -0.5, in1=r_cols[:],
                                                   op0=ALU.mult, op1=ALU.mult).then_inc(kv["qk"], 1)
                else:
                    scaled(da["k"], bank, kv["qk"])

            for p in range(4):
                panel_out(p, None, 2 + p)
                split(qk0 + p + 2)
            dve.wait_ge(lams["done"], 1)

            def diff_item(n, c, base):
                def least(n):
                    s, b = n // TB, n % TB
                    w = P * (b + 1)
                    if c is not None or n + base >= DIFF_SLOTS:
                        dve.wait_ge(a3["turned"], at(base + n + 1 - DIFF_SLOTS, c, 8))
                    if b == 0:
                        dve.wait_ge(a3["bias"], at(base // TB + s + 1, c, 2))
                    for h in range(2):
                        k = 2 * (n % DIFF_SLOTS) + h
                        half = dve.to_reg(at(2 * (base + n) + h + 1, c, 16))
                        dve.wait_ge(loads["alibi"], 16)
                        dve.wait_ge(a3["scores"], half)
                        nc.vector.tensor_tensor_reduce(at3["e"][:, k, 0:w], ps[:, 2 * (n % 2) + h, 0:w],
                                                       da["bias"][:, s % 2, S - P - b * P:S - P - b * P + w], 1.0, FAR,
                                                       ALU.add, ALU.min, at3["least"][:, k:k + 1]).then_inc(a3["least"], 1)

                def inverse(n):
                    k = 2 * (n % DIFF_SLOTS)
                    dve.wait_ge(a3["exps"], at(2 * (base + n) + 2, c, 16))
                    nc.vector.reciprocal(at3["inv"][:, k:k + 2], at3["sums"][:, k:k + 2]).then_inc(a3["inv"], 1)
                    dve.wait_ge(a3["inv"], at(base + n + 1, c, 8))
                    nc.vector.tensor_scalar(at3["second"][:, k + 1:k + 2], at3["inv"][:, k + 1:k + 2], lam[:, 0:1], None,
                                            ALU.mult).then_inc(a3["second"], 1)

                def probs(n):
                    w = P * (n % TB + 1)
                    k = 2 * (n % DIFF_SLOTS)
                    dve.wait_ge(a3["weighed"], at(base + n + 1, c, 8))
                    nc.vector.scalar_tensor_tensor(out=at3["e"][:, k, 0:w], in0=at3["e"][:, k, 0:w],
                                                   scalar=at3["inv"][:, k:k + 1], in1=at3["e"][:, k + 1, 0:w], op0=ALU.mult,
                                                   op1=ALU.subtract).then_inc(a3["probs"], 1)

                def lo(n):
                    w = P * (n % TB + 1)
                    dve.wait_ge(a3["pt_hi"], at(base + n + 1, c, 8))
                    nc.vector.tensor_tensor(at3["pt_lo"][:, n % 2, 0:w], ps[:, 4 + n % 2, 0:w],
                                            at3["pt_hi"][:, n % 2, 0:w].bitcast(F32), ALU.subtract).then_inc(a3["pt"], 1)

                if qk_due(n, c, base):
                    panel_out(3 + (base + n) // 2, c, 7)
                if live(n, c, base):
                    least(n)
                if live(n - 2, c, base):
                    inverse(n - 2)
                if live(n - 3, c, base):
                    probs(n - 3)
                if live(n - 5, c, base):
                    lo(n - 5)
                if qk_due(n, c, base):
                    u = qk0 + 3 + (base + n) // 2 + 2
                    dve.wait_ge(w_hi_ready, at(u + 1, c, 4))
                    nc.vector.tensor_tensor(w_lo[:, u % 2, :], w_raw[:, u % 2, :], w_hi[:, u % 2, :].bitcast(F32),
                                            ALU.subtract).then_inc(w_ready, 1)

            diff_turns(dve, diff_item, 5)
            dve.wait_ge(a3["rms"], 1)
            nc.vector.reciprocal(da["rms"], da["rms"]).then_inc(a3["rms"], 1)
            for h in range(N_DIFF + 1):
                if h < N_DIFF:
                    dve.wait_ge(a3["spread"], h + 1)
                    nc.vector.scalar_tensor_tensor(out=da["o"][:, h, :], in0=da["o"][:, h, :], scalar=subln[:, 0:1],
                                                   in1=ps[:, h % 4, :], op0=ALU.mult, op1=ALU.mult).then_inc(a3["normed"], 1)
                if h:
                    dve.wait_ge(a3["out_hi"], h)
                    nc.vector.tensor_tensor(xg_lo[:, h - 1, :], da["o"][:, h - 1, :], xg_hi[:, h - 1, :].bitcast(F32),
                                            ALU.subtract).then_inc(a3["out_lo"], 1)
            into_residual("bo", KC, "ffn1", "ffn_norm1", 4)
            swiglu("gu1", "ffn1", 4)
            into_residual("down1", FC, "final", None, 6)
            norm_r("final")
            for c in range(KC):
                nc.vector.scalar_tensor_tensor(out=result[:, c, :], in0=x[:, c, :], scalar=column("g_final", c), in1=r_cols[:],
                                               op0=ALU.mult, op1=ALU.mult).then_inc(finals["scaled"], 1)

        @block.gpsimd
        def _(pool):
            def sum_squares(norm, sums=square_sum):
                n = NORM[norm]
                for c in range(KC):
                    k = KC * n + c
                    pool.wait_ge(sq_ready, k + 1)
                    if c == 0:
                        nc.gpsimd.tensor_copy(sums[:], squares[:, 0, :]).then_inc(summed, 1)
                    else:
                        pool.wait_ge(summed, k)
                        nc.gpsimd.tensor_tensor(sums[:], sums[:], squares[:, c % 2, :], ALU.add).then_inc(summed, 1)

            pool.dma_start(rope["pos"][:], positions).then_inc(loads["early"], 16)
            pool.dma_start(lam_in[:], lambdas).then_inc(loads["early"], 16)
            pool.dma_start(rope["pool_w"][:], pool_blocks).then_inc(loads["tables"], 16)
            pool.dma_start(rope["heads"][:], head_rows).then_inc(loads["tables"], 16)
            pool.dma_start(mix["dil"][:], dil_table).then_inc(loads["tables"], 16)
            sum_squares("mix")

            counted = [0]

            def step(ins):
                counted[0] += 1
                ins.then_inc(small["steps"], 1)
                pool.wait_ge(small["steps"], counted[0])

            step(nc.gpsimd.memset(rope["pad"][:, 0:16], 0.0))
            u = rope["pad"]
            for c in range(GC):
                pool.wait_ge(w_in["evacuated"], 4 + 3 * c)
                h_, b_, c_ = (mix["proj"][:, 1 + 3 * c + k, :] for k in range(3))
                step(nc.gpsimd.tensor_tensor(u[:, 16:], c_, h_, ALU.mult))
                step(nc.gpsimd.tensor_scalar(rope["win"][:, 0:S], u[:, 16:], column("w_sconv", 2 * GC + c), None, ALU.mult))
                for k in (1, 0):
                    step(nc.gpsimd.tensor_scalar(rope["win2"][:, 0:S], u[:, 14 + k:14 + k + S], column("w_sconv", k * GC + c),
                                                 None, ALU.mult))
                    step(nc.gpsimd.tensor_tensor(rope["win"][:, 0:S], rope["win"][:, 0:S], rope["win2"][:, 0:S], ALU.add))
                counted[0] += 1
                nc.gpsimd.tensor_tensor(mix["proj"][:, 1 + c, :], b_, rope["win"][:, 0:S], ALU.mult).then_inc(small["steps"], 1)
                pool.wait_ge(small["steps"], counted[0])
                pool.sem_inc(small["conv"], 1)
            for c in range(GC):
                pool.wait_ge(w_in["evacuated"], 8 + c)
                s1, s2 = rope["win"], rope["win2"]
                step(nc.gpsimd.tensor_copy(u[:, 16:], mix["proj"][:, 7 + c, :]))
                step(nc.gpsimd.tensor_tensor(s1[:, 1:], u[:, 1:], u[:, 0:S + 15], ALU.add))
                step(nc.gpsimd.tensor_tensor(s2[:, 3:], s1[:, 3:], s1[:, 1:S + 14], ALU.add))
                if c:
                    step(nc.gpsimd.tensor_tensor(s1[:, 7:], s2[:, 7:], s2[:, 3:S + 12], ALU.add))
                    step(nc.gpsimd.tensor_tensor(s2[:, 15:], s1[:, 15:], s1[:, 7:S + 8], ALU.add))
                for h, t in enumerate((s1, s2)):
                    rows = slice(HD * h, HD * h + HD)
                    step(nc.gpsimd.tensor_scalar(rope["z"][rows, c, :], t[rows, 16:], column("inv_window", c, rows), None, ALU.mult))
                    step(nc.gpsimd.tensor_tensor(rope["z"][rows, c, 0:16], t[rows, 16:32],
                                                 con[rows, CAT["inv_count"] + 16 * c:CAT["inv_count"] + 16 * c + 16], ALU.mult))
                counted[0] += 1
                nc.gpsimd.tensor_tensor(rope["z"][:, c, :], rope["z"][:, c, :], u[:, 16:], ALU.subtract).then_inc(small["steps"], 1)
                pool.wait_ge(small["steps"], counted[0])
                pool.sem_inc(small["pooled"], 1)

            pool.wait_ge(gate["rows"], 1 + N_FORGET)
            with pool.Fori(0, GC) as c:
                for m in range(8):
                    b, h = m // 2, m % 2
                    w = P * (b + 1)
                    pool.wait_ge(a1["least"], at(8 + m - 1 if m >= 2 else 1, c, 16))
                    to = mix["proj"][:, 5 + m % 2, 0:w]
                    nc.gpsimd.tensor_tensor(to, mix["proj"][:, bass.ds(1 + h + c * 2, 1), 0:w].rearrange("p a n -> p (a n)"),
                                            mix["nci"][:, b, bass.ds(h + c * 2, 1)].to_broadcast([P, w]), ALU.add).then_inc(a1["bias_steps"], 1)
                    pool.wait_ge(a1["bias_steps"], at(m + 1, c, 8))
                    to = mix["proj"][:, 5 + m % 2, w - P:w]
                    nc.gpsimd.tensor_tensor(to, to, causal, ALU.add).then_inc(a1["bias"], 1)

            for c in range(KC):
                pool.wait_ge(mem["sq"], c + 1)
                if c == 0:
                    nc.gpsimd.tensor_copy(memory["acc"][:], memory["sq"][:, 0, :]).then_inc(mem["summed"], 1)
                else:
                    pool.wait_ge(mem["summed"], c)
                    nc.gpsimd.tensor_tensor(memory["acc"][:], memory["acc"][:], memory["sq"][:, c % 2, :], ALU.add).then_inc(mem["summed"], 1)
            sum_squares("xa")
            for norm in ("ffn", "first", "ffn0", "kv"):
                sum_squares(norm)
                if norm == "first":
                    sum_squares("a", first["sums"])
            pool.wait_ge(loads["alibi"], 16)
            pool.wait_ge(kv["zero"], 1)
            pool.wait_ge(kv["v"], 8)

            def parts_of(set_, n_split, c, *parts):
                for k, (name, src) in enumerate(parts):
                    n = src.shape[1]
                    hi, lo = (at3[f"{name}{half}{set_}"][:].rearrange("p (a n) -> p a n", a=n) for half in ("hi", "lo"))
                    nc.gpsimd.tensor_tensor(hi, src, da["zero"][:].unsqueeze(2).to_broadcast(src.shape),
                                            ALU.add).then_inc(a3["staged_hi"], 1)
                    split_ = pool.to_reg(at(n_split + k + 1, c, 6))
                    pool.wait_ge(kv["zero"], 1)
                    pool.wait_ge(a3["staged_hi"], split_)
                    ins = nc.gpsimd.tensor_tensor(lo, src, hi.bitcast(F32), ALU.subtract)
                return ins

            def stage_qk(s, c):
                first_pair = c is None
                if not first_pair:
                    pool.wait_ge(a3["scores"], at(8 * (s - 1), c, 16))
                for k, name in enumerate(("k", "q")):
                    pool.wait_ge(kv["qk"], at(2 * s + k + 1, c, 4))
                    parts_of(s, (2 * s if first_pair else 3 * s - 1) + k, c,
                             (name, da[name].unsqueeze(1))).then_inc(a3["staged"], 1)
                if not first_pair:
                    pool.wait_ge(a3["least"], at(8 * (s - 1), c, 16))
                nc.gpsimd.tensor_tensor(da["bias"][:, s, :], da["alibi"][:], column("slopes", at(s, c, 2)).to_broadcast([P, BAND]),
                                        ALU.mult).then_inc(a3["bias"], 1)

            def stage_v(s, c, base, n_split):
                if c is not None or base + s >= 2:
                    pool.wait_ge(a3["pv"], at(TB * (base + s - 1) + (s < 0), c, 2 * TB))
                cols = bass.ds(at((base + s) * P, c, 2 * P), P)
                parts_of(s % 2, n_split, c, ("v", da["v"][:, :, cols])).then_inc(a3["v_staged"], 1)

            stage_qk(0, None)
            stage_qk(1, None)
            stage_v(0, None, 0, 4)
            with pool.Fori(1, N_DIFF // 2) as c:
                for s in range(2):
                    stage_qk(s, c)
                    stage_v(s - 1, c, 0, 3 * s + 1)
            stage_v(1, None, N_DIFF - 2, 3 * N_DIFF - 1)
            sum_squares("ffn1")
            sum_squares("final")

    return nc


def _tiles(w):
    k, n = w.shape
    return w.reshape(k // P, P, n // P, P).transpose(2, 1, 0, 3).reshape(n // P, P, -1)


def _rows(w, per_unit):
    k, n = w.shape
    return w.reshape(k // P // per_unit, per_unit, P, n).transpose(0, 2, 1, 3).reshape(-1, P, per_unit * n)


def _halves(w):
    return [_rows(w[:, h * S:(h + 1) * S], 2) for h in range(w.shape[1] // S)]


def _chunks(a):
    t, n = a.shape
    return a.T.reshape(n // P, P, t).transpose(1, 0, 2)


def _pairs(a, b):
    return np.stack([_tiles(a), _tiles(b)], 1).reshape(-1, P, a.shape[0])


def _columns(v):
    return v.reshape(-1, P).T


def _constants():
    con = np.zeros((P, N_CONSTS), np.float32)
    eye = np.eye(P, dtype=np.float32)
    con[:, CAT["ident"]:CAT["ident"] + P] = eye
    con[:, CAT["ones"]:CAT["ones"] + P] = 1.0
    perm = np.zeros((P, P), np.float32)
    half = ROPE_DIM // 2
    for h in range(P // HD):
        for f in range(half):
            perm[h * HD + f + half, h * HD + f] = -1.0
            perm[h * HD + f, h * HD + f + half] = 1.0
    con[:, CAT["rope_perm"]:CAT["rope_perm"] + P] = perm
    p, j = np.arange(P)[:, None], np.arange(P)[None, :]
    con[:, CAT["causal"]:CAT["causal"] + P] = np.where(j <= p, 0.0, MASKED)
    con[:, CAT["keep"]:CAT["keep"] + P] = p <= j
    for c in range(GC):
        for h in range(2):
            w = POOL_WINDOWS[2 * c + h]
            con[HD * h:HD * h + HD, CAT["inv_count"] + 16 * c:CAT["inv_count"] + 16 * c + 16] = \
                np.float32(1.0) / np.minimum(np.arange(16) + 1, w).astype(np.float32)
    con[:, CAT["pick"] + N_DIFF - 1] = 1.0
    dist = p + (S - P) - np.arange(BAND)[None, :]
    count = sum(((dist % d == 0) & (dist <= w)).astype(np.float64) for w, d in DILATED)
    count = np.where(dist >= 0, count, 0.0)
    dil = np.where(count > 0, -np.log(np.maximum(count, 1.0)), MASKED).astype(np.float32)
    alibi = np.where(dist >= 0, dist, MASKED).astype(np.float32)
    heads = np.zeros((P, N_FORGET, P), np.float32)
    for h in range(N_FORGET):
        heads[h, h, :] = 1.0
    picks = np.zeros((N_DIFF, N_DIFF, P), np.float32)
    for h in range(N_DIFF):
        picks[h, h, :] = 1.0
    return con, dil, alibi, heads.reshape(P, -1), picks.reshape(N_DIFF, -1)


def _lay_out(i):
    a = {n: np.asarray(v) for n, v in i.items()}
    w_in = a["w_in"][0]
    g3 = 3 * G
    gate0 = 9 * G
    gate = np.zeros((D, P), np.float32)
    gate[:, :N_FORGET] = w_in[:, gate0:gate0 + N_FORGET]
    conv = [w_in[:, k * G + c * P:k * G + (c + 1) * P] for c in range(GC) for k in range(3)]
    qk = [w_in[:, g3:g3 + 2 * G], w_in[:, 2 * g3:2 * g3 + 2 * G]]
    panels = np.concatenate([gate] + conv + [w_in[:, gate0 + N_FORGET:]] + qk, 1)
    values = np.concatenate([w_in[:, g3 + 2 * G:2 * g3], w_in[:, 2 * g3 + 2 * G:3 * g3]], 1)
    order = [0, 1, 6, 7, 2, 4, 3, 5]
    w_out = a["w_out"][0].reshape(KC, P, D)[order].reshape(D, D)
    up, xkv, kv, a_in = a["w_up"][0], a["w_xkv"][0], a["kv_w_2"], a["a_w_in_2"][0]
    gu, dn = a["ffn_w_gu_2"], a["ffn_w_down_2"]
    stream = [_tiles(panels), *_halves(values), _rows(w_out, 1), _tiles(xkv[:, :D]), _rows(xkv[:, D:], 1),
              _tiles(a["w_xq"][0]), _rows(a["w_xo"][0], 1), _pairs(up[:, :FF], up[:, FF:]), _rows(a["w_down"][0], 1),
              *_halves(a_in[:, D:]), _tiles(a_in[:, :D]), _rows(a["a_w_out_2"][0], 1),
              _pairs(gu[0][:, :FF], gu[0][:, FF:]), _rows(dn[0], 1),
              *_halves(kv[:, D:]), _pairs(kv[:, :D], a["b_w_q_2"][0]), _rows(a["b_w_o_2"][0], 1),
              _pairs(gu[1][:, :FF], gu[1][:, FF:]), _rows(dn[1], 1)]
    weights = np.concatenate(stream, 0)
    par = np.zeros((P, N_PARAMS), np.float32)

    def put(name, cols):
        par[:cols.shape[0], AT[name]:AT[name] + cols.shape[1]] = cols

    for name, v in (("g_mix", a["g_mix"]), ("g_xa", a["g_xa"]), ("g_mem", a["g_mem"]), ("g_ffn", a["g_ffn"]),
                    ("a_norm", a["a_norm_2"]), ("ffn_norm0", a["ffn_norm_2"][0]), ("kv_norm", a["kv_norm_2"]),
                    ("b_norm", a["b_norm_2"]), ("ffn_norm1", a["ffn_norm_2"][1]), ("g_first", a["g_final"]), ("g_final", a["final_norm_2"]),
                    ("a_v_norm", a["a_v_norm_2"]), ("w_sconv", a["w_sconv"][0]), ("pool_scale", a["pool_scale"]),
                    ("w_ffconv", a["w_ffconv"][0]), ("b_subln", a["b_subln_2"])):
        put(name, _columns(v))
    put("b_forget", a["b_forget"].reshape(N_FORGET, 1))
    par[:, AT["eps"]] = EPS
    half = ROPE_DIM // 2
    freq = np.float32(ROPE_THETA) ** (-np.arange(0, ROPE_DIM, 2, dtype=np.float32) / np.float32(ROPE_DIM))
    for h in range(P // HD):
        for k in range(2):
            par[h * HD + k * half:h * HD + (k + 1) * half, AT["inv_freq"]] = freq
        for c in range(GC):
            par[HD * h:HD * h + HD, AT["inv_window"] + c] = 1.0 / POOL_WINDOWS[2 * c + h]
    par[:, AT["slopes"]:AT["slopes"] + N_DIFF] = 2.0 ** (-8.0 * (np.arange(N_DIFF) + 1) / N_DIFF)
    con, dil, alibi, heads, picks = _constants()
    blocks = np.zeros((P, GC, P), np.float32)
    for c in range(GC):
        for h in range(2):
            blocks[HD * h:HD * h + HD, c, HD * h:HD * h + HD] = a["w_pool"][0][2 * c + h]
    return {
        "weights": weights, "x_cols": _chunks(a["x"][0]), "mem_cols": _chunks(a["mem"][0]),
        "positions": np.broadcast_to(a["positions"], (P, S)), "params": par, "consts": con,
        "dil_table": dil, "head_rows": heads, "alibi_table": alibi, "head_picks": picks, "pool_blocks": blocks,
        "spatial": a["a_w_sp_2"][0].transpose(2, 0, 1).reshape(P, -1),
        "spatial_bias": np.broadcast_to(a["a_b_sp_2"][0].reshape(1, -1), (P, N_SPATIAL * P)),
        "lambdas": np.broadcast_to(a["b_lambda_2"][0].reshape(1, -1), (P, 4 * HD)),
    }


def kernel(**inputs):
    import concourse.bacc as bacc
    from concourse.bass_utils import run_bass_kernel_spmd as run

    nc = bacc.Bacc("TRN2", target_bir_lowering=False, num_devices=1)
    arrays, args = {}, {}
    for name, a in _lay_out(inputs).items():
        a = np.ascontiguousarray(a)
        arrays[f"in_{name}"] = a
        args[name] = nc.dram_tensor(f"in_{name}", a.shape, mybir.dt.from_np(a.dtype), kind="ExternalInput").ap()
    out = nc.dram_tensor("out_cols", (P, KC, S), F32, kind="ExternalOutput").ap()
    bass_two_blocks(nc, out=out, **args)
    got = run(nc, [arrays], core_ids=[0]).results[0]["out_cols"]
    return np.ascontiguousarray(got.transpose(2, 1, 0)).reshape(1, S, D)
```

```python
import math
from contextlib import ExitStack

import numpy as np

import concourse.bass as bass
from concourse import mybir

F32 = mybir.dt.float32
F32R = mybir.dt.float32r
I32 = mybir.dt.int32
ALU = mybir.AluOpType
ACT = mybir.ActivationFunctionType
AX = mybir.AxisListType

P = 128
D = 1024
S = 512
KC = D // P
M = 256
MB = M // P
TB = S // P
HD = 64
FF = 2816
FC = FF // P
G = D // 4
GC = G // P
N_FORGET = G // HD
XA_HEADS = 4
XC = D // XA_HEADS // P
N_DIFF = 8
N_SPATIAL = 8
EPS = 1e-6
MASKED = 1e30
FAR = 3.0e38
ROPE_DIM = HD // 4
ROPE_THETA = 500000.0
DILATED = ((128, 1), (512, 4), (2048, 16))
POOL_WINDOWS = (2, 4, 8, 16)
LAMBDA_INIT = 0.8 - 0.6 * math.exp(-0.3)
MIX_ITEMS = 2 * GC * 2 * TB
MEM_LAG = 4
DIFF_SLOTS = 4
BAND = S + S - P

UNITS = (("w_in", 2 * KC + 5), ("mem_k", KC), ("mem_v", KC), ("w_out", KC), ("xq", KC), ("xo", KC),
         ("up", 2 * FC), ("down", FC), ("a_v", KC), ("a_u", KC), ("a_out", KC), ("gu0", 2 * FC), ("down0", FC),
         ("kv_v", KC), ("qk", 2 * KC), ("bo", KC), ("gu1", 2 * FC), ("down1", FC))
FIRST = {}
N_UNITS = 0
for _name, _n in UNITS:
    FIRST[_name] = N_UNITS
    N_UNITS += _n

PARAMS = (("g_mix", KC), ("g_xa", KC), ("g_mem", KC), ("g_ffn", KC), ("a_norm", KC), ("ffn_norm0", KC),
          ("kv_norm", KC), ("b_norm", KC), ("ffn_norm1", KC), ("g_first", KC), ("a_gain", KC), ("g_final", KC), ("a_v_norm", KC),
          ("b_forget", 1), ("w_sconv", 3 * GC), ("pool_scale", GC), ("w_ffconv", 3 * 2 * FC), ("b_subln", 1),
          ("eps", 1), ("inv_freq", 1), ("inv_window", GC), ("slopes", N_DIFF))
AT = {}
N_PARAMS = 0
for _name, _n in PARAMS:
    AT[_name] = N_PARAMS
    N_PARAMS += _n

CONSTS = (("ident", P), ("ones", P), ("rope_perm", P), ("causal", P), ("keep", P), ("inv_count", GC * 16),
          ("pick", 2 * N_DIFF - 1))
CAT = {}
N_CONSTS = 0
for _name, _n in CONSTS:
    CAT[_name] = N_CONSTS
    N_CONSTS += _n

TWO_PI = 2.0 * math.pi
TURN_1 = 201.0 / 32.0
TURN_2 = round((TWO_PI - TURN_1) * 2.0 ** 17) / 2.0 ** 17
TURN_3 = round((TWO_PI - TURN_1 - TURN_2) * 2.0 ** 27) / 2.0 ** 27
TURN_4 = TWO_PI - TURN_1 - TURN_2 - TURN_3
ROUNDER = 1.5 * 2.0 ** 23
PI_BELOW = 3.1415925


def bass_two_blocks(nc, weights, x_cols, mem_cols, positions, params, consts, dil_table, head_rows, alibi_table, head_picks,
                    pool_blocks, spatial, spatial_bias, lambdas, out):
    ctx = ExitStack()

    def sem(name):
        return ctx.enter_context(nc.semaphore(name))

    def stage(name, *signals):
        return {s: sem(f"{name}_{s}") for s in signals}

    def at(const, i=None, per=0):
        return const if i is None else const + i * per

    def diff_turns(engine, step, depth):
        for n in range(8):
            step(n, None, 0)
        with engine.Fori(1, N_DIFF // 2 - 1) as c:
            for n in range(8):
                step(n, c, 0)
        for n in range(8 + depth):
            step(n, None, 4 * N_DIFF - 8)

    def live(n, c, base):
        return n < 8 and (n >= 0 or c is not None or base > 0)

    def qk_due(n, c, base):
        return n % 2 == 0 and (0 < n < 8 or c is not None or base > 0 and n == 0) and (base == 0 or n == 0)

    with ctx:
        def sb(name, shape, dt=F32, where=ctx):
            return where.enter_context(nc.sbuf_tensor(name, shape, dt))

        x = sb("x", [P, KC, S])
        xg_hi = sb("xg_hi", [P, KC, S], F32R)
        xg_lo = sb("xg_lo", [P, KC, S], F32R)
        w_raw = sb("w_raw", [P, 2, D])
        w_hi = sb("w_hi", [P, 2, D], F32R)
        w_lo = sb("w_lo", [P, 2, D], F32R)
        par = sb("par", [P, N_PARAMS])
        con = sb("con", [P, N_CONSTS])
        r_cols = sb("r_cols", [P, S])
        r_rows = sb("r_rows", [P, TB])
        rms_rows = sb("rms_rows", [P, TB])
        squares = sb("squares", [P, 2, S])
        square_sum = sb("square_sum", [P, S])
        lam_in = sb("lam_in", [P, 4 * HD])
        lam_dot = sb("lam_dot", [P, 2])
        lam_exp = sb("lam_exp", [P, 2])
        lam = sb("lam", [P, 1])
        subln = sb("subln", [P, 1])

        s_ctx = ExitStack()
        mix = dict(hi=sb("mix_hi", [P, KC, S], F32R, s_ctx), lo=sb("mix_lo", [P, KC, S], F32R, s_ctx))
        kv_ctx = ExitStack()
        xa = dict(hi=mix["hi"], lo=mix["lo"], k=sb("xa_k", [P, KC, M], F32, kv_ctx), v=sb("xa_v", [P, MB, D], F32, kv_ctx))
        kv_ctx.close()
        rope = dict(
            pos=sb("pos", [P, S], I32, s_ctx), ang=sb("ang", [P, S], F32, s_ctx),
            turns=sb("turns", [P, S], F32, s_ctx), red=sb("red", [P, S], F32, s_ctx),
            cos=sb("cos", [P, S], F32, s_ctx), sin=sb("sin", [P, S], F32, s_ctx),
            prod=sb("rope_prod", [P, S], F32, s_ctx), g1=sb("gate_a", [P, S], F32, s_ctx))
        m_ctx = ExitStack()
        mix.update(
            proj=sb("proj", [P, 17, S], F32, m_ctx), v=sb("mix_v", [P, TB, 2 * G], F32, m_ctx),
            dil=sb("dil", [P, BAND], F32, m_ctx),
            c_rows=sb("c_rows", [P, S], F32, m_ctx), nci=sb("nci", [P, TB, N_FORGET], F32, m_ctx))
        memory = dict(
            sq=sb("mem_sq", [P, 2, M], F32, m_ctx), acc=sb("mem_acc", [P, M], F32, m_ctx),
            rms=sb("mem_rms", [P, M], F32, m_ctx), rms_rows=sb("mem_rms_rows", [P, MB], F32, m_ctx),
            r_cols=sb("mem_r_cols", [P, M], F32, m_ctx), r_rows=sb("mem_r_rows", [P, MB], F32, m_ctx))
        m_top = ExitStack()
        rope.update(
            heads=sb("heads", [P, N_FORGET * P], F32, m_top),
            g2=sb("gate_b", [P, S], F32, m_top),
            g3=sb("gate_c", [P, S], F32, m_top), g4=sb("gate_d", [P, S], F32, m_top),
            pad=sb("pad", [P, S + 16], F32, m_top), win=sb("win", [P, S + 16], F32, m_top),
            win2=sb("win2", [P, S + 16], F32, m_top), z=sb("pooled", [P, GC, S], F32, m_top),
            pool_w=sb("pool_w", [P, GC, P], F32, m_top))
        m_top.close()

        def attention_buffers(tag, where, q_cols, k_cols, v_cols, n_e, s_cols, turned):
            names = {}
            for set_ in range(2):
                for part, cols in (("q", q_cols), ("k", k_cols), ("v", v_cols)):
                    for half in ("hi", "lo"):
                        names[f"{part}{half}{set_}"] = sb(f"{tag}_{part}_{half}{set_}", [P, cols], F32R, where)
            names["pt_hi"] = sb(f"{tag}_pt_hi", [P, 2, turned], F32R, where)
            names["pt_lo"] = sb(f"{tag}_pt_lo", [P, 2, turned], F32R, where)
            names["e"] = sb(f"{tag}_e", [P, n_e, s_cols], F32, where)
            names["least"] = sb(f"{tag}_least", [P, n_e], F32, where)
            names["sums"] = sb(f"{tag}_sums", [P, n_e], F32, where)
            names["inv"] = sb(f"{tag}_inv", [P, n_e], F32, where)
            return names

        at1 = dict(e=sb("at1_e", [P, 3, S], F32, m_ctx), least=sb("at1_least", [P, 3], F32, m_ctx),
                   sums=sb("at1_sums", [P, 3], F32, m_ctx), inv=sb("at1_inv", [P, 3], F32, m_ctx),
                   pt_hi=xg_hi[:, 4:6, :], pt_lo=xg_lo[:, 4:6, :])
        for set_ in range(2):
            for part in ("qhi", "qlo", "khi", "klo"):
                at1[f"{part}{set_}"] = sb(f"at1_{part}{set_}", [P, S], F32R, m_ctx)
            at1[f"vhi{set_}"] = xg_hi[:, 6 + set_, :]
            at1[f"vlo{set_}"] = xg_lo[:, 6 + set_, :]
        m_ctx.close()

        def mem_split(to, c):
            return to[:, c // 2, c % 2 * M:(c % 2 + 1) * M]

        def mem_input(c):
            if c < 4:
                return squares[:, c // 2, c % 2 * M:(c % 2 + 1) * M]
            return (square_sum[:] if c < 6 else mix["proj"][:, 0, :])[:, c % 2 * M:(c % 2 + 1) * M]

        c_ctx = ExitStack()
        xa.update(q=sb("xa_q", [P, KC, S], F32, c_ctx))
        at2 = attention_buffers("at2", c_ctx, XC * S, XC * M, MB * XC * P, 3, M, M)
        c_ctx.close()
        s_ctx.close()
        f_ctx = ExitStack()
        ffn = dict(
            hi=sb("hid_hi", [P, FC, S], F32R, f_ctx), lo=sb("hid_lo", [P, FC, S], F32R, f_ctx),
            ua=sb("up_a", [P, S + 2], F32, f_ctx), ug=sb("up_g", [P, S + 2], F32, f_ctx),
            ta=sb("conv_a", [P, S], F32, f_ctx), tg=sb("conv_g", [P, S], F32, f_ctx),
            gate=sb("gate", [P, S], F32, f_ctx), h=sb("hid", [P, S], F32, f_ctx))
        f_ctx.close()
        g_ctx = ExitStack()
        sg = dict(
            hi=sb("sg_hi", [P, KC, S], F32R, g_ctx), lo=sb("sg_lo", [P, KC, S], F32R, g_ctx),
            u=sb("sg_u", [P, KC, S], F32, g_ctx), v=sb("sg_v", [P, TB, D], F32, g_ctx),
            v_hi=sb("sg_v_hi", [P, TB, D], F32R, g_ctx), v_lo=sb("sg_v_lo", [P, TB, D], F32R, g_ctx),
            v_sum=sb("sg_v_sum", [P, TB, 2], F32, g_ctx), mean=sb("sg_mean", [P, TB], F32, g_ctx),
            v_sq=sb("sg_v_sq", [P, TB], F32, g_ctx), std=sb("sg_std", [P, TB], F32, g_ctx),
            r=sb("sg_r", [P, TB], F32, g_ctx), z=sb("sg_z", [P, S], F32, g_ctx),
            w=sb("sp_w", [P, N_SPATIAL * P], F32, g_ctx), w_hi=sb("sp_w_hi", [P, N_SPATIAL * P], F32R, g_ctx),
            w_lo=sb("sp_w_lo", [P, N_SPATIAL * P], F32R, g_ctx), b=sb("sp_b", [P, N_SPATIAL, P], F32, g_ctx))
        first = dict(
            r=sb("first_r", [P, S], F32, g_ctx), r_rows=sb("first_r_rows", [P, TB], F32, g_ctx),
            sums=sb("first_sums", [P, S], F32, g_ctx), sums_rows=sb("first_sums_rows", [P, TB], F32, g_ctx))
        g_ctx.close()
        d_ctx = ExitStack()
        da = dict(
            v=sb("da_v", [P, TB, D], F32, d_ctx), o=sb("da_o", [P, KC, S], F32, d_ctx),
            xb_hi=sb("xb_hi", [P, KC, S], F32R, d_ctx), xb_lo=sb("xb_lo", [P, KC, S], F32R, d_ctx),
            alibi=sb("alibi", [P, BAND], F32, d_ctx), bias=sb("da_bias", [P, 2, BAND], F32, d_ctx),
            zero=sb("da_zero", [P, 1], F32, d_ctx), k=squares[:, 0, :], q=squares[:, 1, :])
        at3 = attention_buffers("at3", d_ctx, S, S, S, 2 * DIFF_SLOTS, S, S)
        at3["second"] = sb("at3_second", [P, 2 * DIFF_SLOTS], F32, d_ctx)
        da["picks"] = at3["e"][0:N_DIFF, 0:N_DIFF * P // S, :].rearrange("p a n -> p (a n)")
        da["rms"] = at3["e"][0:N_DIFF, N_DIFF * P // S, :]
        d_ctx.close()
        o_ctx = ExitStack()
        result = sb("result", [P, KC, S], F32, o_ctx)
        o_ctx.close()

        ps = ctx.enter_context(nc.psum_tensor("ps", [P, 8, S], F32))

        ident = con[:, CAT["ident"]:CAT["ident"] + P]
        ones = con[:, CAT["ones"]:CAT["ones"] + P]
        causal = con[:, CAT["causal"]:CAT["causal"] + P]

        def column(name, c=0, rows=slice(0, P)):
            return par[rows, bass.ds(AT[name] + c, 1)]

        loads = stage("loaded", "input", "con", "early", "tables", "mem", "spatial", "alibi")
        N_EARLY, N_TABLES = 2, 3
        w_loaded = [sem("weights_loaded_0"), sem("weights_loaded_1")]
        w_hi_ready = sem("weights_hi_ready")
        w_ready = sem("weights_ready")
        used = sem("units_used")
        x_ready = sem("x_ready")
        xg_hi_ready = sem("xg_hi_ready")
        xg_ready = sem("xg_ready")
        sq_ready = sem("squares_ready")
        summed = sem("squares_summed")
        sums_ready = sem("square_sums_ready")
        rms_ready = sem("rms_ready")
        r_ready = sem("r_ready")
        rows_sums_ready = sem("row_square_sums_ready")
        rows_rms_ready = sem("row_rms_ready")
        rows_ready = sem("r_rows_ready")
        w_in = stage("w_in", "evacuated", "v_ready")
        gate = stage("gate", "steps", "abs", "exp", "c", "turned", "rows")
        rot = stage("rope", "steps", "trig", "swapped", "prod", "prod_cos", "done")
        small = stage("mixer", "steps", "conv", "pooled", "product", "hi")
        mix_ready = sem("mix_ready")
        a1 = stage("at1", "staged_hi", "staged", "v_staged", "scores", "least", "exps", "inv", "probs", "turned", "pt_hi", "pt",
                   "pv", "out_hi", "bias", "bias_steps")
        a2 = stage("at2", "staged_hi", "staged", "scores", "least", "exps", "inv", "probs", "turned", "pt_hi", "pt",
                   "pv", "out_hi", "out")
        a3 = stage("at3", "staged_hi", "staged", "v_staged", "scores", "least", "exps", "inv", "second", "weighed", "probs",
                   "turned", "pt_hi", "pt", "pv", "out", "bias", "sq", "summed", "rms", "spread", "normed", "out_hi",
                   "out_lo")
        lams = stage("lambda", "dots", "exps", "done")
        mem = stage("mem", "hi", "lo", "sq", "summed", "sums", "rms", "r", "k_ready", "v_ready")
        xqs = stage("xq", "ready")
        ffn_stages = {"up": stage("up", "scaled", "tapped", "steps", "gated", "product", "hid_hi", "hid", "zero"),
                      "gu0": stage("gu0", "scaled", "gated", "product", "hid_hi", "hid"),
                      "gu1": stage("gu1", "scaled", "gated", "product", "hid_hi", "hid")}
        a_in = stage("a_in", "scaled", "u", "v", "steps", "v_sq", "std", "normed", "v_hi", "v_lo",
                     "w", "w_hi", "w_lo", "first", "z_done", "z", "product", "hi", "ready")
        kv = stage("kv", "v", "qk", "xb_hi", "xb", "zero")
        proj_sums = sem("residual_sums")
        RESIDUALS = ("w_out", "xo", "down", "a_out", "down0", "bo", "down1")
        finals = stage("final", "scaled", "stored")

        NORM = {"mix": 0, "xa": 1, "ffn": 2, "first": 3, "a": 4, "ffn0": 5, "kv": 6, "ffn1": 7, "final": 8}
        SPLIT = {"mix": 0, "xa": 1, "ffn": 2, "first": 3, "ffn0": 4, "kv": 5, "ffn1": 6}
        ROWS = {"mix": 0, "first": 1, "a": 2, "kv": 3}

        block = ctx.enter_context(nc.Block())

        @block.sync
        def _(sp):
            sp.dma_start(x[:], x_cols).then_inc(loads["input"], 16)
            sp.dma_start(par[:], params).then_inc(loads["input"], 16)
            for u in range(2):
                sp.dma_start(w_raw[:, u, :], weights[u]).then_inc(w_loaded[u], 16)
            with sp.Fori(1, N_UNITS // 2) as i:
                for s in range(2):
                    sp.wait_ge(w_ready, i * 2 + (s - 1))
                    sp.dma_start(w_raw[:, s, :], weights[bass.ds(i * 2 + s, 1), :, :].rearrange("u p n -> p (u n)")
                                 ).then_inc(w_loaded[s], 16)
            for u in range(N_UNITS // 2 * 2, N_UNITS):
                sp.wait_ge(w_ready, u - 1)
                sp.dma_start(w_raw[:, u % 2, :], weights[u]).then_inc(w_loaded[u % 2], 16)
            for c in range(KC):
                sp.wait_ge(finals["scaled"], c + 1)
                sp.dma_start(out[:, c, :], result[:, c, :]).then_inc(finals["stored"], 16)
            sp.wait_ge(finals["stored"], 16 * KC)

        @block.tensor
        def _(pe):
            def product(to, wh, wl, xh, xl, start, stop):
                nc.tensor.matmul(to, wh, xh, start=start, stop=False)
                nc.tensor.matmul(to, wh, xl, start=False, stop=False)
                return nc.tensor.matmul(to, wl, xh, start=False, stop=stop)

            def tile(s, k):
                return w_hi[:, s, k * P:(k + 1) * P], w_lo[:, s, k * P:(k + 1) * P]

            def panel(u, i, to, hi, lo, chunks_ready=None):
                pe.wait_ge(w_ready, at(u + 1, i, 2))
                for k in range(KC):
                    if chunks_ready is not None:
                        pe.wait_ge(xg_ready, chunks_ready + k + 1)
                    wh, wl = tile(u % 2, k)
                    mm = product(to, wh, wl, hi[:, k, :], lo[:, k, :], k == 0, k == KC - 1)
                mm.then_inc(used, 1)

            def square_sums(norm, bank, rows_bank=None, sums=square_sum):
                pe.wait_ge(summed, KC * (NORM[norm] + 1))
                nc.tensor.matmul(ps[:, bank, :], ones, sums[:], start=True, stop=True).then_inc(sums_ready, 1)
                if rows_bank is not None:
                    for b in range(TB):
                        mm = nc.tensor.matmul(ps[:, rows_bank, b:b + 1], sums[:, b * P:(b + 1) * P],
                                              ones[:, 0:1], start=True, stop=True)
                    mm.then_inc(rows_sums_ready, 1)

            def values(first, u, hi, lo, n_blocks, banks, per_unit):
                halves = 2 // per_unit
                pe.wait_ge(w_ready, u + 1)
                for kk in range(per_unit):
                    k = (u - first) * per_unit + kk
                    for b in range(n_blocks):
                        for h in range(halves):
                            cols = slice((kk * halves + h) * S, (kk * halves + h + 1) * S)
                            mm = product(ps[:, banks[b * halves + h], :],
                                         hi[:, k, b * P:(b + 1) * P], lo[:, k, b * P:(b + 1) * P],
                                         w_hi[:, u % 2, cols], w_lo[:, u % 2, cols], k == 0, k == KC - 1)
                mm.then_inc(used, 1)

            def into_residual(name, n, bank0, hi, lo, ready, chunk_ready, bank_free):
                u0 = FIRST[name]

                def unit(k, i, first, final):
                    u = u0 + k
                    pe.wait_ge(w_ready, at(u + 1, i, 2))
                    pe.wait_ge(ready, at(chunk_ready(k), i, 2))
                    kk = at(k, i, 2)
                    for j in range(KC):
                        if first and j in bank_free:
                            pe.wait_ge(*bank_free[j])
                        wh, wl = tile(u % 2, j)
                        mm = product(ps[:, (bank0 + j) % 8, :], wh, wl, hi[:, kk, :], lo[:, kk, :], first, final)
                        if final and j < KC - 1:
                            mm.then_inc(proj_sums, 1)
                    mm.then_inc(used, 1)

                unit(0, None, True, False)
                unit(1, None, False, False)
                if n > 4:
                    with pe.Fori(0, n // 2 - 2) as i:
                        unit(2, i, False, False)
                        unit(3, i, False, False)
                unit(n - 2, None, False, False)
                unit(n - 1, None, False, True)

            def hidden(name, norm, st, base):
                u0 = FIRST[name]
                panel(u0, None, ps[:, base, :], xg_hi, xg_lo, KC * SPLIT[norm])
                square_sums(norm, (base + 2) % 8)
                panel(u0 + 1, None, ps[:, base + 1, :], xg_hi, xg_lo)
                with pe.Fori(0, FC - 1) as i:
                    for s in range(2):
                        pe.wait_ge(st["scaled"], at(s + 1, i, 2))
                        panel(u0 + 2 + s, i, ps[:, base + s, :], xg_hi, xg_lo)

            def attention_turn(a, buf, n_items, s_of, t_of, pv_of):
                for m in range(n_items + 3):
                    if m < n_items:
                        s_of(m)
                    if 0 <= m - 2 < n_items:
                        t_of(m - 2)
                    if 0 <= m - 3 < n_items:
                        pv_of(m - 3)

            u0 = FIRST["w_in"]
            pe.wait_ge(loads["con"], 16)
            panel(u0, None, ps[:, 0, :], xg_hi, xg_lo, 0)
            square_sums("mix", 2, 3)
            panel(u0 + 1, None, ps[:, 1, :], xg_hi, xg_lo)
            with pe.Fori(0, 7) as i:
                for s in range(2):
                    pe.wait_ge(w_in["evacuated"], at(s + 1, i, 2))
                    panel(u0 + 2 + s, i, ps[:, s, :], xg_hi, xg_lo)
            pe.wait_ge(w_in["evacuated"], 15)
            panel(u0 + 16, None, ps[:, 0, :], xg_hi, xg_lo)
            for u in range(u0 + 17, u0 + 21):
                values(u0 + 17, u, xg_hi, xg_lo, TB, (4, 5, 6, 7), 2)
                c = u - u0 - 17
                if c >= 2:
                    pe.wait_ge(rot["prod"], c - 1)
                pe.wait_ge(w_in["evacuated"], 10 + c)
                pe.wait_ge(r_ready, 1)
                pe.wait_ge(rows_ready, 1)
                nc.tensor.matmul(ps[:, 2 + c % 2, :], con[:, CAT["rope_perm"]:CAT["rope_perm"] + P],
                                 mix["proj"][:, 9 + c, :], start=True, stop=True).then_inc(rot["swapped"], 1)
            for c in range(GC):
                pe.wait_ge(small["pooled"], c + 1)
                pe.wait_ge(loads["tables"], 16 * N_TABLES)
                pe.wait_ge(w_in["evacuated"], 17)
                nc.tensor.matmul(ps[:, c, :], rope["pool_w"][:, c, :], rope["z"][:, c, :],
                                 start=True, stop=True).then_inc(small["product"], 1)
            pe.wait_ge(gate["c"], 1)
            pe.wait_ge(rot["prod"], 4)
            for b in range(TB):
                mm = nc.tensor.matmul(ps[:, 2, b * N_FORGET:(b + 1) * N_FORGET], mix["c_rows"][0:N_FORGET, b * P:(b + 1) * P],
                                      ident[0:N_FORGET, 0:N_FORGET], start=True, stop=True)
            mm.then_inc(gate["turned"], 1)
            pe.wait_ge(loads["tables"], 16 * N_TABLES)
            pe.wait_ge(mix_ready, 4)
            for h in range(N_FORGET):
                if h >= 2:
                    pe.wait_ge(gate["rows"], h)
                nc.tensor.matmul(ps[:, h % 2, :], rope["heads"][0:N_FORGET, h * P:(h + 1) * P],
                                 mix["c_rows"][0:N_FORGET, :], start=True, stop=True).then_inc(gate["turned"], 1)
            pe.wait_ge(gate["rows"], 1 + N_FORGET)

            def group_buffers(t, names):
                return (at1[f"{name}{t // 8 % 2}"] for name in names)

            def scores(t):
                b, h = t % 8 // 2, t % 2
                rows = slice(HD * h, HD * h + HD)
                if t % 8 == 0:
                    pe.wait_ge(a1["staged"], t // 8 + 1)
                if t >= 2:
                    pe.wait_ge(a1["least"], t - 1)
                w = P * (b + 1)
                qh, ql, kh, kl = group_buffers(t, ("qhi", "qlo", "khi", "klo"))
                product(ps[:, t % 2, 0:w], qh[rows, b * P:(b + 1) * P], ql[rows, b * P:(b + 1) * P],
                        kh[rows, 0:w], kl[rows, 0:w], True, True).then_inc(a1["scores"], 1)

            def turn(t):
                pe.wait_ge(a1["probs"], t + 1)
                if t >= 2:
                    pe.wait_ge(a1["pt"], t - 1)
                for j in range(t % 8 // 2 + 1):
                    mm = nc.tensor.transpose(ps[:, 2 + t % 2, j * P:(j + 1) * P], at1["e"][:, t % 3, j * P:(j + 1) * P], ident)
                mm.then_inc(a1["turned"], 1)

            def weigh(t):
                b, h = t % 8 // 2, t % 2
                pe.wait_ge(a1["pt"], t + 1)
                if t % 8 == 0:
                    pe.wait_ge(a1["v_staged"], t // 8 + 1)
                    pe.wait_ge(mix_ready, 4 + t // 8)
                vh, vl = group_buffers(t, ("vhi", "vlo"))
                for j in range(b + 1):
                    cols = slice(j * P, (j + 1) * P)
                    mm = product(ps[:, 4 + h, b * P:(b + 1) * P], vh[:, cols], vl[:, cols],
                                 at1["pt_hi"][:, t % 2, cols], at1["pt_lo"][:, t % 2, cols], j == 0, j == b)
                mm.then_inc(a1["pv"], 1)

            def memory_half(t):
                m, half = t // 2, t % 2
                u = FIRST["mem_k"] + m
                if half == 0:
                    pe.wait_ge(w_ready, u + 1)
                    if m == 0:
                        pe.wait_ge(mem["lo"], KC)
                    if m == 1:
                        pe.wait_ge(mem["rms"], 2)
                    if 2 <= m < KC:
                        pe.wait_ge(mem["k_ready"], m - 1)
                    if m == KC:
                        pe.wait_ge(mem["k_ready"], KC)
                    if m == KC + 4:
                        pe.wait_ge(mem["v_ready"], MB)
                if m < KC:
                    for k in range(KC // 2 * half, KC // 2 * (half + 1)):
                        wh, wl = tile(u % 2, k)
                        mm = product(ps[:, 6 + m % 2, 0:M], wh, wl, mem_split(xg_hi, k), mem_split(xg_lo, k), k == 0, k == KC - 1)
                else:
                    k = 2 * (m % 4) + half
                    cols = slice(half * S, (half + 1) * S)
                    for b in range(MB):
                        block_ = slice(b * P, (b + 1) * P)
                        mm = product(ps[:, 6 + b, :], mem_split(xg_hi, k)[:, block_], mem_split(xg_lo, k)[:, block_],
                                     w_hi[:, u % 2, cols], w_lo[:, u % 2, cols], k == 0, k == KC - 1)
                if half:
                    mm.then_inc(used, 1)
                if t == 1:
                    pe.wait_ge(mem["summed"], KC)
                    nc.tensor.matmul(ps[:, 7, 0:M], ones, memory["acc"][:], start=True, stop=True)
                    for b in range(MB):
                        mm = nc.tensor.matmul(ps[:, 7, M + b:M + b + 1], memory["acc"][:, b * P:(b + 1) * P], ones[:, 0:1],
                                              start=True, stop=True)
                    mm.then_inc(mem["sums"], 1)

            for t in range(MIX_ITEMS + 5):
                if 0 <= t - 3 < MIX_ITEMS:
                    turn(t - 3)
                if t < MIX_ITEMS:
                    scores(t)
                if 0 <= t - MEM_LAG < 4 * KC:
                    memory_half(t - MEM_LAG)
                if t >= 5:
                    weigh(t - 5)

            into_residual("w_out", KC, 0, mix["hi"], mix["lo"], mix_ready, lambda k: k + 1,
                          {0: (a1["least"], MIX_ITEMS), 2: (a1["pt"], MIX_ITEMS), 4: (mix_ready, 8),
                           6: (mem["v_ready"], 2 * MB)})

            u0 = FIRST["xq"]
            panel(u0, None, ps[:, 0, :], xg_hi, xg_lo, KC * SPLIT["xa"])
            square_sums("xa", 6)
            panel(u0 + 1, None, ps[:, 1, :], xg_hi, xg_lo)
            with pe.Fori(0, KC // 2 - 1) as i:
                for s in range(2):
                    pe.wait_ge(xqs["ready"], at(s + 1, i, 2))
                    panel(u0 + 2 + s, i, ps[:, s, :], xg_hi, xg_lo)
            pe.wait_ge(xqs["ready"], KC)
            pe.wait_ge(mem["v_ready"], 2 * MB)
            with pe.Fori(0, XA_HEADS // 2) as c:
                def item(n):
                    return n // TB, n % TB

                def scores(n):
                    s, b = item(n)
                    if b == 0:
                        pe.wait_ge(a2["staged"], at(s + 1, c, 2))
                    if n >= 2:
                        pe.wait_ge(a2["exps"], at(n - 1, c, 8))
                    qh, ql, kh, kl = (at2[f"{p}{s}"] for p in ("qhi", "qlo", "khi", "klo"))
                    for d in range(XC):
                        qc = slice(d * S + b * P, d * S + (b + 1) * P)
                        kc = slice(d * M, (d + 1) * M)
                        mm = product(ps[:, n % 2, 0:M], qh[:, qc], ql[:, qc], kh[:, kc], kl[:, kc], d == 0, d == XC - 1)
                    mm.then_inc(a2["scores"], 1)

                def turn(n):
                    pe.wait_ge(a2["probs"], at(n + 1, c, 8))
                    if n >= 2:
                        pe.wait_ge(a2["pt"], at(n - 1, c, 8))
                    for j in range(MB):
                        mm = nc.tensor.transpose(ps[:, 2 + n % 2, j * P:(j + 1) * P],
                                                 at2["e"][:, n % 3, j * P:(j + 1) * P], ident)
                    mm.then_inc(a2["turned"], 1)

                def weigh(n):
                    s, b = item(n)
                    pe.wait_ge(a2["pt"], at(n + 1, c, 8))
                    vh, vl = at2[f"vhi{s}"], at2[f"vlo{s}"]
                    for d in range(XC):
                        for j in range(MB):
                            vc = slice((j * XC + d) * P, (j * XC + d + 1) * P)
                            pc = slice(j * P, (j + 1) * P)
                            mm = product(ps[:, 4 + 2 * s + d, b * P:(b + 1) * P], vh[:, vc], vl[:, vc],
                                         at2["pt_hi"][:, n % 2, pc], at2["pt_lo"][:, n % 2, pc], j == 0, j == MB - 1)
                    mm.then_inc(a2["pv"], 1)

                attention_turn(a2, at2, 8, scores, turn, weigh)

            into_residual("xo", KC, 0, xa["hi"], xa["lo"], a2["out"], lambda k: k + 1, {0: (a2["pt"], 16), 4: (a2["out"], KC)})

            st = ffn_stages["up"]
            hidden("up", "ffn", st, 0)
            into_residual("down", FC, 2, ffn["hi"], ffn["lo"], st["hid"], lambda k: k + 1,
                          {0: (r_ready, NORM["ffn"] + 1), 6: (st["scaled"], 2 * FC - 1), 7: (st["scaled"], 2 * FC)})

            u0 = FIRST["a_v"]
            for u in range(u0, u0 + 4):
                pe.wait_ge(xg_ready, KC * SPLIT["first"] + max(4, 2 * (u - u0 + 1)))
                values(u0, u, xg_hi, xg_lo, TB, (2, 3, 4, 5), 2)
                if u == u0 + 1:
                    square_sums("first", 6, 7)
                if u == u0 + 2:
                    square_sums("a", 0, 1, first["sums"])
            pe.wait_ge(rows_rms_ready, ROWS["first"] + 1)
            pe.wait_ge(a_in["first"], 2)
            for u in range(u0 + 4, u0 + KC):
                values(u0 + 4, u, xg_hi, xg_lo, TB, (6, 7, 0, 1), 2)
            u0 = FIRST["a_u"]
            pe.wait_ge(a_in["v"], 4)
            panel(u0, None, ps[:, 2, :], xg_hi, xg_lo)
            panel(u0 + 1, None, ps[:, 3, :], xg_hi, xg_lo)
            with pe.Fori(0, KC // 2 - 1) as i:
                for s in range(2):
                    pe.wait_ge(a_in["scaled"], at(s + 1, i, 2))
                    panel(u0 + 2 + s, i, ps[:, 2 + s, :], xg_hi, xg_lo)
            pe.wait_ge(a_in["w_lo"], 1)
            for g in range(N_SPATIAL):
                if g >= 2:
                    pe.wait_ge(a_in["z"], g - 1)
                for b in range(TB):
                    if g == 0:
                        pe.wait_ge(a_in["v_lo"], b + 1)
                    mm = product(ps[:, 4 + g % 2, b * P:(b + 1) * P],
                                 sg["v_hi"][:, b, g * P:(g + 1) * P], sg["v_lo"][:, b, g * P:(g + 1) * P],
                                 sg["w_hi"][:, g * P:(g + 1) * P], sg["w_lo"][:, g * P:(g + 1) * P], True, True)
                mm.then_inc(a_in["z_done"], 1)
            into_residual("a_out", KC, 0, sg["hi"], sg["lo"], a_in["ready"], lambda k: k + 1,
                          {0: (a_in["v"], 8), 2: (a_in["scaled"], KC), 4: (a_in["z"], N_SPATIAL - 1), 5: (a_in["z"], N_SPATIAL)})

            st = ffn_stages["gu0"]
            hidden("gu0", "ffn0", st, 0)
            into_residual("down0", FC, 2, ffn["hi"], ffn["lo"], st["hid"], lambda k: k + 1,
                          {0: (r_ready, NORM["ffn0"] + 1), 6: (st["scaled"], 2 * FC - 1), 7: (st["scaled"], 2 * FC)})

            u0 = FIRST["kv_v"]
            for u in range(u0, u0 + 4):
                pe.wait_ge(xg_ready, KC * SPLIT["kv"] + max(4, 2 * (u - u0 + 1)))
                values(u0, u, xg_hi, xg_lo, TB, (2, 3, 4, 5), 2)
                if u == u0 + 1:
                    pe.wait_ge(xg_ready, KC * SPLIT["kv"] + 6)
                    square_sums("kv", 6, 7)
            pe.wait_ge(r_ready, NORM["kv"] + 1)
            pe.wait_ge(rows_ready, ROWS["kv"] + 1)
            pe.wait_ge(x_ready, KC * NORM["kv"])
            for u in range(u0 + 4, u0 + KC):
                values(u0 + 4, u, xg_hi, xg_lo, TB, (6, 7, 0, 1), 2)
            qk0 = FIRST["qk"]

            def half_panel(u, i, to, hi, lo, half):
                if half == 0:
                    pe.wait_ge(w_ready, at(u + 1, i, 4))
                for k in range(KC // 2 * half, KC // 2 * (half + 1)):
                    wh, wl = tile(u % 2, k)
                    mm = product(to, wh, wl, hi[:, k, :], lo[:, k, :], k == 0, k == KC - 1)
                if half:
                    mm.then_inc(used, 1)

            def qk_input(p):
                return (da["xb_hi"], da["xb_lo"]) if p % 2 else (xg_hi, xg_lo)

            pe.wait_ge(kv["v"], 4)
            for p in range(4):
                if p == 1:
                    pe.wait_ge(kv["xb"], KC)
                for half in range(2):
                    half_panel(qk0 + p, None, ps[:, 2 + p, :], *qk_input(p), half)
            pe.wait_ge(kv["v"], 8)
            pe.wait_ge(kv["qk"], 4)

            def diff_item(n, c, base):
                def scores(n):
                    s, b = n // TB, n % TB
                    if b == 0:
                        pe.wait_ge(a3["staged"], at(2 * (base // TB + s + 1), c, 4))
                    if c is not None or n + base >= 2:
                        pe.wait_ge(a3["least"], at(2 * (base + n - 1), c, 16))
                    w = P * (b + 1)
                    qh, ql, kh, kl = (at3[f"{p}{s % 2}"] for p in ("qhi", "qlo", "khi", "klo"))
                    block_ = slice(b * P, (b + 1) * P)
                    for k, (q_, k_) in enumerate(((qh, kh), (qh, kl), (ql, kh))):
                        for h in range(2):
                            rows = slice(HD * h, HD * h + HD)
                            mm = nc.tensor.matmul(ps[:, 2 * (n % 2) + h, 0:w], q_[rows, block_], k_[rows, 0:w],
                                                  start=k == 0, stop=k == 2)
                            if k == 2:
                                mm.then_inc(a3["scores"], 1)

                def turn(n):
                    b = n % TB
                    pe.wait_ge(a3["probs"], at(base + n + 1, c, 8))
                    if c is not None or n + base >= 2:
                        pe.wait_ge(a3["pt"], at(base + n - 1, c, 8))
                    for j in range(b + 1):
                        mm = nc.tensor.transpose(ps[:, 4 + n % 2, j * P:(j + 1) * P],
                                                 at3["e"][:, 2 * (n % DIFF_SLOTS), j * P:(j + 1) * P], ident)
                    mm.then_inc(a3["turned"], 1)

                def weigh(n):
                    s, b = n // TB, n % TB
                    pe.wait_ge(a3["pt"], at(base + n + 1, c, 8))
                    if b == 0:
                        pe.wait_ge(a3["v_staged"], at(base // TB + s + 1, c, 2))
                        pe.wait_ge(a3["out"], at(base // TB + s + 1, c, 2))
                    vh, vl = at3[f"vhi{s % 2}"], at3[f"vlo{s % 2}"]
                    for j in range(b + 1):
                        cols = slice(j * P, (j + 1) * P)
                        mm = product(ps[:, 6, b * P:(b + 1) * P], vh[:, cols], vl[:, cols],
                                     at3["pt_hi"][:, n % 2, cols], at3["pt_lo"][:, n % 2, cols], j == 0, j == b)
                    mm.then_inc(a3["pv"], 1)

                if live(n - 4, c, base):
                    turn(n - 4)
                if live(n, c, base):
                    scores(n)
                if base == 0:
                    p = 4 + n // 2
                    if n % 2 == 0:
                        pe.wait_ge(kv["qk"], at(p, c, 4))
                    half_panel(qk0 + p, c, ps[:, 7, :], *qk_input(p), n % 2)
                if live(n - 6, c, base):
                    weigh(n - 6)
                if n >= 8:
                    head_sums(n - 8)

            def head_sums(h):
                if h == 0:
                    pe.wait_ge(a3["least"], 8 * N_DIFF - 2)
                pe.wait_ge(a3["sq"], h + 1)
                pick = con[:, CAT["pick"] + N_DIFF - 1 - h:CAT["pick"] + 2 * N_DIFF - 1 - h]
                nc.tensor.matmul(ps[0:N_DIFF, 0, :], pick, squares[:, h % 2, :], start=h == 0,
                                 stop=h == N_DIFF - 1).then_inc(a3["summed"], 1)

            diff_turns(pe, diff_item, 6)
            for h in range(6, N_DIFF):
                head_sums(h)
            pe.wait_ge(a3["least"], 8 * N_DIFF)
            pe.wait_ge(loads["alibi"], 2 * 16)
            pe.wait_ge(a3["rms"], 2)
            for h in range(N_DIFF):
                if h >= 4:
                    pe.wait_ge(a3["normed"], h - 3)
                pick = da["picks"][:, h * P:(h + 1) * P]
                nc.tensor.matmul(ps[:, h % 4, :], pick, da["rms"], start=True, stop=True).then_inc(a3["spread"], 1)
            into_residual("bo", KC, 4, xg_hi, xg_lo, a3["out_lo"], lambda k: k + 1, {0: (a3["out"], N_DIFF + 1), 3: (kv["qk"], 2 * KC), 4: (a3["normed"], N_DIFF)})

            st = ffn_stages["gu1"]
            hidden("gu1", "ffn1", st, 4)
            into_residual("down1", FC, 6, ffn["hi"], ffn["lo"], st["hid"], lambda k: k + 1,
                          {0: (r_ready, NORM["ffn1"] + 1), 6: (st["scaled"], 2 * FC - 1), 7: (st["scaled"], 2 * FC)})
            pe.wait_ge(x_ready, KC * NORM["final"])
            square_sums("final", 0)

        @block.scalar
        def _(act):
            def split(u, i=None):
                if u >= N_UNITS:
                    return
                act.wait_ge(w_loaded[u % 2], at(16 * (u // 2 + 1), i, 16))
                if u >= 2:
                    act.wait_ge(used, at(u - 1, i, 2))
                nc.scalar.activation(w_hi[:, u % 2, :], w_raw[:, u % 2, :], ACT.Copy).then_inc(w_hi_ready, 1)

            def norm_input(norm, gain, finals_only=False):
                n = NORM[norm]
                for c in range(KC):
                    if n == 0:
                        act.wait_ge(loads["input"], 2 * 16)
                    else:
                        act.wait_ge(x_ready, KC * (n - 1) + c + 1)
                    if not finals_only:
                        nc.scalar.activation(xg_hi[:, c, :], x[:, c, :], ACT.Copy, scale=column(gain, c)).then_inc(xg_hi_ready, 1)
                    k = KC * n + c
                    if k >= 2:
                        act.wait_ge(summed, k - 1)
                    nc.scalar.activation(squares[:, c % 2, :], x[:, c, :], ACT.Square).then_inc(sq_ready, 1)

            def norm_rms(norm, bank=None, rows_bank=None):
                n = NORM[norm]
                if norm == "a":
                    act.wait_ge(a_in["first"], 4)
                    nc.scalar.activation(first["sums"][:], first["sums"][:], ACT.Sqrt, bias=column("eps"), scale=1.0 / D).then_inc(rms_ready, 1)
                    nc.scalar.activation(first["sums_rows"][:], first["sums_rows"][:], ACT.Sqrt, bias=column("eps"),
                                         scale=1.0 / D).then_inc(rows_rms_ready, 1)
                    return
                act.wait_ge(sums_ready, n + 1)
                if rows_bank is not None:
                    act.wait_ge(rows_sums_ready, ROWS[norm] + 1)
                nc.scalar.activation(square_sum[:], ps[:, bank, :], ACT.Sqrt, bias=column("eps"), scale=1.0 / D).then_inc(rms_ready, 1)
                if rows_bank is not None:
                    if ROWS[norm]:
                        act.wait_ge(rows_ready, ROWS[norm])
                    nc.scalar.activation(rms_rows[:], ps[:, rows_bank, 0:TB], ACT.Sqrt, bias=column("eps"),
                                         scale=1.0 / D).then_inc(rows_rms_ready, 1)

            def splits_of(name, n, skip_last=0):
                u0 = FIRST[name]
                with act.Fori(0, n // 2 - 1) as i:
                    split(u0 + 2, i)
                    split(u0 + 3, i)
                split(u0 + n)
                if not skip_last:
                    split(u0 + n + 1)

            def into_residual(name, n, norm, gain):
                splits_of(name, n, 1)
                norm_input(norm, gain, gain is None)
                split(FIRST[name] + n + 1)

            act.dma_start(con[:], consts).then_inc(loads["con"], 16)
            act.wait_ge(rot["steps"], 11)
            nc.scalar.activation(rope["sin"][:], rope["red"][:], ACT.Sin).then_inc(rot["trig"], 1)
            nc.scalar.activation(rope["cos"][:], rope["ang"][:], ACT.Sin).then_inc(rot["trig"], 1)
            split(0)
            norm_input("mix", "g_mix")
            split(1)
            norm_rms("mix", 2, 3)
            u0 = FIRST["w_in"]
            split(u0 + 2)
            act.wait_ge(lams["dots"], 4)
            nc.scalar.activation(lam_exp[:], lam_dot[:], ACT.Exp).then_inc(lams["exps"], 1)
            with act.Fori(0, 4) as i:
                split(u0 + 3, i)
                split(u0 + 4, i)
            act.wait_ge(w_in["evacuated"], 1)
            nc.scalar.activation(rope["g1"][0:N_FORGET, :], mix["proj"][0:N_FORGET, 0, :], ACT.Abs,
                                 bias=column("b_forget", 0, slice(0, N_FORGET))).then_inc(gate["abs"], 1)
            act.wait_ge(gate["abs"], 1)
            nc.scalar.activation(rope["g2"][0:N_FORGET, :], rope["g1"][0:N_FORGET, :], ACT.Exp, scale=-1.0).then_inc(gate["exp"], 1)
            with act.Fori(0, 5) as i:
                split(u0 + 11, i)
                split(u0 + 12, i)
            for c in range(GC):
                act.wait_ge(small["conv"], c + 1)
                nc.scalar.activation(mix["hi"][:, c, :], mix["proj"][:, 1 + c, :], ACT.Copy).then_inc(small["hi"], 1)
            for c in range(GC):
                act.wait_ge(small["product"], c + 1)
                nc.scalar.activation(mix["hi"][:, GC + c, :], ps[:, c, :], ACT.Copy, scale=column("pool_scale", c)).then_inc(small["hi"], 1)
            split(u0 + 21)
            split(u0 + 22)
            act.wait_ge(gate["turned"], 1)
            nc.scalar.activation(mix["nci"][:].rearrange("p b h -> p (b h)"), ps[:, 2, 0:TB * N_FORGET], ACT.Copy,
                                 scale=-1.0).then_inc(gate["rows"], 1)
            act.wait_ge(mix_ready, 4)
            for h in range(N_FORGET):
                act.wait_ge(gate["turned"], h + 2)
                nc.scalar.activation(mix["proj"][:, 1 + h, :], ps[:, h % 2, :], ACT.Copy).then_inc(gate["rows"], 1)

            def exps_and_turned(a, buf, n_items, exp, hi, extra=None):
                for m in range(n_items + 4):
                    if m < n_items:
                        exp(m)
                    if 0 <= m - 2 < n_items:
                        hi(m - 2)
                    if extra is not None:
                        extra(m - 4)

            act.wait_ge(summed, KC)
            act.wait_ge(r_ready, 1)
            act.wait_ge(gate["c"], 1)
            act.dma_start(squares[:].rearrange("p a t -> p (a t)"), mem_cols[:, 0:4, :].rearrange("p c t -> p (c t)")
                          ).then_inc(loads["mem"], 16)
            act.dma_start(square_sum[:], mem_cols[:, 4:6, :].rearrange("p c t -> p (c t)")).then_inc(loads["mem"], 16)
            act.dma_start(mix["proj"][:, 0, :], mem_cols[:, 6:8, :].rearrange("p c t -> p (c t)")).then_inc(loads["mem"], 16)

            act.wait_ge(rot["done"], 4)
            act.wait_ge(w_in["evacuated"], 17)
            act.wait_ge(w_in["v_ready"], TB)
            act.wait_ge(used, FIRST["w_in"] + 2 * KC + 5)

            def stage_part(g, name, src, scale):
                to = at1[f"{name}{g % 2}"].rearrange("p (a n) -> p a n", a=src.shape[1])
                return nc.scalar.activation(to, src, ACT.Copy, scale=scale).then_inc(a1["staged_hi"], 1)

            def stage_qk(g):
                s, c = g % 2, g // 2
                if g >= 2:
                    act.wait_ge(a1["scores"], 8 * (g - 1))
                stage_part(g, "qhi", mix["proj"][:, 9 + 4 * s + c:10 + 4 * s + c, :], -HD ** -0.5)
                stage_part(g, "khi", mix["proj"][:, 11 + 4 * s + c:12 + 4 * s + c, :], 1.0)

            def stage_v(g):
                s, c = g % 2, g // 2
                if g >= 2:
                    act.wait_ge(a1["pv"], 8 * (g - 1))
                stage_part(g, "vhi", mix["v"][:, :, G * s + c * P:G * s + (c + 1) * P], 1.0)

            def exp(t):
                act.wait_ge(a1["least"], t + 1)
                w = P * (t % 8 // 2 + 1)
                nc.scalar.activation(at1["e"][:, t % 3, 0:w], at1["e"][:, t % 3, 0:w], ACT.Exp, scale=-1.0,
                                     bias=at1["least"][:, t % 3:t % 3 + 1],
                                     accum_out=at1["sums"][:, t % 3:t % 3 + 1]).then_inc(a1["exps"], 1)

            def hi(t):
                act.wait_ge(a1["turned"], t + 1)
                if t >= 2:
                    act.wait_ge(a1["pv"], t - 1)
                w = P * (t % 8 // 2 + 1)
                nc.scalar.activation(at1["pt_hi"][:, t % 2, 0:w], ps[:, 2 + t % 2, 0:w], ACT.Copy).then_inc(a1["pt_hi"], 1)

            def output(g):
                act.wait_ge(a1["pv"], 8 * (g + 1))
                for h in range(2):
                    rows = slice(HD * h, HD * h + HD)
                    nc.scalar.activation(mix["hi"][rows, 4 + g, :], ps[rows, 4 + h, :], ACT.Copy).then_inc(a1["out_hi"], 1)

            def memory_in(c):
                if c == 0:
                    act.wait_ge(loads["mem"], 3 * 16)
                nc.scalar.activation(mem_split(xg_hi, c), mem_input(c), ACT.Copy, scale=column("g_mem", c)).then_inc(mem["hi"], 1)
                if c >= 2:
                    act.wait_ge(mem["summed"], c - 1)
                nc.scalar.activation(memory["sq"][:, c % 2, :], mem_input(c), ACT.Square).then_inc(mem["sq"], 1)

            def memory_out(t):
                if t == 2:
                    act.wait_ge(mem["sums"], 1)
                    nc.scalar.activation(memory["rms"][:], ps[:, 7, 0:M], ACT.Sqrt, bias=column("eps"), scale=1.0 / D).then_inc(mem["rms"], 1)
                    nc.scalar.activation(memory["rms_rows"][:], ps[:, 7, M:M + MB], ACT.Sqrt, bias=column("eps"),
                                         scale=1.0 / D).then_inc(mem["rms"], 1)
                m = t // 2 - 1
                if t % 2 == 0 and 0 <= m < 2 * KC:
                    if m in (KC + 3, KC + 7):
                        h = (m - KC) // 4
                        act.wait_ge(used, FIRST["mem_k"] + m + 1)
                        act.wait_ge(mem["r"], 2)
                        for b in range(MB):
                            nc.scalar.activation(xa["v"][:, b, h * S:(h + 1) * S], ps[:, 6 + b, :], ACT.Copy,
                                                 scale=memory["r_rows"][:, b:b + 1]).then_inc(mem["v_ready"], 1)
                    split(FIRST["mem_k"] + m + 2)

            stage_qk(0)
            stage_v(0)
            for t in range(MIX_ITEMS + 6):
                if 0 <= t - 4 < MIX_ITEMS:
                    hi(t - 4)
                if t % 8 == 5 and t > 8:
                    output(t // 8 - 1)
                if 0 <= t - 1 < MIX_ITEMS:
                    exp(t - 1)
                g = t // 8 + 1
                if t % 8 == 1 and g < 2 * GC:
                    stage_qk(g)
                if t % 8 == 6 and g < 2 * GC:
                    stage_v(g)
                if t < KC // 2:
                    memory_in(2 * t)
                    memory_in(2 * t + 1)
                memory_out(t - MEM_LAG)

            u0 = FIRST["w_out"]
            split(u0 + 2)
            split(u0 + 3)
            for u in range(u0 + 4, u0 + KC + 1):
                split(u)
            norm_input("xa", "g_xa")
            split(u0 + KC + 1)
            norm_rms("xa", 6)
            splits_of("xq", KC)
            act.wait_ge(xqs["ready"], KC)
            act.wait_ge(mem["v_ready"], 2 * MB)
            with act.Fori(0, XA_HEADS // 2) as c:
                for s in range(2):
                    parts = ((f"qhi{s}", xa["q"][:, bass.ds(c * (2 * XC) + XC * s, XC), :], -(XC * P) ** -0.5),
                             (f"khi{s}", xa["k"][:, bass.ds(c * (2 * XC) + XC * s, XC), :], 1.0),
                             (f"vhi{s}", xa["v"][:, :, bass.ds(c * (2 * XC * P) + XC * P * s, XC * P)], 1.0))
                    for name, src, scale in parts:
                        to = at2[name][:].rearrange("p (a n) -> p a n", a=src.shape[1])
                        nc.scalar.activation(to, src, ACT.Copy, scale=scale).then_inc(a2["staged_hi"], 1)

                def exp(n):
                    if n >= 3:
                        act.wait_ge(a2["turned"], at(n - 2, c, 8))
                    act.wait_ge(a2["least"], at(n + 1, c, 8))
                    nc.scalar.activation(at2["e"][:, n % 3, :], ps[:, n % 2, 0:M], ACT.Exp, scale=-1.0,
                                         bias=at2["least"][:, n % 3:n % 3 + 1],
                                         accum_out=at2["sums"][:, n % 3:n % 3 + 1]).then_inc(a2["exps"], 1)

                def hi(n):
                    act.wait_ge(a2["turned"], at(n + 1, c, 8))
                    if n >= 2:
                        act.wait_ge(a2["pv"], at(n - 1, c, 8))
                    nc.scalar.activation(at2["pt_hi"][:, n % 2, :], ps[:, 2 + n % 2, 0:M], ACT.Copy).then_inc(a2["pt_hi"], 1)

                def outputs(n):
                    if n not in (TB - 1, 2 * TB - 1):
                        return
                    s = n // TB
                    act.wait_ge(a2["pv"], at(n + 1, c, 8))
                    for d in range(XC):
                        nc.scalar.activation(xa["hi"][:, bass.ds(c * (2 * XC) + XC * s + d, 1), :].rearrange("p a n -> p (a n)"),
                                             ps[:, 4 + 2 * s + d, :], ACT.Copy).then_inc(a2["out_hi"], 1)

                exps_and_turned(a2, at2, 8, exp, hi, outputs)
            into_residual("xo", KC, "ffn", "g_ffn")

            st = ffn_stages["up"]
            norm_rms("ffn", 2)

            def conv_gate(i, done):
                act.wait_ge(st["steps"], at(4 * done + 4, i, 4))
                nc.scalar.activation(ffn["gate"][:], ffn["tg"][:], ACT.Silu).then_inc(st["gated"], 1)

            def conv_hidden(i, done):
                act.wait_ge(st["product"], at(done + 1, i, 1))
                nc.scalar.activation(ffn["hi"][:, bass.ds(at(done, i, 1), 1), :].rearrange("p a n -> p (a n)"), ffn["h"][:],
                                     ACT.Copy).then_inc(st["hid_hi"], 1)

            def conv_turn(i, first):
                u = FIRST["up"]
                if not first:
                    conv_gate(i, -1)
                for s, (src, to) in enumerate(((ffn["ua"], ffn["ta"]), (ffn["ug"], ffn["tg"]))):
                    split(u + 2 + s, i)
                    if s == 0 and not first:
                        act.wait_ge(st["product"], at(0, i, 1))
                    act.wait_ge(st["scaled"], at(s + 1, i, 2))
                    nc.scalar.activation(to[:], src[:, 2:S + 2], ACT.Copy,
                                         scale=column("w_ffconv", at(2 * 2 * FC + s * FC, i, 1))).then_inc(st["tapped"], 1)
                    if s == 0 and not first:
                        conv_hidden(i, -1)

            conv_turn(None, True)
            with act.Fori(1, FC) as i:
                conv_turn(i, False)
            conv_gate(None, FC - 1)
            conv_hidden(None, FC - 1)
            act.wait_ge(st["hid"], FC)
            act.dma_start(sg["w"][:], spatial).then_inc(loads["spatial"], 16)
            act.dma_start(sg["b"][:].rearrange("p g t -> p (g t)"), spatial_bias).then_inc(loads["spatial"], 16)
            into_residual("down", FC, "first", "a_gain")

            u0 = FIRST["a_v"]
            for c in range(KC):
                k = KC * NORM["a"] + c
                act.wait_ge(summed, k - 1)
                nc.scalar.activation(squares[:, c % 2, :], x[:, c, :], ACT.Square, scale=column("g_first", c)).then_inc(sq_ready, 1)
                if c == KC // 2:
                    split(u0 + 2)
            split(u0 + 3)
            norm_rms("first", 6, 7)
            split(u0 + 4)
            norm_rms("a")
            split(u0 + 5)
            for h in range(2):
                if h:
                    for u in range(u0 + 6, u0 + KC + 2):
                        split(u)
                act.wait_ge(used, u0 + 4 * h + 4)
                act.wait_ge(rows_ready, ROWS["a"] + 1)
                for b in range(TB):
                    bank = ((2, 3, 4, 5), (6, 7, 0, 1))[h][b]
                    nc.scalar.activation(sg["v"][:, b, h * S:(h + 1) * S], ps[:, bank, :], ACT.Gelu_apprx_tanh,
                                         scale=r_rows[:, b:b + 1], accum_out=sg["v_sum"][:, b, h:h + 1]).then_inc(a_in["v"], 1)
            u0 = FIRST["a_u"]

            def gate_panel(s, i):
                act.wait_ge(a_in["scaled"], at(s + 1, i, 2))
                ut = sg["u"][:, bass.ds(at(s, i, 2), 1), :].rearrange("p a n -> p (a n)")
                nc.scalar.activation(ut, ut, ACT.Gelu_apprx_tanh).then_inc(a_in["u"], 1)
                split(u0 + 2 + s, i)

            for b in range(TB):
                act.wait_ge(a_in["steps"], 2)
                nc.scalar.activation(sg["hi"][:, 2 * b:2 * b + 2, :], sg["v"][:, b, :].rearrange("p (a n) -> p a n", a=2),
                                     ACT.Square, bias=sg["mean"][:, b:b + 1], accum_out=sg["v_sq"][:, b:b + 1]).then_inc(a_in["v_sq"], 1)
            gate_panel(0, None)
            act.wait_ge(a_in["v_sq"], TB)
            nc.scalar.activation(sg["std"][:], sg["v_sq"][:], ACT.Sqrt, bias=column("eps"), scale=1.0 / D).then_inc(a_in["std"], 1)
            act.wait_ge(a_in["w"], 1)
            nc.scalar.activation(sg["w_hi"][:], sg["w"][:], ACT.Copy).then_inc(a_in["w_hi"], 1)
            gate_panel(1, None)
            for b in range(TB):
                act.wait_ge(a_in["normed"], b + 1)
                nc.scalar.activation(sg["v_hi"][:, b, :], sg["v"][:, b, :], ACT.Copy).then_inc(a_in["v_hi"], 1)
            with act.Fori(1, KC // 2) as i:
                for s in range(2):
                    gate_panel(s, i)
            for g in range(N_SPATIAL):
                act.wait_ge(a_in["product"], g + 1)
                nc.scalar.activation(sg["hi"][:, g, :], sg["u"][:, g, :], ACT.Copy).then_inc(a_in["hi"], 1)
            into_residual("a_out", KC, "ffn0", "ffn_norm0")

            def swiglu(name, norm, base):
                st = ffn_stages[name]
                norm_rms(norm, (base + 2) % 8)
                with act.Fori(0, FC) as i:
                    act.wait_ge(st["scaled"], at(1, i, 2))
                    nc.scalar.activation(ffn["gate"][:], ffn["tg"][:], ACT.Silu).then_inc(st["gated"], 1)
                    split(FIRST[name] + 2, i)
                    split(FIRST[name] + 3, i)
                    act.wait_ge(st["product"], at(1, i, 1))
                    nc.scalar.activation(ffn["hi"][:, bass.ds(at(0, i, 1), 1), :].rearrange("p a n -> p (a n)"), ffn["h"][:],
                                         ACT.Copy).then_inc(st["hid_hi"], 1)

            swiglu("gu0", "ffn0", 0)
            into_residual("down0", FC, "kv", "kv_norm")

            act.dma_start(da["alibi"][:], alibi_table).then_inc(loads["alibi"], 16)
            u0 = FIRST["kv_v"]
            split(u0 + 2)
            norm_rms("kv", 6, 7)
            for h in range(2):
                for u in range(u0 + 4 * h + (h == 0), u0 + 4 * h + 4):
                    split(u + 2)
                    if h:
                        for c in range(2 * (u - u0 - 4), 2 * (u - u0 - 4) + 2):
                            nc.scalar.activation(da["xb_hi"][:, c, :], x[:, c, :], ACT.Copy,
                                                 scale=column("b_norm", c)).then_inc(kv["xb_hi"], 1)
                act.wait_ge(used, u0 + 4 * h + 4)
                act.wait_ge(rows_ready, ROWS["kv"] + 1)
                for b in range(TB):
                    bank = ((2, 3, 4, 5), (6, 7, 0, 1))[h][b]
                    nc.scalar.activation(da["v"][:, b, h * S:(h + 1) * S], ps[:, bank, :], ACT.Copy,
                                         scale=r_rows[:, b:b + 1]).then_inc(kv["v"], 1)
            qk0 = FIRST["qk"]
            for p in range(4):
                split(qk0 + p + 2)

            def diff_item(n, c, base):
                def hi(n):
                    act.wait_ge(a3["turned"], at(base + n + 1, c, 8))
                    if c is not None or n + base >= 2:
                        act.wait_ge(a3["pv"], at(base + n - 1, c, 8))
                    w = P * (n % TB + 1)
                    nc.scalar.activation(at3["pt_hi"][:, n % 2, 0:w], ps[:, 4 + n % 2, 0:w], ACT.Copy).then_inc(a3["pt_hi"], 1)

                def exp(n):
                    w = P * (n % TB + 1)
                    for h in range(2):
                        k = 2 * (n % DIFF_SLOTS) + h
                        act.wait_ge(a3["least"], at(2 * (base + n) + h + 1, c, 16))
                        nc.scalar.activation(at3["e"][:, k, 0:w], at3["e"][:, k, 0:w], ACT.Exp, scale=-1.0,
                                             bias=at3["least"][:, k:k + 1], accum_out=at3["sums"][:, k:k + 1]).then_inc(a3["exps"], 1)

                def second(n):
                    act.wait_ge(a3["second"], at(base + n + 1, c, 8))
                    w = P * (n % TB + 1)
                    k = 2 * (n % DIFF_SLOTS) + 1
                    nc.scalar.activation(at3["e"][:, k, 0:w], at3["e"][:, k, 0:w], ACT.Copy,
                                         scale=at3["second"][:, k:k + 1]).then_inc(a3["weighed"], 1)

                def output(n):
                    s = n // TB
                    act.wait_ge(a3["pv"], at(base + n + 1, c, 8))
                    h = bass.ds(at(base // TB + s, c, 2), 1)
                    nc.scalar.activation(da["o"][:, h, :].rearrange("p a n -> p (a n)"), ps[:, 6, :],
                                         ACT.Copy).then_inc(a3["out"], 1)

                if live(n - 5, c, base):
                    hi(n - 5)
                if n % TB == 2 and live(n - 7, c, base):
                    output(n - 7)
                if live(n - 1, c, base):
                    exp(n - 1)
                if live(n - 2, c, base):
                    second(n - 2)
                if qk_due(n, c, base):
                    split_qk(n, c, base)
                if n >= 8:
                    head_square(n - 8)

            def split_qk(n, c, base):
                u = qk0 + 3 + (base + n) // 2 + 2
                act.wait_ge(w_loaded[u % 2], at(16 * (u // 2 + 1), c, 32))
                act.wait_ge(used, at(u - 1, c, 4))
                nc.scalar.activation(w_hi[:, u % 2, :], w_raw[:, u % 2, :], ACT.Copy).then_inc(w_hi_ready, 1)

            def head_square(h):
                if h == 0:
                    act.wait_ge(a3["staged"], 2 * N_DIFF)
                act.wait_ge(a3["out"], h + 2)
                if h >= 2:
                    act.wait_ge(a3["summed"], h - 1)
                nc.scalar.activation(squares[:, h % 2, :], da["o"][:, h, :], ACT.Square).then_inc(a3["sq"], 1)

            act.sem_inc(a3["out"], 1)
            diff_turns(act, diff_item, 7)
            act.wait_ge(a3["turned"], 4 * N_DIFF)
            act.dma_start(da["picks"], head_picks).then_inc(loads["alibi"], 16)
            head_square(N_DIFF - 1)
            act.wait_ge(a3["summed"], N_DIFF)
            nc.scalar.activation(da["rms"], ps[0:N_DIFF, 0, :], ACT.Sqrt, bias=column("eps", 0, slice(0, N_DIFF)),
                                 scale=1.0 / P).then_inc(a3["rms"], 1)
            for h in range(N_DIFF):
                act.wait_ge(a3["normed"], h + 1)
                nc.scalar.activation(xg_hi[:, h, :], da["o"][:, h, :], ACT.Copy).then_inc(a3["out_hi"], 1)
            into_residual("bo", KC, "ffn1", "ffn_norm1")
            swiglu("gu1", "ffn1", 4)
            into_residual("down1", FC, "final", None)
            norm_rms("final", 0)

        @block.vector
        def _(dve):
            def split(u, i=None):
                if u >= N_UNITS:
                    return
                dve.wait_ge(w_hi_ready, at(u + 1, i, 2))
                nc.vector.tensor_tensor(w_lo[:, u % 2, :], w_raw[:, u % 2, :], w_hi[:, u % 2, :].bitcast(F32),
                                        ALU.subtract).then_inc(w_ready, 1)

            def gained(norm, gain, c):
                dve.wait_ge(xg_hi_ready, KC * SPLIT[norm] + c + 1)
                nc.vector.scalar_tensor_tensor(out=xg_lo[:, c, :], in0=x[:, c, :], scalar=column(gain, c),
                                               in1=xg_hi[:, c, :].bitcast(F32), op0=ALU.mult,
                                               op1=ALU.subtract).then_inc(xg_ready, 1)

            def norm_r(norm, rows=False):
                n = NORM[norm]
                dve.wait_ge(rms_ready, n + 1)
                nc.vector.reciprocal(r_cols[:], square_sum[:]).then_inc(r_ready, 1)
                if rows:
                    dve.wait_ge(rows_rms_ready, ROWS[norm] + 1)
                    nc.vector.reciprocal(r_rows[:], rms_rows[:]).then_inc(rows_ready, 1)
                dve.wait_ge(r_ready, n + 1)

            def scaled(to, bank, signal, cols=S, r=None):
                return nc.vector.tensor_tensor(to, ps[:, bank, 0:cols], r_cols[:] if r is None else r,
                                               ALU.mult).then_inc(signal, 1)

            def chunk(t, c):
                return t[:, bass.ds(c, 1), :].rearrange("p a n -> p (a n)")

            def splits_of(name, n, skip_last=0):
                u0 = FIRST[name]
                with dve.Fori(0, n // 2 - 1) as i:
                    split(u0 + 2, i)
                    split(u0 + 3, i)
                split(u0 + n)
                if not skip_last:
                    split(u0 + n + 1)

            def into_residual(name, n, norm, gain, bank0, final_splits=True):
                if final_splits:
                    splits_of(name, n, 1)
                done = KC * (NORM[norm] - 1)
                for j in range(KC + 1):
                    if j < KC:
                        if j < KC - 1:
                            dve.wait_ge(proj_sums, (KC - 1) * RESIDUALS.index(name) + j + 1)
                        else:
                            dve.wait_ge(used, FIRST[name] + n)
                        nc.vector.tensor_tensor(x[:, j, :], ps[:, (bank0 + j) % 8, :], x[:, j, :],
                                                ALU.add).then_inc(x_ready, 1)
                    if j and gain is not None:
                        gained(norm, gain, j - 1)
                split(FIRST[name] + n + 1)

            counted = [0]

            def step(ins, s):
                counted[0] += 1
                ins.then_inc(s, 1)
                dve.wait_ge(s, counted[0])

            dve.wait_ge(loads["early"], 16 * N_EARLY)
            dve.wait_ge(loads["input"], 2 * 16)
            ang, turns, red = rope["ang"][:], rope["turns"][:], rope["red"][:]
            step(nc.vector.tensor_copy(ang, rope["pos"][:]), rot["steps"])
            step(nc.vector.tensor_scalar(ang, ang, column("inv_freq"), None, ALU.mult), rot["steps"])
            step(nc.vector.tensor_scalar(turns, ang, 1.0 / TWO_PI, ROUNDER, ALU.mult, ALU.add), rot["steps"])
            step(nc.vector.tensor_scalar(turns, turns, -ROUNDER, None, ALU.add), rot["steps"])
            for part, src in ((TURN_1, ang), (TURN_2, red), (TURN_3, red), (TURN_4, red)):
                step(nc.vector.scalar_tensor_tensor(out=red, in0=turns, scalar=-part, in1=src, op0=ALU.mult,
                                                    op1=ALU.add), rot["steps"])
            step(nc.vector.tensor_scalar(red, red, PI_BELOW, -PI_BELOW, ALU.min, ALU.max), rot["steps"])
            step(nc.vector.scalar_tensor_tensor(out=ang, in0=red, scalar=-1.0, in1=red, op0=ALU.mult, op1=ALU.max), rot["steps"])
            step(nc.vector.tensor_scalar(ang, ang, -1.0, math.pi / 2, ALU.mult, ALU.add), rot["steps"])
            split(0)
            for c in range(KC):
                if c == 0:
                    dve.wait_ge(loads["input"], 2 * 16)
                gained("mix", "g_mix", c)
            split(1)
            dve.wait_ge(loads["early"], 16 * N_EARLY)
            for h in range(2):
                a, b = (lam_in[:, (2 * h + k) * HD:(2 * h + k + 1) * HD] for k in range(2))
                nc.vector.tensor_tensor_reduce(a, a, b, 1.0, 0.0, ALU.mult, ALU.add, lam_dot[:, h:h + 1]).then_inc(lams["dots"], 1)
            nc.vector.tensor_tensor(par[:, AT["a_gain"]:AT["a_gain"] + KC], par[:, AT["g_first"]:AT["g_first"] + KC],
                                    par[:, AT["a_norm"]:AT["a_norm"] + KC], ALU.mult).then_inc(lams["dots"], 1)
            nc.vector.tensor_scalar(subln[:], column("b_subln"), 1.0 - LAMBDA_INIT, None, ALU.mult).then_inc(lams["dots"], 1)
            norm_r("mix", True)
            u0 = FIRST["w_in"]
            dve.wait_ge(used, u0 + 1)
            scaled(mix["proj"][:, 0, :], 0, w_in["evacuated"])
            split(u0 + 2)
            with dve.Fori(0, 4) as i:
                for s in range(2):
                    dve.wait_ge(used, at(u0 + 2 + s, i, 2))
                    scaled(chunk(mix["proj"], at(1 + s, i, 2)), 1 - s, w_in["evacuated"])
                    split(u0 + 3 + s, i)
            dve.wait_ge(lams["exps"], 1)
            nc.vector.tensor_scalar(lam[:], lam_exp[:, 0:1], lam_exp[:, 1:2], LAMBDA_INIT, ALU.subtract,
                                    ALU.add).then_inc(lams["done"], 1)

            counted[0] = 0
            g1, g2, g3, g4 = (t[0:N_FORGET, :] for t in (rope["g1"], rope["g2"], rope["g3"], rope["g4"]))

            def gate_steps(p):
                if p == 0:
                    step(nc.vector.tensor_scalar(g3, g2, 2.0, None, ALU.add), gate["steps"])
                    step(nc.vector.reciprocal(g1, g3), gate["steps"])
                if p == 1:
                    step(nc.vector.tensor_tensor(g3, g2, g1, ALU.mult), gate["steps"])
                    step(nc.vector.tensor_tensor(g4, g3, g3, ALU.mult), gate["steps"])
                if p == 2:
                    step(nc.vector.tensor_scalar(g1, g4, 1.0 / 15, None, ALU.mult), gate["steps"])
                if 2 <= p < 5:
                    for k in (13 - 4 * (p - 2), 11 - 4 * (p - 2)):
                        step(nc.vector.scalar_tensor_tensor(out=g1, in0=g1, scalar=1.0 / k, in1=g4, op0=ALU.add,
                                                            op1=ALU.mult), gate["steps"])
                if p == 5:
                    step(nc.vector.scalar_tensor_tensor(out=g1, in0=g1, scalar=1.0, in1=g3, op0=ALU.add, op1=ALU.mult),
                         gate["steps"])
                    step(nc.vector.tensor_scalar(g2, mix["proj"][0:N_FORGET, 0, :], column("b_forget", 0, slice(0, N_FORGET)),
                                                 0.0, ALU.add, ALU.min), gate["steps"])
                if p == 6:
                    step(nc.vector.scalar_tensor_tensor(out=g2, in0=g1, scalar=-2.0, in1=g2, op0=ALU.mult, op1=ALU.add),
                         gate["steps"])
                    step(nc.vector.memset(g3, 1.0), gate["steps"])
                if p == 7:
                    nc.vector.tensor_tensor_scan(mix["c_rows"][0:N_FORGET, :], g3, g2, 0.0, ALU.mult, ALU.add).then_inc(gate["c"], 1)

            dve.wait_ge(gate["exp"], 1)
            for p in range(8):
                dve.wait_ge(used, u0 + 10 + p)
                scaled(mix["proj"][:, 9 + p, :], 1 - p % 2, w_in["evacuated"])
                split(u0 + 11 + p)
                gate_steps(p)
            split(u0 + 19)
            dve.wait_ge(rot["trig"], 2)
            for c in range(4):
                if c == 1:
                    split(u0 + 20)
                pc = mix["proj"][:, 9 + c, :]
                dve.wait_ge(rot["swapped"], c + 1)
                if c:
                    dve.wait_ge(rot["done"], c)
                nc.vector.tensor_tensor(rope["prod"][:], ps[:, 2 + c % 2, :], rope["sin"][:], ALU.mult).then_inc(rot["prod"], 1)
                nc.vector.tensor_tensor(pc, pc, rope["cos"][:], ALU.mult).then_inc(rot["prod_cos"], 1)
                dve.wait_ge(rot["prod_cos"], c + 1)
                dve.wait_ge(rot["prod"], c + 1)
                nc.vector.tensor_tensor(pc, pc, rope["prod"][:], ALU.add).then_inc(rot["done"], 1)
            for c in range(GC):
                dve.wait_ge(small["hi"], c + 1)
                nc.vector.tensor_tensor(mix["lo"][:, c, :], mix["proj"][:, 1 + c, :], mix["hi"][:, c, :].bitcast(F32),
                                        ALU.subtract).then_inc(mix_ready, 1)
            for c in range(GC):
                dve.wait_ge(small["hi"], GC + c + 1)
                nc.vector.scalar_tensor_tensor(out=mix["lo"][:, GC + c, :], in0=ps[:, c, :], scalar=column("pool_scale", c),
                                               in1=mix["hi"][:, GC + c, :].bitcast(F32), op0=ALU.mult,
                                               op1=ALU.subtract).then_inc(mix_ready, 1)
            split(u0 + 21)
            dve.wait_ge(used, u0 + 21)
            for b in range(TB):
                nc.vector.tensor_scalar(mix["v"][:, b, :], ps[:, 4 + b, :], r_rows[:, b:b + 1], None,
                                        ALU.mult).then_inc(w_in["v_ready"], 1)
            split(u0 + 22)

            def softmax_turn(n_items, least, probs, lo, outputs):
                for m in range(n_items + 4):
                    if m < n_items:
                        least(m)
                    if 0 <= m - 1 < n_items:
                        probs(m - 1)
                    if 0 <= m - 2 < n_items:
                        lo(m - 2)
                    outputs(m - 4)

            dve.wait_ge(rot["done"], 4)
            dve.wait_ge(w_in["v_ready"], TB)

            def stage_part(g, n_split, name, src, scale):
                dve.wait_ge(a1["staged_hi"], n_split)
                hi, lo = (at1[f"{name}{half}{g % 2}"].rearrange("p (a n) -> p a n", a=src.shape[1]) for half in ("hi", "lo"))
                if scale is None:
                    return nc.vector.tensor_tensor(lo, src, hi.bitcast(F32), ALU.subtract)
                return nc.vector.scalar_tensor_tensor(out=lo, in0=src, scalar=scale, in1=hi.bitcast(F32), op0=ALU.mult,
                                                      op1=ALU.subtract)

            def stage_qk(g):
                s, c = g % 2, g // 2
                stage_part(g, 3 * g + 1, "q", mix["proj"][:, 9 + 4 * s + c:10 + 4 * s + c, :], -HD ** -0.5)
                stage_part(g, 3 * g + 2, "k", mix["proj"][:, 11 + 4 * s + c:12 + 4 * s + c, :], None).then_inc(a1["staged"], 1)

            def stage_v(g):
                s, c = g % 2, g // 2
                stage_part(g, 3 * g + 3, "v", mix["v"][:, :, G * s + c * P:G * s + (c + 1) * P], None).then_inc(a1["v_staged"], 1)

            def least(t):
                b = t % 8 // 2
                w = P * (b + 1)
                if t >= 3:
                    dve.wait_ge(a1["turned"], t - 2)
                if t // 8 % 2:
                    dve.wait_ge(a1["bias"], t // 16 * 8 + t % 8 + 1)
                    bias = mix["proj"][:, 5 + t % 2, 0:w]
                else:
                    dve.wait_ge(loads["tables"], 16 * N_TABLES)
                    bias = mix["dil"][:, S - P - b * P:S - P - b * P + w]
                dve.wait_ge(a1["scores"], t + 1)
                nc.vector.tensor_tensor_reduce(at1["e"][:, t % 3, 0:w], ps[:, t % 2, 0:w], bias, 1.0, FAR, ALU.add,
                                               ALU.min, at1["least"][:, t % 3:t % 3 + 1]).then_inc(a1["least"], 1)

            def probs(t):
                w = P * (t % 8 // 2 + 1)
                k = t % 3
                dve.wait_ge(a1["exps"], t + 1)
                nc.vector.reciprocal(at1["inv"][:, k:k + 1], at1["sums"][:, k:k + 1]).then_inc(a1["inv"], 1)
                dve.wait_ge(a1["inv"], t + 1)
                nc.vector.tensor_scalar(at1["e"][:, k, 0:w], at1["e"][:, k, 0:w], at1["inv"][:, k:k + 1], None,
                                        ALU.mult).then_inc(a1["probs"], 1)

            def lo(t):
                w = P * (t % 8 // 2 + 1)
                dve.wait_ge(a1["pt_hi"], t + 1)
                nc.vector.tensor_tensor(at1["pt_lo"][:, t % 2, 0:w], ps[:, 2 + t % 2, 0:w],
                                        at1["pt_hi"][:, t % 2, 0:w].bitcast(F32), ALU.subtract).then_inc(a1["pt"], 1)

            def output(g):
                dve.wait_ge(a1["out_hi"], 2 * g + 2)
                for h in range(2):
                    rows = slice(HD * h, HD * h + HD)
                    ins = nc.vector.tensor_tensor(mix["lo"][rows, 4 + g, :], ps[rows, 4 + h, :], mix["hi"][rows, 4 + g, :].bitcast(F32),
                                                  ALU.subtract)
                ins.then_inc(mix_ready, 1)

            def memory_in(c):
                dve.wait_ge(mem["hi"], c + 1)
                nc.vector.scalar_tensor_tensor(out=mem_split(xg_lo, c), in0=mem_input(c), scalar=column("g_mem", c),
                                               in1=mem_split(xg_hi, c).bitcast(F32), op0=ALU.mult,
                                               op1=ALU.subtract).then_inc(mem["lo"], 1)

            def memory_out(t):
                if t == 2:
                    dve.wait_ge(mem["rms"], 2)
                    nc.vector.reciprocal(memory["r_cols"][:], memory["rms"][:]).then_inc(mem["r"], 1)
                    nc.vector.reciprocal(memory["r_rows"][:], memory["rms_rows"][:]).then_inc(mem["r"], 1)
                    dve.wait_ge(mem["r"], 2)
                m = t // 2 - 1
                if t % 2 == 0 and 0 <= m < KC:
                    dve.wait_ge(used, FIRST["mem_k"] + m + 1)
                    scaled(xa["k"][:, m, :], 6 + m % 2, mem["k_ready"], M, memory["r_cols"][:])
                if t % 2 == 0 and 0 <= m < 2 * KC:
                    split(FIRST["mem_k"] + m + 2)

            stage_qk(0)
            stage_v(0)
            for t in range(MIX_ITEMS + 6):
                if t % 8 == 5 and t > 8:
                    output(t // 8 - 1)
                if t < MIX_ITEMS:
                    least(t)
                if 0 <= t - 2 < MIX_ITEMS:
                    probs(t - 2)
                if 0 <= t - 4 < MIX_ITEMS:
                    lo(t - 4)
                g = t // 8 + 1
                if t % 8 == 1 and g < 2 * GC:
                    stage_qk(g)
                if t % 8 == 6 and g < 2 * GC:
                    stage_v(g)
                if t < KC // 2:
                    memory_in(2 * t)
                    memory_in(2 * t + 1)
                memory_out(t - MEM_LAG)

            u0 = FIRST["w_out"]
            for u in range(u0 + 2, u0 + KC + 1):
                split(u)
            into_residual("w_out", KC, "xa", "g_xa", 0, False)
            norm_r("xa")
            u0 = FIRST["xq"]
            with dve.Fori(0, KC // 2) as i:
                for s in range(2):
                    dve.wait_ge(used, at(u0 + 1 + s, i, 2))
                    scaled(chunk(xa["q"], at(s, i, 2)), s, xqs["ready"])
                    split(u0 + 2 + s, i)
            def staging(a, buf, c, n_done, parts):
                for k, (name, src, scale) in enumerate(parts):
                    dve.wait_ge(a["staged_hi"], at(n_done + k + 1, c, 6))
                    n = src.shape[1]
                    hi = buf[name.replace("lo", "hi")][:].bitcast(F32).rearrange("p (a n) -> p a n", a=n)
                    lo = buf[name][:].rearrange("p (a n) -> p a n", a=n)
                    if scale is None:
                        ins = nc.vector.tensor_tensor(lo, src, hi, ALU.subtract)
                    else:
                        ins = nc.vector.scalar_tensor_tensor(out=lo, in0=src, scalar=scale, in1=hi, op0=ALU.mult,
                                                             op1=ALU.subtract)
                ins.then_inc(a["staged"], 1)

            dve.wait_ge(xqs["ready"], KC)
            with dve.Fori(0, XA_HEADS // 2) as c:
                for s in range(2):
                    staging(a2, at2, c, 3 * s,
                            ((f"qlo{s}", xa["q"][:, bass.ds(c * (2 * XC) + XC * s, XC), :], -(XC * P) ** -0.5),
                             (f"klo{s}", xa["k"][:, bass.ds(c * (2 * XC) + XC * s, XC), :], None),
                             (f"vlo{s}", xa["v"][:, :, bass.ds(c * (2 * XC * P) + XC * P * s, XC * P)], None)))

                def least(n):
                    dve.wait_ge(a2["scores"], at(n + 1, c, 8))
                    nc.vector.tensor_reduce(at2["least"][:, n % 3:n % 3 + 1], ps[:, n % 2, 0:M], AX.X, ALU.min).then_inc(a2["least"], 1)

                def probs(n):
                    k = n % 3
                    dve.wait_ge(a2["exps"], at(n + 1, c, 8))
                    nc.vector.reciprocal(at2["inv"][:, k:k + 1], at2["sums"][:, k:k + 1]).then_inc(a2["inv"], 1)
                    dve.wait_ge(a2["inv"], at(n + 1, c, 8))
                    nc.vector.tensor_scalar(at2["e"][:, k, :], at2["e"][:, k, :], at2["inv"][:, k:k + 1], None,
                                            ALU.mult).then_inc(a2["probs"], 1)

                def lo(n):
                    dve.wait_ge(a2["pt_hi"], at(n + 1, c, 8))
                    nc.vector.tensor_tensor(at2["pt_lo"][:, n % 2, :], ps[:, 2 + n % 2, 0:M],
                                            at2["pt_hi"][:, n % 2, :].bitcast(F32), ALU.subtract).then_inc(a2["pt"], 1)

                def outputs(n):
                    if n not in (TB - 1, 2 * TB - 1):
                        return
                    s = n // TB
                    for d in range(XC):
                        dve.wait_ge(a2["out_hi"], at(XC * s + d + 1, c, 2 * XC))
                        at_ = c * (2 * XC) + XC * s + d
                        nc.vector.tensor_tensor(chunk(xa["lo"], at_), ps[:, 4 + 2 * s + d, :],
                                                chunk(xa["hi"], at_).bitcast(F32), ALU.subtract).then_inc(a2["out"], 1)

                softmax_turn(8, least, probs, lo, outputs)
            into_residual("xo", KC, "ffn", "g_ffn", 0)

            st = ffn_stages["up"]
            nc.vector.memset(ffn["ua"][:, 0:2], 0.0).then_inc(st["zero"], 1)
            nc.vector.memset(ffn["ug"][:, 0:2], 0.0).then_inc(st["zero"], 1)
            norm_r("ffn")
            dve.wait_ge(st["zero"], 2)
            def conv_product(i, done):
                dve.wait_ge(st["gated"], at(done + 1, i, 1))
                nc.vector.tensor_tensor(ffn["h"][:], ffn["ta"][:], ffn["gate"][:], ALU.mult).then_inc(st["product"], 1)

            def conv_lo(i, done):
                dve.wait_ge(st["hid_hi"], at(done + 1, i, 1))
                nc.vector.tensor_tensor(chunk(ffn["lo"], at(done, i, 1)), ffn["h"][:],
                                        chunk(ffn["hi"], at(done, i, 1)).bitcast(F32), ALU.subtract).then_inc(st["hid"], 1)

            def conv_taps(i, s, src, to):
                dve.wait_ge(st["tapped"], at(s + 1, i, 2))
                dve.wait_ge(st["scaled"], at(s + 1, i, 2))
                for k in (1, 0):
                    nc.vector.scalar_tensor_tensor(out=to[:], in0=src[:, k:S + k],
                                                   scalar=column("w_ffconv", at(k * 2 * FC + s * FC, i, 1)),
                                                   in1=to[:], op0=ALU.mult, op1=ALU.add).then_inc(st["steps"], 1)
                    dve.wait_ge(st["steps"], at(2 * s + 2 - k, i, 4))

            def conv_turn(i, first):
                u = FIRST["up"]
                dve.wait_ge(used, at(u + 1, i, 2))
                scaled(ffn["ua"][:, 2:S + 2], 0, st["scaled"])
                split(u + 2, i)
                if not first:
                    conv_product(i, -1)
                dve.wait_ge(used, at(u + 2, i, 2))
                scaled(ffn["ug"][:, 2:S + 2], 1, st["scaled"])
                split(u + 3, i)
                conv_taps(i, 0, ffn["ua"], ffn["ta"])
                if not first:
                    conv_lo(i, -1)
                conv_taps(i, 1, ffn["ug"], ffn["tg"])

            conv_turn(None, True)
            with dve.Fori(1, FC) as i:
                conv_turn(i, False)
            conv_product(None, FC - 1)
            conv_lo(None, FC - 1)
            into_residual("down", FC, "first", "a_gain", 2)

            dve.wait_ge(loads["spatial"], 2 * 16)
            for g in range(N_SPATIAL):
                wg = sg["w"][:, g * P:(g + 1) * P]
                ins = nc.vector.tensor_tensor(wg, wg, con[:, CAT["keep"]:CAT["keep"] + P], ALU.mult)
            ins.then_inc(a_in["w"], 1)
            u0 = FIRST["a_v"]
            split(u0 + 2)
            split(u0 + 3)
            dve.wait_ge(rms_ready, NORM["first"] + 1)
            nc.vector.reciprocal(first["r"][:], square_sum[:]).then_inc(r_ready, 1)
            dve.wait_ge(rows_rms_ready, ROWS["first"] + 1)
            nc.vector.reciprocal(first["r_rows"][:], rms_rows[:]).then_inc(rows_ready, 1)
            dve.wait_ge(r_ready, NORM["first"] + 1)
            dve.wait_ge(rows_ready, ROWS["first"] + 1)
            dve.wait_ge(sums_ready, NORM["a"] + 1)
            dve.wait_ge(rows_sums_ready, ROWS["a"] + 1)
            for k, (src, to, to_rows) in enumerate(((ps[:, 0, :], first["sums"], first["sums_rows"]),
                                                    (first["sums"][:], first["sums"], first["sums_rows"]))):
                if k:
                    dve.wait_ge(a_in["first"], 2 * k)
                nc.vector.tensor_tensor(to[:], src, first["r"][:], ALU.mult).then_inc(a_in["first"], 1)
                nc.vector.tensor_tensor(to_rows[:], to_rows[:] if k else ps[:, 1, 0:TB], first["r_rows"][:],
                                        ALU.mult).then_inc(a_in["first"], 1)
            split(u0 + 4)
            dve.wait_ge(rms_ready, NORM["a"] + 1)
            nc.vector.reciprocal(first["sums"][:], first["sums"][:]).then_inc(a_in["first"], 1)
            dve.wait_ge(rows_rms_ready, ROWS["a"] + 1)
            nc.vector.reciprocal(first["sums_rows"][:], first["sums_rows"][:]).then_inc(a_in["first"], 1)
            dve.wait_ge(a_in["first"], 6)
            nc.vector.tensor_tensor(r_cols[:], first["sums"][:], first["r"][:], ALU.mult).then_inc(r_ready, 1)
            nc.vector.tensor_tensor(r_rows[:], first["sums_rows"][:], first["r_rows"][:], ALU.mult).then_inc(rows_ready, 1)
            dve.wait_ge(r_ready, NORM["a"] + 1)
            for u in range(u0 + 5, u0 + KC + 2):
                split(u)
            dve.wait_ge(a_in["v"], 2 * TB)
            nc.vector.tensor_tensor(sg["mean"][:], sg["v_sum"][:, :, 0], sg["v_sum"][:, :, 1], ALU.add).then_inc(a_in["steps"], 1)
            dve.wait_ge(a_in["steps"], 1)
            nc.vector.tensor_scalar(sg["mean"][:], sg["mean"][:], -1.0 / D, None, ALU.mult).then_inc(a_in["steps"], 1)
            u0 = FIRST["a_u"]

            def gate_panel(s, i):
                dve.wait_ge(used, at(u0 + 1 + s, i, 2))
                scaled(chunk(sg["u"], at(s, i, 2)), 2 + s, a_in["scaled"])
                split(u0 + 2 + s, i)

            gate_panel(0, None)
            dve.wait_ge(a_in["std"], 1)
            nc.vector.reciprocal(sg["r"][:], sg["std"][:]).then_inc(a_in["steps"], 1)
            gate_panel(1, None)
            dve.wait_ge(a_in["steps"], 3)
            for b in range(TB + 1):
                if b < TB:
                    nc.vector.tensor_scalar(sg["v"][:, b, :], sg["v"][:, b, :], sg["mean"][:, b:b + 1], sg["r"][:, b:b + 1], ALU.add,
                                            ALU.mult).then_inc(a_in["normed"], 1)
                if b:
                    dve.wait_ge(a_in["v_hi"], b)
                    nc.vector.tensor_tensor(sg["v_lo"][:, b - 1, :], sg["v"][:, b - 1, :], sg["v_hi"][:, b - 1, :].bitcast(F32),
                                            ALU.subtract).then_inc(a_in["v_lo"], 1)
            dve.wait_ge(a_in["w_hi"], 1)
            nc.vector.tensor_tensor(sg["w_lo"][:], sg["w"][:], sg["w_hi"][:].bitcast(F32), ALU.subtract).then_inc(a_in["w_lo"], 1)
            with dve.Fori(1, KC // 2) as i:
                for s in range(2):
                    gate_panel(s, i)
            dve.wait_ge(loads["spatial"], 2 * 16)
            dve.wait_ge(a_in["u"], KC)
            for g in range(N_SPATIAL + 1):
                if g < N_SPATIAL:
                    dve.wait_ge(a_in["z_done"], g + 1)
                    if g:
                        dve.wait_ge(a_in["product"], g)
                    nc.vector.scalar_tensor_tensor(
                        out=sg["z"][:].rearrange("p (b t) -> p b t", b=TB),
                        in0=ps[:, 4 + g % 2, :].rearrange("p (b t) -> p b t", b=TB), scalar=column("a_v_norm", g),
                        in1=sg["b"][:, g, :].unsqueeze(1).to_broadcast([P, TB, P]), op0=ALU.mult, op1=ALU.add).then_inc(a_in["z"], 1)
                    dve.wait_ge(a_in["z"], g + 1)
                    nc.vector.tensor_tensor(sg["u"][:, g, :], sg["u"][:, g, :], sg["z"][:], ALU.mult).then_inc(a_in["product"], 1)
                if g:
                    dve.wait_ge(a_in["hi"], g)
                    nc.vector.tensor_tensor(sg["lo"][:, g - 1, :], sg["u"][:, g - 1, :], sg["hi"][:, g - 1, :].bitcast(F32),
                                            ALU.subtract).then_inc(a_in["ready"], 1)
            for c in range(KC):
                nc.vector.scalar_tensor_tensor(out=x[:, c, :], in0=x[:, c, :], scalar=column("g_first", c), in1=first["r"][:],
                                               op0=ALU.mult, op1=ALU.mult).then_inc(x_ready, 1)
            dve.wait_ge(x_ready, KC * NORM["a"])
            into_residual("a_out", KC, "ffn0", "ffn_norm0", 0)

            def swiglu(name, norm, base):
                st = ffn_stages[name]
                norm_r(norm)
                u0 = FIRST[name]
                with dve.Fori(0, FC) as i:
                    for s, to in enumerate((ffn["tg"], ffn["ta"])):
                        dve.wait_ge(used, at(u0 + 1 + s, i, 2))
                        scaled(to[:], base + s, st["scaled"])
                        split(u0 + 2 + s, i)
                    dve.wait_ge(st["gated"], at(1, i, 1))
                    dve.wait_ge(st["scaled"], at(2, i, 2))
                    nc.vector.tensor_tensor(ffn["h"][:], ffn["ta"][:], ffn["gate"][:], ALU.mult).then_inc(st["product"], 1)
                    dve.wait_ge(st["hid_hi"], at(1, i, 1))
                    nc.vector.tensor_tensor(chunk(ffn["lo"], at(0, i, 1)), ffn["h"][:], chunk(ffn["hi"], at(0, i, 1)).bitcast(F32),
                                            ALU.subtract).then_inc(st["hid"], 1)

            swiglu("gu0", "ffn0", 0)
            into_residual("down0", FC, "kv", "kv_norm", 2)

            nc.vector.memset(da["zero"][:], 0.0).then_inc(kv["zero"], 1)
            u0 = FIRST["kv_v"]
            split(u0 + 2)
            norm_r("kv", True)
            for u in range(u0 + 1, u0 + KC):
                split(u + 2)
                for c in range(2 * (u - u0 - 4), 2 * (u - u0 - 4) + 2):
                    if c >= 0:
                        dve.wait_ge(kv["xb_hi"], c + 1)
                        nc.vector.scalar_tensor_tensor(out=da["xb_lo"][:, c, :], in0=x[:, c, :], scalar=column("b_norm", c),
                                                       in1=da["xb_hi"][:, c, :].bitcast(F32), op0=ALU.mult,
                                                       op1=ALU.subtract).then_inc(kv["xb"], 1)
            qk0 = FIRST["qk"]

            def panel_out(p, i, bank):
                dve.wait_ge(used, at(qk0 + p + 1, i, 4))
                if p >= 2:
                    dve.wait_ge(a3["staged"], at(p - 1, i, 4))
                if p % 2:
                    nc.vector.scalar_tensor_tensor(out=da["q"], in0=ps[:, bank, :], scalar=-HD ** -0.5, in1=r_cols[:],
                                                   op0=ALU.mult, op1=ALU.mult).then_inc(kv["qk"], 1)
                else:
                    scaled(da["k"], bank, kv["qk"])

            for p in range(4):
                panel_out(p, None, 2 + p)
                split(qk0 + p + 2)
            dve.wait_ge(lams["done"], 1)

            def diff_item(n, c, base):
                def least(n):
                    s, b = n // TB, n % TB
                    w = P * (b + 1)
                    if c is not None or n + base >= DIFF_SLOTS:
                        dve.wait_ge(a3["turned"], at(base + n + 1 - DIFF_SLOTS, c, 8))
                    if b == 0:
                        dve.wait_ge(a3["bias"], at(base // TB + s + 1, c, 2))
                    for h in range(2):
                        k = 2 * (n % DIFF_SLOTS) + h
                        half = dve.to_reg(at(2 * (base + n) + h + 1, c, 16))
                        dve.wait_ge(loads["alibi"], 16)
                        dve.wait_ge(a3["scores"], half)
                        nc.vector.tensor_tensor_reduce(at3["e"][:, k, 0:w], ps[:, 2 * (n % 2) + h, 0:w],
                                                       da["bias"][:, s % 2, S - P - b * P:S - P - b * P + w], 1.0, FAR,
                                                       ALU.add, ALU.min, at3["least"][:, k:k + 1]).then_inc(a3["least"], 1)

                def inverse(n):
                    k = 2 * (n % DIFF_SLOTS)
                    dve.wait_ge(a3["exps"], at(2 * (base + n) + 2, c, 16))
                    nc.vector.reciprocal(at3["inv"][:, k:k + 2], at3["sums"][:, k:k + 2]).then_inc(a3["inv"], 1)
                    dve.wait_ge(a3["inv"], at(base + n + 1, c, 8))
                    nc.vector.tensor_scalar(at3["second"][:, k + 1:k + 2], at3["inv"][:, k + 1:k + 2], lam[:, 0:1], None,
                                            ALU.mult).then_inc(a3["second"], 1)

                def probs(n):
                    w = P * (n % TB + 1)
                    k = 2 * (n % DIFF_SLOTS)
                    dve.wait_ge(a3["weighed"], at(base + n + 1, c, 8))
                    nc.vector.scalar_tensor_tensor(out=at3["e"][:, k, 0:w], in0=at3["e"][:, k, 0:w],
                                                   scalar=at3["inv"][:, k:k + 1], in1=at3["e"][:, k + 1, 0:w], op0=ALU.mult,
                                                   op1=ALU.subtract).then_inc(a3["probs"], 1)

                def lo(n):
                    w = P * (n % TB + 1)
                    dve.wait_ge(a3["pt_hi"], at(base + n + 1, c, 8))
                    nc.vector.tensor_tensor(at3["pt_lo"][:, n % 2, 0:w], ps[:, 4 + n % 2, 0:w],
                                            at3["pt_hi"][:, n % 2, 0:w].bitcast(F32), ALU.subtract).then_inc(a3["pt"], 1)

                if qk_due(n, c, base):
                    panel_out(3 + (base + n) // 2, c, 7)
                if live(n, c, base):
                    least(n)
                if live(n - 2, c, base):
                    inverse(n - 2)
                if live(n - 3, c, base):
                    probs(n - 3)
                if live(n - 5, c, base):
                    lo(n - 5)
                if qk_due(n, c, base):
                    u = qk0 + 3 + (base + n) // 2 + 2
                    dve.wait_ge(w_hi_ready, at(u + 1, c, 4))
                    nc.vector.tensor_tensor(w_lo[:, u % 2, :], w_raw[:, u % 2, :], w_hi[:, u % 2, :].bitcast(F32),
                                            ALU.subtract).then_inc(w_ready, 1)

            diff_turns(dve, diff_item, 5)
            dve.wait_ge(a3["rms"], 1)
            nc.vector.reciprocal(da["rms"], da["rms"]).then_inc(a3["rms"], 1)
            for h in range(N_DIFF + 1):
                if h < N_DIFF:
                    dve.wait_ge(a3["spread"], h + 1)
                    nc.vector.scalar_tensor_tensor(out=da["o"][:, h, :], in0=da["o"][:, h, :], scalar=subln[:, 0:1],
                                                   in1=ps[:, h % 4, :], op0=ALU.mult, op1=ALU.mult).then_inc(a3["normed"], 1)
                if h:
                    dve.wait_ge(a3["out_hi"], h)
                    nc.vector.tensor_tensor(xg_lo[:, h - 1, :], da["o"][:, h - 1, :], xg_hi[:, h - 1, :].bitcast(F32),
                                            ALU.subtract).then_inc(a3["out_lo"], 1)
            into_residual("bo", KC, "ffn1", "ffn_norm1", 4)
            swiglu("gu1", "ffn1", 4)
            into_residual("down1", FC, "final", None, 6)
            norm_r("final")
            for c in range(KC):
                nc.vector.scalar_tensor_tensor(out=result[:, c, :], in0=x[:, c, :], scalar=column("g_final", c), in1=r_cols[:],
                                               op0=ALU.mult, op1=ALU.mult).then_inc(finals["scaled"], 1)

        @block.gpsimd
        def _(pool):
            def sum_squares(norm, sums=square_sum):
                n = NORM[norm]
                for c in range(KC):
                    k = KC * n + c
                    pool.wait_ge(sq_ready, k + 1)
                    if c == 0:
                        nc.gpsimd.tensor_copy(sums[:], squares[:, 0, :]).then_inc(summed, 1)
                    else:
                        pool.wait_ge(summed, k)
                        nc.gpsimd.tensor_tensor(sums[:], sums[:], squares[:, c % 2, :], ALU.add).then_inc(summed, 1)

            pool.dma_start(rope["pos"][:], positions).then_inc(loads["early"], 16)
            pool.dma_start(lam_in[:], lambdas).then_inc(loads["early"], 16)
            pool.dma_start(rope["pool_w"][:], pool_blocks).then_inc(loads["tables"], 16)
            pool.dma_start(rope["heads"][:], head_rows).then_inc(loads["tables"], 16)
            pool.dma_start(mix["dil"][:], dil_table).then_inc(loads["tables"], 16)
            sum_squares("mix")

            counted = [0]

            def step(ins):
                counted[0] += 1
                ins.then_inc(small["steps"], 1)
                pool.wait_ge(small["steps"], counted[0])

            step(nc.gpsimd.memset(rope["pad"][:, 0:16], 0.0))
            u = rope["pad"]
            for c in range(GC):
                pool.wait_ge(w_in["evacuated"], 4 + 3 * c)
                h_, b_, c_ = (mix["proj"][:, 1 + 3 * c + k, :] for k in range(3))
                step(nc.gpsimd.tensor_tensor(u[:, 16:], c_, h_, ALU.mult))
                step(nc.gpsimd.tensor_scalar(rope["win"][:, 0:S], u[:, 16:], column("w_sconv", 2 * GC + c), None, ALU.mult))
                for k in (1, 0):
                    step(nc.gpsimd.tensor_scalar(rope["win2"][:, 0:S], u[:, 14 + k:14 + k + S], column("w_sconv", k * GC + c),
                                                 None, ALU.mult))
                    step(nc.gpsimd.tensor_tensor(rope["win"][:, 0:S], rope["win"][:, 0:S], rope["win2"][:, 0:S], ALU.add))
                counted[0] += 1
                nc.gpsimd.tensor_tensor(mix["proj"][:, 1 + c, :], b_, rope["win"][:, 0:S], ALU.mult).then_inc(small["steps"], 1)
                pool.wait_ge(small["steps"], counted[0])
                pool.sem_inc(small["conv"], 1)
            for c in range(GC):
                pool.wait_ge(w_in["evacuated"], 8 + c)
                s1, s2 = rope["win"], rope["win2"]
                step(nc.gpsimd.tensor_copy(u[:, 16:], mix["proj"][:, 7 + c, :]))
                step(nc.gpsimd.tensor_tensor(s1[:, 1:], u[:, 1:], u[:, 0:S + 15], ALU.add))
                step(nc.gpsimd.tensor_tensor(s2[:, 3:], s1[:, 3:], s1[:, 1:S + 14], ALU.add))
                if c:
                    step(nc.gpsimd.tensor_tensor(s1[:, 7:], s2[:, 7:], s2[:, 3:S + 12], ALU.add))
                    step(nc.gpsimd.tensor_tensor(s2[:, 15:], s1[:, 15:], s1[:, 7:S + 8], ALU.add))
                for h, t in enumerate((s1, s2)):
                    rows = slice(HD * h, HD * h + HD)
                    step(nc.gpsimd.tensor_scalar(rope["z"][rows, c, :], t[rows, 16:], column("inv_window", c, rows), None, ALU.mult))
                    step(nc.gpsimd.tensor_tensor(rope["z"][rows, c, 0:16], t[rows, 16:32],
                                                 con[rows, CAT["inv_count"] + 16 * c:CAT["inv_count"] + 16 * c + 16], ALU.mult))
                counted[0] += 1
                nc.gpsimd.tensor_tensor(rope["z"][:, c, :], rope["z"][:, c, :], u[:, 16:], ALU.subtract).then_inc(small["steps"], 1)
                pool.wait_ge(small["steps"], counted[0])
                pool.sem_inc(small["pooled"], 1)

            for c in range(KC):
                pool.wait_ge(mem["sq"], c + 1)
                if c == 0:
                    nc.gpsimd.tensor_copy(memory["acc"][:], memory["sq"][:, 0, :]).then_inc(mem["summed"], 1)
                else:
                    pool.wait_ge(mem["summed"], c)
                    nc.gpsimd.tensor_tensor(memory["acc"][:], memory["acc"][:], memory["sq"][:, c % 2, :], ALU.add).then_inc(mem["summed"], 1)
            pool.wait_ge(gate["rows"], 1 + N_FORGET)
            with pool.Fori(0, GC) as c:
                for m in range(8):
                    b, h = m // 2, m % 2
                    w = P * (b + 1)
                    pool.wait_ge(a1["least"], at(8 + m - 1 if m >= 2 else 1, c, 16))
                    to = mix["proj"][:, 5 + m % 2, 0:w]
                    nc.gpsimd.tensor_tensor(to, mix["proj"][:, bass.ds(1 + h + c * 2, 1), 0:w].rearrange("p a n -> p (a n)"),
                                            mix["nci"][:, b, bass.ds(h + c * 2, 1)].to_broadcast([P, w]), ALU.add).then_inc(a1["bias_steps"], 1)
                    pool.wait_ge(a1["bias_steps"], at(m + 1, c, 8))
                    to = mix["proj"][:, 5 + m % 2, w - P:w]
                    nc.gpsimd.tensor_tensor(to, to, causal, ALU.add).then_inc(a1["bias"], 1)

            sum_squares("xa")
            for norm in ("ffn", "first", "ffn0", "kv"):
                sum_squares(norm)
                if norm == "first":
                    sum_squares("a", first["sums"])
            pool.wait_ge(loads["alibi"], 16)
            pool.wait_ge(kv["zero"], 1)
            pool.wait_ge(kv["v"], 8)

            def parts_of(set_, n_split, c, *parts):
                for k, (name, src) in enumerate(parts):
                    n = src.shape[1]
                    hi, lo = (at3[f"{name}{half}{set_}"][:].rearrange("p (a n) -> p a n", a=n) for half in ("hi", "lo"))
                    nc.gpsimd.tensor_tensor(hi, src, da["zero"][:].unsqueeze(2).to_broadcast(src.shape),
                                            ALU.add).then_inc(a3["staged_hi"], 1)
                    split_ = pool.to_reg(at(n_split + k + 1, c, 6))
                    pool.wait_ge(kv["zero"], 1)
                    pool.wait_ge(a3["staged_hi"], split_)
                    ins = nc.gpsimd.tensor_tensor(lo, src, hi.bitcast(F32), ALU.subtract)
                return ins

            def stage_qk(s, c):
                first_pair = c is None
                if not first_pair:
                    pool.wait_ge(a3["scores"], at(8 * (s - 1), c, 16))
                for k, name in enumerate(("k", "q")):
                    pool.wait_ge(kv["qk"], at(2 * s + k + 1, c, 4))
                    parts_of(s, (2 * s if first_pair else 3 * s - 1) + k, c,
                             (name, da[name].unsqueeze(1))).then_inc(a3["staged"], 1)
                if not first_pair:
                    pool.wait_ge(a3["least"], at(8 * (s - 1), c, 16))
                nc.gpsimd.tensor_tensor(da["bias"][:, s, :], da["alibi"][:], column("slopes", at(s, c, 2)).to_broadcast([P, BAND]),
                                        ALU.mult).then_inc(a3["bias"], 1)

            def stage_v(s, c, base, n_split):
                if c is not None or base + s >= 2:
                    pool.wait_ge(a3["pv"], at(TB * (base + s - 1) + (s < 0), c, 2 * TB))
                cols = bass.ds(at((base + s) * P, c, 2 * P), P)
                parts_of(s % 2, n_split, c, ("v", da["v"][:, :, cols])).then_inc(a3["v_staged"], 1)

            stage_qk(0, None)
            stage_qk(1, None)
            stage_v(0, None, 0, 4)
            with pool.Fori(1, N_DIFF // 2) as c:
                for s in range(2):
                    stage_qk(s, c)
                    stage_v(s - 1, c, 0, 3 * s + 1)
            stage_v(1, None, N_DIFF - 2, 3 * N_DIFF - 1)
            sum_squares("ffn1")
            sum_squares("final")

    return nc


def _tiles(w):
    k, n = w.shape
    return w.reshape(k // P, P, n // P, P).transpose(2, 1, 0, 3).reshape(n // P, P, -1)


def _rows(w, per_unit):
    k, n = w.shape
    return w.reshape(k // P // per_unit, per_unit, P, n).transpose(0, 2, 1, 3).reshape(-1, P, per_unit * n)


def _halves(w):
    return [_rows(w[:, h * S:(h + 1) * S], 2) for h in range(w.shape[1] // S)]


def _chunks(a):
    t, n = a.shape
    return a.T.reshape(n // P, P, t).transpose(1, 0, 2)


def _pairs(a, b):
    return np.stack([_tiles(a), _tiles(b)], 1).reshape(-1, P, a.shape[0])


def _columns(v):
    return v.reshape(-1, P).T


def _constants():
    con = np.zeros((P, N_CONSTS), np.float32)
    eye = np.eye(P, dtype=np.float32)
    con[:, CAT["ident"]:CAT["ident"] + P] = eye
    con[:, CAT["ones"]:CAT["ones"] + P] = 1.0
    perm = np.zeros((P, P), np.float32)
    half = ROPE_DIM // 2
    for h in range(P // HD):
        for f in range(half):
            perm[h * HD + f + half, h * HD + f] = -1.0
            perm[h * HD + f, h * HD + f + half] = 1.0
    con[:, CAT["rope_perm"]:CAT["rope_perm"] + P] = perm
    p, j = np.arange(P)[:, None], np.arange(P)[None, :]
    con[:, CAT["causal"]:CAT["causal"] + P] = np.where(j <= p, 0.0, MASKED)
    con[:, CAT["keep"]:CAT["keep"] + P] = p <= j
    for c in range(GC):
        for h in range(2):
            w = POOL_WINDOWS[2 * c + h]
            con[HD * h:HD * h + HD, CAT["inv_count"] + 16 * c:CAT["inv_count"] + 16 * c + 16] = \
                np.float32(1.0) / np.minimum(np.arange(16) + 1, w).astype(np.float32)
    con[:, CAT["pick"] + N_DIFF - 1] = 1.0
    dist = p + (S - P) - np.arange(BAND)[None, :]
    count = sum(((dist % d == 0) & (dist <= w)).astype(np.float64) for w, d in DILATED)
    count = np.where(dist >= 0, count, 0.0)
    dil = np.where(count > 0, -np.log(np.maximum(count, 1.0)), MASKED).astype(np.float32)
    alibi = np.where(dist >= 0, dist, MASKED).astype(np.float32)
    heads = np.zeros((P, N_FORGET, P), np.float32)
    for h in range(N_FORGET):
        heads[h, h, :] = 1.0
    picks = np.zeros((N_DIFF, N_DIFF, P), np.float32)
    for h in range(N_DIFF):
        picks[h, h, :] = 1.0
    return con, dil, alibi, heads.reshape(P, -1), picks.reshape(N_DIFF, -1)


def _lay_out(i):
    a = {n: np.asarray(v) for n, v in i.items()}
    w_in = a["w_in"][0]
    g3 = 3 * G
    gate0 = 9 * G
    gate = np.zeros((D, P), np.float32)
    gate[:, :N_FORGET] = w_in[:, gate0:gate0 + N_FORGET]
    conv = [w_in[:, k * G + c * P:k * G + (c + 1) * P] for c in range(GC) for k in range(3)]
    qk = [w_in[:, g3:g3 + 2 * G], w_in[:, 2 * g3:2 * g3 + 2 * G]]
    panels = np.concatenate([gate] + conv + [w_in[:, gate0 + N_FORGET:]] + qk, 1)
    values = np.concatenate([w_in[:, g3 + 2 * G:2 * g3], w_in[:, 2 * g3 + 2 * G:3 * g3]], 1)
    order = [0, 1, 6, 7, 2, 4, 3, 5]
    w_out = a["w_out"][0].reshape(KC, P, D)[order].reshape(D, D)
    up, xkv, kv, a_in = a["w_up"][0], a["w_xkv"][0], a["kv_w_2"], a["a_w_in_2"][0]
    gu, dn = a["ffn_w_gu_2"], a["ffn_w_down_2"]
    stream = [_tiles(panels), *_halves(values), _tiles(xkv[:, :D]), *_halves(xkv[:, D:]), _rows(w_out, 1),
              _tiles(a["w_xq"][0]), _rows(a["w_xo"][0], 1), _pairs(up[:, :FF], up[:, FF:]), _rows(a["w_down"][0], 1),
              *_halves(a_in[:, D:]), _tiles(a_in[:, :D]), _rows(a["a_w_out_2"][0], 1),
              _pairs(gu[0][:, :FF], gu[0][:, FF:]), _rows(dn[0], 1),
              *_halves(kv[:, D:]), _pairs(kv[:, :D], a["b_w_q_2"][0]), _rows(a["b_w_o_2"][0], 1),
              _pairs(gu[1][:, :FF], gu[1][:, FF:]), _rows(dn[1], 1)]
    weights = np.concatenate(stream, 0)
    par = np.zeros((P, N_PARAMS), np.float32)

    def put(name, cols):
        par[:cols.shape[0], AT[name]:AT[name] + cols.shape[1]] = cols

    for name, v in (("g_mix", a["g_mix"]), ("g_xa", a["g_xa"]), ("g_mem", a["g_mem"]), ("g_ffn", a["g_ffn"]),
                    ("a_norm", a["a_norm_2"]), ("ffn_norm0", a["ffn_norm_2"][0]), ("kv_norm", a["kv_norm_2"]),
                    ("b_norm", a["b_norm_2"]), ("ffn_norm1", a["ffn_norm_2"][1]), ("g_first", a["g_final"]), ("g_final", a["final_norm_2"]),
                    ("a_v_norm", a["a_v_norm_2"]), ("w_sconv", a["w_sconv"][0]), ("pool_scale", a["pool_scale"]),
                    ("w_ffconv", a["w_ffconv"][0]), ("b_subln", a["b_subln_2"])):
        put(name, _columns(v))
    put("b_forget", a["b_forget"].reshape(N_FORGET, 1))
    par[:, AT["eps"]] = EPS
    half = ROPE_DIM // 2
    freq = np.float32(ROPE_THETA) ** (-np.arange(0, ROPE_DIM, 2, dtype=np.float32) / np.float32(ROPE_DIM))
    for h in range(P // HD):
        for k in range(2):
            par[h * HD + k * half:h * HD + (k + 1) * half, AT["inv_freq"]] = freq
        for c in range(GC):
            par[HD * h:HD * h + HD, AT["inv_window"] + c] = 1.0 / POOL_WINDOWS[2 * c + h]
    par[:, AT["slopes"]:AT["slopes"] + N_DIFF] = 2.0 ** (-8.0 * (np.arange(N_DIFF) + 1) / N_DIFF)
    con, dil, alibi, heads, picks = _constants()
    blocks = np.zeros((P, GC, P), np.float32)
    for c in range(GC):
        for h in range(2):
            blocks[HD * h:HD * h + HD, c, HD * h:HD * h + HD] = a["w_pool"][0][2 * c + h]
    return {
        "weights": weights, "x_cols": _chunks(a["x"][0]), "mem_cols": _chunks(a["mem"][0]),
        "positions": np.broadcast_to(a["positions"], (P, S)), "params": par, "consts": con,
        "dil_table": dil, "head_rows": heads, "alibi_table": alibi, "head_picks": picks, "pool_blocks": blocks,
        "spatial": a["a_w_sp_2"][0].transpose(2, 0, 1).reshape(P, -1),
        "spatial_bias": np.broadcast_to(a["a_b_sp_2"][0].reshape(1, -1), (P, N_SPATIAL * P)),
        "lambdas": np.broadcast_to(a["b_lambda_2"][0].reshape(1, -1), (P, 4 * HD)),
    }


def kernel(**inputs):
    import concourse.bacc as bacc
    from concourse.bass_utils import run_bass_kernel_spmd as run

    nc = bacc.Bacc("TRN2", target_bir_lowering=False, num_devices=1)
    arrays, args = {}, {}
    for name, a in _lay_out(inputs).items():
        a = np.ascontiguousarray(a)
        arrays[f"in_{name}"] = a
        args[name] = nc.dram_tensor(f"in_{name}", a.shape, mybir.dt.from_np(a.dtype), kind="ExternalInput").ap()
    out = nc.dram_tensor("out_cols", (P, KC, S), F32, kind="ExternalOutput").ap()
    bass_two_blocks(nc, out=out, **args)
    got = run(nc, [arrays], core_ids=[0]).results[0]["out_cols"]
    return np.ascontiguousarray(got.transpose(2, 1, 0)).reshape(1, S, D)
```

```python
import math
from contextlib import ExitStack

import numpy as np

import concourse.bass as bass
from concourse import mybir

F32 = mybir.dt.float32
F32R = mybir.dt.float32r
I32 = mybir.dt.int32
ALU = mybir.AluOpType
ACT = mybir.ActivationFunctionType
AX = mybir.AxisListType

P = 128
D = 1024
S = 512
KC = D // P
M = 256
MB = M // P
TB = S // P
HD = 64
FF = 2816
FC = FF // P
G = D // 4
GC = G // P
N_FORGET = G // HD
XA_HEADS = 4
XC = D // XA_HEADS // P
N_DIFF = 8
N_SPATIAL = 8
EPS = 1e-6
MASKED = 1e30
FAR = 3.0e38
ROPE_DIM = HD // 4
ROPE_THETA = 500000.0
DILATED = ((128, 1), (512, 4), (2048, 16))
POOL_WINDOWS = (2, 4, 8, 16)
LAMBDA_INIT = 0.8 - 0.6 * math.exp(-0.3)
MIX_ITEMS = 2 * GC * 2 * TB
EARLY_PANELS = 3
XA_ITEMS = XA_HEADS * TB
XQ_FIRST = 3
MEM_LAG = 4
DIFF_SLOTS = 4
BAND = S + S - P

UNITS = (("w_in", 2 * KC + 5), ("mem_k", KC), ("mem_v", KC), ("w_out", KC), ("xq", KC), ("xo", KC),
         ("up", 2 * FC), ("down", FC), ("a_v", KC), ("a_u", KC), ("a_out", KC), ("gu0", 2 * FC), ("down0", FC),
         ("kv_v", KC), ("qk", 2 * KC), ("bo", KC), ("gu1", 2 * FC), ("down1", FC))
FIRST = {}
N_UNITS = 0
for _name, _n in UNITS:
    FIRST[_name] = N_UNITS
    N_UNITS += _n

PARAMS = (("g_mix", KC), ("g_xa", KC), ("g_mem", KC), ("g_ffn", KC), ("a_norm", KC), ("ffn_norm0", KC),
          ("kv_norm", KC), ("b_norm", KC), ("ffn_norm1", KC), ("g_first", KC), ("a_gain", KC), ("g_final", KC), ("a_v_norm", KC),
          ("b_forget", 1), ("w_sconv", 3 * GC), ("pool_scale", GC), ("w_ffconv", 3 * 2 * FC), ("b_subln", 1),
          ("eps", 1), ("inv_freq", 1), ("inv_window", GC), ("slopes", N_DIFF))
AT = {}
N_PARAMS = 0
for _name, _n in PARAMS:
    AT[_name] = N_PARAMS
    N_PARAMS += _n

CONSTS = (("ident", P), ("ones", P), ("rope_perm", P), ("causal", P), ("keep", P), ("inv_count", GC * 16),
          ("pick", 2 * N_DIFF - 1))
CAT = {}
N_CONSTS = 0
for _name, _n in CONSTS:
    CAT[_name] = N_CONSTS
    N_CONSTS += _n

TWO_PI = 2.0 * math.pi
TURN_1 = 201.0 / 32.0
TURN_2 = round((TWO_PI - TURN_1) * 2.0 ** 17) / 2.0 ** 17
TURN_3 = round((TWO_PI - TURN_1 - TURN_2) * 2.0 ** 27) / 2.0 ** 27
TURN_4 = TWO_PI - TURN_1 - TURN_2 - TURN_3
ROUNDER = 1.5 * 2.0 ** 23
PI_BELOW = 3.1415925


def bass_two_blocks(nc, weights, x_cols, mem_cols, positions, params, consts, dil_table, head_rows, alibi_table, head_picks,
                    pool_blocks, spatial, spatial_bias, lambdas, out):
    ctx = ExitStack()

    def sem(name):
        return ctx.enter_context(nc.semaphore(name))

    def stage(name, *signals):
        return {s: sem(f"{name}_{s}") for s in signals}

    def at(const, i=None, per=0):
        return const if i is None else const + i * per

    def diff_turns(engine, step, depth):
        for n in range(8):
            step(n, None, 0)
        with engine.Fori(1, N_DIFF // 2 - 1) as c:
            for n in range(8):
                step(n, c, 0)
        for n in range(8 + depth):
            step(n, None, 4 * N_DIFF - 8)

    def live(n, c, base):
        return n < 8 and (n >= 0 or c is not None or base > 0)

    def qk_due(n, c, base):
        return n % 2 == 0 and (0 < n < 8 or c is not None or base > 0 and n == 0) and (base == 0 or n <= 2)

    with ctx:
        def sb(name, shape, dt=F32, where=ctx):
            return where.enter_context(nc.sbuf_tensor(name, shape, dt))

        x = sb("x", [P, KC, S])
        xg_hi = sb("xg_hi", [P, KC, S], F32R)
        xg_lo = sb("xg_lo", [P, KC, S], F32R)
        w_raw = sb("w_raw", [P, 2, D])
        w_hi = sb("w_hi", [P, 2, D], F32R)
        w_lo = sb("w_lo", [P, 2, D], F32R)
        par = sb("par", [P, N_PARAMS])
        con = sb("con", [P, N_CONSTS])
        r_cols = sb("r_cols", [P, S])
        r_rows = sb("r_rows", [P, TB])
        rms_rows = sb("rms_rows", [P, TB])
        squares = sb("squares", [P, 2, S])
        square_sum = sb("square_sum", [P, S])
        lam_in = sb("lam_in", [P, 4 * HD])
        lam_dot = sb("lam_dot", [P, 2])
        lam_exp = sb("lam_exp", [P, 2])
        lam = sb("lam", [P, 1])
        subln = sb("subln", [P, 1])

        s_ctx = ExitStack()
        mix = dict(hi=sb("mix_hi", [P, KC, S], F32R, s_ctx), lo=sb("mix_lo", [P, KC, S], F32R, s_ctx))
        kv_ctx = ExitStack()
        xa = dict(hi=mix["hi"], lo=mix["lo"], k=sb("xa_k", [P, KC, M], F32, kv_ctx), v=sb("xa_v", [P, MB, D], F32, kv_ctx))
        kv_ctx.close()
        rope = dict(
            pos=sb("pos", [P, S], I32, s_ctx), ang=sb("ang", [P, S], F32, s_ctx),
            turns=sb("turns", [P, S], F32, s_ctx), red=sb("red", [P, S], F32, s_ctx),
            cos=sb("cos", [P, S], F32, s_ctx), sin=sb("sin", [P, S], F32, s_ctx),
            prod=sb("rope_prod", [P, S], F32, s_ctx), heads=sb("heads", [P, N_FORGET * P], F32, s_ctx))
        m_ctx = ExitStack()
        mix.update(
            proj=sb("proj", [P, 17, S], F32, m_ctx), v=sb("mix_v", [P, TB, 2 * G], F32, m_ctx),
            dil=sb("dil", [P, BAND], F32, m_ctx),
            c_rows=sb("c_rows", [P, S], F32, m_ctx), nci=sb("nci", [P, TB, N_FORGET], F32, m_ctx))
        memory = dict(
            sq=sb("mem_sq", [P, 2, M], F32, m_ctx), acc=sb("mem_acc", [P, M], F32, m_ctx),
            rms=sb("mem_rms", [P, M], F32, m_ctx), rms_rows=sb("mem_rms_rows", [P, MB], F32, m_ctx),
            r_cols=sb("mem_r_cols", [P, M], F32, m_ctx), r_rows=sb("mem_r_rows", [P, MB], F32, m_ctx))
        m_top = ExitStack()
        rope.update(
            g1=sb("gate_a", [P, S], F32, m_top),
            g2=sb("gate_b", [P, S], F32, m_top),
            g3=sb("gate_c", [P, S], F32, m_top), g4=sb("gate_d", [P, S], F32, m_top),
            pad=sb("pad", [P, S + 16], F32, m_top), win=sb("win", [P, S + 16], F32, m_top),
            win2=sb("win2", [P, S + 16], F32, m_top), z=sb("pooled", [P, GC, S], F32, m_top),
            pool_w=sb("pool_w", [P, GC, P], F32, m_top))
        m_top.close()

        def attention_buffers(tag, where, q_cols, k_cols, v_cols, n_e, s_cols, turned):
            names = {}
            for set_ in range(2):
                for part, cols in (("q", q_cols), ("k", k_cols), ("v", v_cols)):
                    for half in ("hi", "lo"):
                        names[f"{part}{half}{set_}"] = sb(f"{tag}_{part}_{half}{set_}", [P, cols], F32R, where)
            names["pt_hi"] = sb(f"{tag}_pt_hi", [P, 2, turned], F32R, where)
            names["pt_lo"] = sb(f"{tag}_pt_lo", [P, 2, turned], F32R, where)
            names["e"] = sb(f"{tag}_e", [P, n_e, s_cols], F32, where)
            names["least"] = sb(f"{tag}_least", [P, n_e], F32, where)
            names["sums"] = sb(f"{tag}_sums", [P, n_e], F32, where)
            names["inv"] = sb(f"{tag}_inv", [P, n_e], F32, where)
            return names

        at1 = dict(e=sb("at1_e", [P, 3, S], F32, m_ctx), least=sb("at1_least", [P, 3], F32, m_ctx),
                   sums=sb("at1_sums", [P, 3], F32, m_ctx), inv=sb("at1_inv", [P, 3], F32, m_ctx),
                   pt_hi=xg_hi[:, 4:6, :], pt_lo=xg_lo[:, 4:6, :])
        for set_ in range(2):
            for part in ("qhi", "qlo", "khi", "klo"):
                at1[f"{part}{set_}"] = sb(f"at1_{part}{set_}", [P, S], F32R, m_ctx)
            at1[f"vhi{set_}"] = xg_hi[:, 6 + set_, :]
            at1[f"vlo{set_}"] = xg_lo[:, 6 + set_, :]
        m_ctx.close()

        def mem_split(to, c):
            return to[:, c // 2, c % 2 * M:(c % 2 + 1) * M]

        def mem_input(c):
            if c < 4:
                return squares[:, c // 2, c % 2 * M:(c % 2 + 1) * M]
            return (square_sum[:] if c < 6 else mix["proj"][:, 0, :])[:, c % 2 * M:(c % 2 + 1) * M]

        c_ctx = ExitStack()
        xa.update(q=sb("xa_q", [P, KC, S], F32, c_ctx))
        at2 = attention_buffers("at2", c_ctx, XC * S, XC * M, MB * XC * P, 3, M, MB * S)
        c_ctx.close()
        s_ctx.close()
        f_ctx = ExitStack()
        ffn = dict(
            hi=sb("hid_hi", [P, FC, S], F32R, f_ctx), lo=sb("hid_lo", [P, FC, S], F32R, f_ctx),
            ua=sb("up_a", [P, S + 2], F32, f_ctx), ug=sb("up_g", [P, S + 2], F32, f_ctx),
            ta=sb("conv_a", [P, S], F32, f_ctx), tg=sb("conv_g", [P, S], F32, f_ctx),
            gate=sb("gate", [P, S], F32, f_ctx), h=sb("hid", [P, S], F32, f_ctx))
        f_ctx.close()
        g_ctx = ExitStack()
        sg = dict(
            hi=sb("sg_hi", [P, KC, S], F32R, g_ctx), lo=sb("sg_lo", [P, KC, S], F32R, g_ctx),
            u=sb("sg_u", [P, KC, S], F32, g_ctx), v=sb("sg_v", [P, TB, D], F32, g_ctx),
            v_hi=sb("sg_v_hi", [P, TB, D], F32R, g_ctx), v_lo=sb("sg_v_lo", [P, TB, D], F32R, g_ctx),
            v_sum=sb("sg_v_sum", [P, TB, 2], F32, g_ctx), mean=sb("sg_mean", [P, TB], F32, g_ctx),
            v_sq=sb("sg_v_sq", [P, TB], F32, g_ctx), std=sb("sg_std", [P, TB], F32, g_ctx),
            r=sb("sg_r", [P, TB], F32, g_ctx), z=sb("sg_z", [P, S], F32, g_ctx),
            w=sb("sp_w", [P, N_SPATIAL * P], F32, g_ctx), w_hi=sb("sp_w_hi", [P, N_SPATIAL * P], F32R, g_ctx),
            w_lo=sb("sp_w_lo", [P, N_SPATIAL * P], F32R, g_ctx), b=sb("sp_b", [P, N_SPATIAL, P], F32, g_ctx))
        first = dict(
            r=sb("first_r", [P, S], F32, g_ctx), r_rows=sb("first_r_rows", [P, TB], F32, g_ctx),
            sums=sb("first_sums", [P, S], F32, g_ctx), sums_rows=sb("first_sums_rows", [P, TB], F32, g_ctx))
        g_ctx.close()
        d_ctx = ExitStack()
        da = dict(
            v=sb("da_v", [P, TB, D], F32, d_ctx), o=sb("da_o", [P, KC, S], F32, d_ctx),
            xb_hi=sb("xb_hi", [P, KC, S], F32R, d_ctx), xb_lo=sb("xb_lo", [P, KC, S], F32R, d_ctx),
            alibi=sb("alibi", [P, BAND], F32, d_ctx), bias=sb("da_bias", [P, 2, BAND], F32, d_ctx),
            zero=sb("da_zero", [P, 1], F32, d_ctx), k=squares[:, 0, :], q=squares[:, 1, :])
        at3 = attention_buffers("at3", d_ctx, S, S, S, 2 * DIFF_SLOTS, S, S)
        at3["second"] = sb("at3_second", [P, 2 * DIFF_SLOTS], F32, d_ctx)
        da["picks"] = at3["e"][0:N_DIFF, 0:N_DIFF * P // S, :].rearrange("p a n -> p (a n)")
        da["rms"] = at3["e"][0:N_DIFF, N_DIFF * P // S, :]
        d_ctx.close()
        o_ctx = ExitStack()
        result = sb("result", [P, KC, S], F32, o_ctx)
        o_ctx.close()

        ps = ctx.enter_context(nc.psum_tensor("ps", [P, 8, S], F32))

        ident = con[:, CAT["ident"]:CAT["ident"] + P]
        ones = con[:, CAT["ones"]:CAT["ones"] + P]
        causal = con[:, CAT["causal"]:CAT["causal"] + P]

        def column(name, c=0, rows=slice(0, P)):
            return par[rows, bass.ds(AT[name] + c, 1)]

        loads = stage("loaded", "input", "rest", "con", "early", "tables", "mem", "spatial", "alibi")
        N_EARLY, N_TABLES = 2, 3
        w_loaded = [sem("weights_loaded_0"), sem("weights_loaded_1")]
        w_hi_ready = sem("weights_hi_ready")
        w_ready = sem("weights_ready")
        used = sem("units_used")
        x_ready = sem("x_ready")
        xg_hi_ready = sem("xg_hi_ready")
        xg_ready = sem("xg_ready")
        sq_ready = sem("squares_ready")
        summed = sem("squares_summed")
        sums_ready = sem("square_sums_ready")
        rms_ready = sem("rms_ready")
        r_ready = sem("r_ready")
        rows_sums_ready = sem("row_square_sums_ready")
        rows_rms_ready = sem("row_rms_ready")
        rows_ready = sem("r_rows_ready")
        w_in = stage("w_in", "evacuated", "v_ready")
        gate = stage("gate", "steps", "abs", "exp", "c", "turned", "rows")
        rot = stage("rope", "steps", "trig", "swapped", "prod", "prod_cos", "done")
        small = stage("mixer", "steps", "conv", "pooled", "product", "hi")
        mix_ready = sem("mix_ready")
        a1 = stage("at1", "staged_hi", "staged", "v_staged", "scores", "least", "exps", "inv", "probs", "turned", "pt_hi", "pt",
                   "pv", "out_hi", "bias", "bias_steps")
        a2 = stage("at2", "staged_hi", "staged", "v_staged", "scores", "least", "exps", "inv", "probs", "turned", "pt_hi", "pt",
                   "pv", "out_hi", "out")
        a3 = stage("at3", "staged_hi", "staged", "v_staged", "scores", "least", "exps", "inv", "second", "weighed", "probs",
                   "turned", "pt_hi", "pt", "pv", "out", "bias", "sq", "summed", "rms", "spread", "normed", "out_hi",
                   "out_lo")
        lams = stage("lambda", "dots", "exps", "done")
        mem = stage("mem", "hi", "lo", "sq", "summed", "sums", "rms", "r", "k_ready", "v_ready")
        xqs = stage("xq", "ready")
        ffn_stages = {"up": stage("up", "scaled", "tapped", "steps", "gated", "product", "hid_hi", "hid", "zero"),
                      "gu0": stage("gu0", "scaled", "gated", "product", "hid_hi", "hid"),
                      "gu1": stage("gu1", "scaled", "gated", "product", "hid_hi", "hid")}
        a_in = stage("a_in", "scaled", "u", "v", "steps", "v_sq", "std", "normed", "v_hi", "v_lo",
                     "w", "w_hi", "w_lo", "first", "z_done", "z", "product", "hi", "ready")
        kv = stage("kv", "v", "qk", "xb_hi", "xb", "zero")
        proj_sums = sem("residual_sums")
        RESIDUALS = ("w_out", "xo", "down", "a_out", "down0", "bo", "down1")
        finals = stage("final", "pairs", "r_rows", "diagonal", "spread", "scaled", "stored")

        NORM = {"mix": 0, "xa": 1, "ffn": 2, "first": 3, "a": 4, "ffn0": 5, "kv": 6, "ffn1": 7, "final": 8}
        SPLIT = {"mix": 0, "xa": 1, "ffn": 2, "first": 3, "ffn0": 4, "kv": 5, "ffn1": 6}
        final = dict(squares=result, diagonal=square_sum[:])
        FINAL_BANKS = [(6 + b) % 8 for b in range(TB)]
        ROWS = {"mix": 0, "first": 1, "a": 2, "kv": 3}

        block = ctx.enter_context(nc.Block())

        @block.sync
        def _(sp):
            sp.dma_start(par[:], params).then_inc(loads["input"], 16)
            sp.dma_start(x[:, 0:KC // 2, :], x_cols[:, 0:KC // 2, :]).then_inc(loads["input"], 16)
            sp.dma_start(w_raw[:, 0, :], weights[0]).then_inc(w_loaded[0], 16)
            sp.dma_start(x[:, KC // 2:, :], x_cols[:, KC // 2:, :]).then_inc(loads["rest"], 16)
            sp.dma_start(w_raw[:, 1, :], weights[1]).then_inc(w_loaded[1], 16)
            with sp.Fori(1, N_UNITS // 2) as i:
                for s in range(2):
                    sp.wait_ge(w_ready, i * 2 + (s - 1))
                    sp.dma_start(w_raw[:, s, :], weights[bass.ds(i * 2 + s, 1), :, :].rearrange("u p n -> p (u n)")
                                 ).then_inc(w_loaded[s], 16)
            for u in range(N_UNITS // 2 * 2, N_UNITS):
                sp.wait_ge(w_ready, u - 1)
                sp.dma_start(w_raw[:, u % 2, :], weights[u]).then_inc(w_loaded[u % 2], 16)
            for c in range(KC):
                sp.wait_ge(finals["scaled"], c + 1)
                sp.dma_start(out[:, c, :], result[:, c, :]).then_inc(finals["stored"], 16)
            sp.wait_ge(finals["stored"], 16 * KC)

        @block.tensor
        def _(pe):
            def product(to, wh, wl, xh, xl, start, stop):
                nc.tensor.matmul(to, wh, xh, start=start, stop=False)
                nc.tensor.matmul(to, wh, xl, start=False, stop=False)
                return nc.tensor.matmul(to, wl, xh, start=False, stop=stop)

            def tile(s, k):
                return w_hi[:, s, k * P:(k + 1) * P], w_lo[:, s, k * P:(k + 1) * P]

            def panel(u, i, to, hi, lo, chunks_ready=None):
                pe.wait_ge(w_ready, at(u + 1, i, 2))
                for k in range(KC):
                    if chunks_ready is not None:
                        pe.wait_ge(xg_ready, chunks_ready + k + 1)
                    wh, wl = tile(u % 2, k)
                    mm = product(to, wh, wl, hi[:, k, :], lo[:, k, :], k == 0, k == KC - 1)
                mm.then_inc(used, 1)

            def square_sums(norm, bank, rows_bank=None, sums=square_sum):
                pe.wait_ge(summed, KC * (NORM[norm] + 1))
                nc.tensor.matmul(ps[:, bank, :], ones, sums[:], start=True, stop=True).then_inc(sums_ready, 1)
                if rows_bank is not None:
                    for b in range(TB):
                        mm = nc.tensor.matmul(ps[:, rows_bank, b:b + 1], sums[:, b * P:(b + 1) * P],
                                              ones[:, 0:1], start=True, stop=True)
                    mm.then_inc(rows_sums_ready, 1)

            def values(first, u, hi, lo, n_blocks, banks, per_unit):
                halves = 2 // per_unit
                pe.wait_ge(w_ready, u + 1)
                for kk in range(per_unit):
                    k = (u - first) * per_unit + kk
                    for b in range(n_blocks):
                        for h in range(halves):
                            cols = slice((kk * halves + h) * S, (kk * halves + h + 1) * S)
                            mm = product(ps[:, banks[b * halves + h], :],
                                         hi[:, k, b * P:(b + 1) * P], lo[:, k, b * P:(b + 1) * P],
                                         w_hi[:, u % 2, cols], w_lo[:, u % 2, cols], k == 0, k == KC - 1)
                mm.then_inc(used, 1)

            def into_residual(name, n, bank0, hi, lo, ready, chunk_ready, bank_free):
                u0 = FIRST[name]

                def unit(k, i, first, final):
                    u = u0 + k
                    pe.wait_ge(w_ready, at(u + 1, i, 2))
                    pe.wait_ge(ready, at(chunk_ready(k), i, 2))
                    kk = at(k, i, 2)
                    for j in range(KC):
                        if first and j in bank_free:
                            pe.wait_ge(*bank_free[j])
                        wh, wl = tile(u % 2, j)
                        mm = product(ps[:, (bank0 + j) % 8, :], wh, wl, hi[:, kk, :], lo[:, kk, :], first, final)
                        if final and j < KC - 1:
                            mm.then_inc(proj_sums, 1)
                    mm.then_inc(used, 1)

                unit(0, None, True, False)
                unit(1, None, False, False)
                if n > 4:
                    with pe.Fori(0, n // 2 - 2) as i:
                        unit(2, i, False, False)
                        unit(3, i, False, False)
                unit(n - 2, None, False, False)
                unit(n - 1, None, False, True)

            def hidden(name, norm, st, base):
                u0 = FIRST[name]
                panel(u0, None, ps[:, base, :], xg_hi, xg_lo, KC * SPLIT[norm])
                square_sums(norm, (base + 2) % 8)
                panel(u0 + 1, None, ps[:, base + 1, :], xg_hi, xg_lo)
                with pe.Fori(0, FC - 1) as i:
                    for s in range(2):
                        pe.wait_ge(st["scaled"], at(s + 1, i, 2))
                        panel(u0 + 2 + s, i, ps[:, base + s, :], xg_hi, xg_lo)

            u0 = FIRST["w_in"]
            pe.wait_ge(loads["con"], 16)
            panel(u0, None, ps[:, 0, :], xg_hi, xg_lo, 0)
            square_sums("mix", 2, 3)
            panel(u0 + 1, None, ps[:, 1, :], xg_hi, xg_lo)
            with pe.Fori(0, 7) as i:
                for s in range(2):
                    pe.wait_ge(w_in["evacuated"], at(s + 1, i, 2))
                    panel(u0 + 2 + s, i, ps[:, s, :], xg_hi, xg_lo)
            pe.wait_ge(w_in["evacuated"], 15)
            panel(u0 + 16, None, ps[:, 0, :], xg_hi, xg_lo)
            pe.wait_ge(r_ready, 1)
            pe.wait_ge(rows_ready, 1)
            for u in range(u0 + 17, u0 + 21):
                values(u0 + 17, u, xg_hi, xg_lo, TB, (4, 5, 6, 7), 2)
                for c in {u0 + 17: (0, 1), u0 + 18: (2, 3)}.get(u, ()):
                    pe.wait_ge(w_in["evacuated"], 10 + c)
                    if c >= 2:
                        pe.wait_ge(rot["prod"], c - 1)
                    nc.tensor.matmul(ps[:, 2 + c % 2, :], con[:, CAT["rope_perm"]:CAT["rope_perm"] + P],
                                     mix["proj"][:, 9 + c, :], start=True, stop=True).then_inc(rot["swapped"], 1)
                if u == u0 + 18:
                    pe.wait_ge(loads["tables"], 16 * N_TABLES)
                    pe.wait_ge(w_in["evacuated"], 17)
                    for c in range(GC):
                        pe.wait_ge(small["pooled"], c + 1)
                        nc.tensor.matmul(ps[:, c, :], rope["pool_w"][:, c, :], rope["z"][:, c, :],
                                         start=True, stop=True).then_inc(small["product"], 1)
            pe.wait_ge(gate["c"], 1)
            pe.wait_ge(rot["prod"], 4)
            for b in range(TB):
                mm = nc.tensor.matmul(ps[:, 2, b * N_FORGET:(b + 1) * N_FORGET], mix["c_rows"][0:N_FORGET, b * P:(b + 1) * P],
                                      ident[0:N_FORGET, 0:N_FORGET], start=True, stop=True)
            mm.then_inc(gate["turned"], 1)
            pe.wait_ge(mix_ready, 4)
            pe.wait_ge(w_in["v_ready"], TB)

            def gate_rows(h):
                if h == 2:
                    pe.wait_ge(gate["rows"], 1)
                if h >= 2:
                    pe.wait_ge(gate["rows"], h)
                nc.tensor.matmul(ps[:, 6 + h % 2, :], rope["heads"][0:N_FORGET, h * P:(h + 1) * P],
                                 mix["c_rows"][0:N_FORGET, :], start=True, stop=True).then_inc(gate["turned"], 1)

            def group_buffers(t, names):
                return (at1[f"{name}{t // 8 % 2}"] for name in names)

            def scores(t):
                b, h = t % 8 // 2, t % 2
                rows = slice(HD * h, HD * h + HD)
                if t % 8 == 0:
                    pe.wait_ge(a1["staged"], t // 8 + 1)
                if t >= 2:
                    pe.wait_ge(a1["least"], t - 1)
                w = P * (b + 1)
                qh, ql, kh, kl = group_buffers(t, ("qhi", "qlo", "khi", "klo"))
                product(ps[:, t % 2, 0:w], qh[rows, b * P:(b + 1) * P], ql[rows, b * P:(b + 1) * P],
                        kh[rows, 0:w], kl[rows, 0:w], True, True).then_inc(a1["scores"], 1)

            def turn(t):
                pe.wait_ge(a1["probs"], t + 1)
                if t >= 2:
                    pe.wait_ge(a1["pt"], t - 1)
                for j in range(t % 8 // 2 + 1):
                    mm = nc.tensor.transpose(ps[:, 2 + t % 2, j * P:(j + 1) * P], at1["e"][:, t % 3, j * P:(j + 1) * P], ident)
                mm.then_inc(a1["turned"], 1)

            def weigh(t):
                b, h = t % 8 // 2, t % 2
                pe.wait_ge(a1["pt"], t + 1)
                if t % 8 == 0:
                    pe.wait_ge(a1["v_staged"], t // 8 + 1)
                    pe.wait_ge(mix_ready, 4 + t // 8)
                vh, vl = group_buffers(t, ("vhi", "vlo"))
                for j in range(b + 1):
                    cols = slice(j * P, (j + 1) * P)
                    mm = product(ps[:, 4 + h, b * P:(b + 1) * P], vh[:, cols], vl[:, cols],
                                 at1["pt_hi"][:, t % 2, cols], at1["pt_lo"][:, t % 2, cols], j == 0, j == b)
                mm.then_inc(a1["pv"], 1)

            def memory_half(t):
                m, half = t // 2, t % 2
                u = FIRST["mem_k"] + m
                if half == 0:
                    pe.wait_ge(w_ready, u + 1)
                    if m == 0:
                        pe.wait_ge(mem["lo"], KC)
                        pe.wait_ge(gate["rows"], 1 + N_FORGET)
                    if m == 1:
                        pe.wait_ge(mem["rms"], 2)
                    if 2 <= m < KC:
                        pe.wait_ge(mem["k_ready"], m - 1)
                    if m == KC:
                        pe.wait_ge(mem["k_ready"], KC)
                    if m == KC + 4:
                        pe.wait_ge(mem["v_ready"], MB)
                if m < KC:
                    for k in range(KC // 2 * half, KC // 2 * (half + 1)):
                        wh, wl = tile(u % 2, k)
                        mm = product(ps[:, 6 + m % 2, 0:M], wh, wl, mem_split(xg_hi, k), mem_split(xg_lo, k), k == 0, k == KC - 1)
                else:
                    k = 2 * (m % 4) + half
                    cols = slice(half * S, (half + 1) * S)
                    for b in range(MB):
                        block_ = slice(b * P, (b + 1) * P)
                        mm = product(ps[:, 6 + b, :], mem_split(xg_hi, k)[:, block_], mem_split(xg_lo, k)[:, block_],
                                     w_hi[:, u % 2, cols], w_lo[:, u % 2, cols], k == 0, k == KC - 1)
                if half:
                    mm.then_inc(used, 1)
                if t == 1:
                    pe.wait_ge(mem["summed"], KC)
                    nc.tensor.matmul(ps[:, 7, 0:M], ones, memory["acc"][:], start=True, stop=True)
                    for b in range(MB):
                        mm = nc.tensor.matmul(ps[:, 7, M + b:M + b + 1], memory["acc"][:, b * P:(b + 1) * P], ones[:, 0:1],
                                              start=True, stop=True)
                    mm.then_inc(mem["sums"], 1)

            for t in range(MIX_ITEMS + 5):
                if 0 <= t - 3 < MIX_ITEMS:
                    turn(t - 3)
                if t < MIX_ITEMS:
                    scores(t)
                if t < N_FORGET:
                    gate_rows(t)
                if 0 <= t - MEM_LAG < 4 * KC:
                    memory_half(t - MEM_LAG)
                if t >= 5:
                    weigh(t - 5)

            into_residual("w_out", KC, 0, mix["hi"], mix["lo"], mix_ready, lambda k: k + 1,
                          {0: (a1["least"], MIX_ITEMS), 2: (a1["pt"], MIX_ITEMS), 4: (mix_ready, 8),
                           6: (mem["v_ready"], 2 * MB)})

            u0 = FIRST["xq"]
            panel(u0, None, ps[:, 0, :], xg_hi, xg_lo, KC * SPLIT["xa"])
            square_sums("xa", 6)
            panel(u0 + 1, None, ps[:, 1, :], xg_hi, xg_lo)
            panel(u0 + 2, None, ps[:, 2, :], xg_hi, xg_lo)

            def scores(t):
                h, b = t // TB, t % TB
                if b == 0:
                    pe.wait_ge(a2["staged"], h + 1)
                if t >= 2:
                    pe.wait_ge(a2["exps"], t - 1)
                qh, ql, kh, kl = (at2[f"{name}{h % 2}"] for name in ("qhi", "qlo", "khi", "klo"))
                for d in range(XC):
                    qc = slice(d * S + b * P, d * S + (b + 1) * P)
                    kc = slice(d * M, (d + 1) * M)
                    mm = product(ps[:, t % 2, 0:M], qh[:, qc], ql[:, qc], kh[:, kc], kl[:, kc], d == 0, d == XC - 1)
                mm.then_inc(a2["scores"], 1)

            def turn(t):
                pe.wait_ge(a2["probs"], t + 1)
                if t >= 2:
                    pe.wait_ge(a2["pt"], t - 1)
                for j in range(MB):
                    mm = nc.tensor.transpose(ps[:, 2 + t % 2, j * P:(j + 1) * P], at2["e"][:, t % 3, j * P:(j + 1) * P], ident)
                mm.then_inc(a2["turned"], 1)

            def weigh(h):
                pe.wait_ge(a2["pt"], TB * (h + 1))
                pe.wait_ge(a2["v_staged"], h + 1)
                if h:
                    pe.wait_ge(a2["out"], XC * h)
                vh, vl = (at2[f"{name}{h % 2}"] for name in ("vhi", "vlo"))
                for d in range(XC):
                    for j in range(MB):
                        vc = slice((j * XC + d) * P, (j * XC + d + 1) * P)
                        pc = slice(j * S, (j + 1) * S)
                        mm = product(ps[:, 4 + d, :], vh[:, vc], vl[:, vc], at2["pt_hi"][:, h % 2, pc], at2["pt_lo"][:, h % 2, pc],
                                     j == 0, j == MB - 1)
                mm.then_inc(a2["pv"], 1)

            def query_half(t):
                j = t // 2
                u = u0 + XQ_FIRST + j
                if t % 2 == 0:
                    pe.wait_ge(w_ready, u + 1)
                    if j == 0:
                        pe.wait_ge(rms_ready, NORM["xa"] + 1)
                    if j >= 2:
                        pe.wait_ge(xqs["ready"], XQ_FIRST + j - 1)
                for k in range(KC // 2 * (t % 2), KC // 2 * (t % 2 + 1)):
                    wh, wl = tile(u % 2, k)
                    mm = product(ps[:, 6 + j % 2, :], wh, wl, xg_hi[:, k, :], xg_lo[:, k, :], k == 0, k == KC - 1)
                if t % 2:
                    mm.then_inc(used, 1)

            pe.wait_ge(xqs["ready"], XC)
            for t in range(XA_ITEMS + 5):
                if t == 3:
                    pe.wait_ge(xqs["ready"], XQ_FIRST)
                if 0 <= t - 3 < XA_ITEMS:
                    turn(t - 3)
                if t < XA_ITEMS:
                    scores(t)
                if t < 2 * (KC - XQ_FIRST):
                    query_half(t)
                if t % TB == 0 and t >= 2 * TB:
                    weigh(t // TB - 2)

            into_residual("xo", KC, 0, xa["hi"], xa["lo"], a2["out"], lambda k: k + 1, {0: (a2["exps"], XA_ITEMS), 2: (a2["pt"], XA_ITEMS), 4: (a2["out"], KC), 6: (xqs["ready"], KC)})

            st = ffn_stages["up"]
            hidden("up", "ffn", st, 0)
            into_residual("down", FC, 2, ffn["hi"], ffn["lo"], st["hid"], lambda k: k + 1,
                          {0: (r_ready, NORM["ffn"] + 1), 6: (st["scaled"], 2 * FC - 1), 7: (st["scaled"], 2 * FC)})

            u0 = FIRST["a_v"]
            for u in range(u0, u0 + 4):
                pe.wait_ge(xg_ready, KC * SPLIT["first"] + max(4, 2 * (u - u0 + 1)))
                values(u0, u, xg_hi, xg_lo, TB, (2, 3, 4, 5), 2)
                if u == u0 + 1:
                    square_sums("first", 6, 7)
                if u == u0 + 2:
                    square_sums("a", 0, 1, first["sums"])
            pe.wait_ge(rows_rms_ready, ROWS["first"] + 1)
            pe.wait_ge(a_in["first"], 2)
            for u in range(u0 + 4, u0 + KC):
                values(u0 + 4, u, xg_hi, xg_lo, TB, (6, 7, 0, 1), 2)
            u0 = FIRST["a_u"]
            pe.wait_ge(a_in["v"], 4)
            panel(u0, None, ps[:, 2, :], xg_hi, xg_lo)
            panel(u0 + 1, None, ps[:, 3, :], xg_hi, xg_lo)
            with pe.Fori(0, KC // 2 - 1) as i:
                for s in range(2):
                    pe.wait_ge(a_in["scaled"], at(s + 1, i, 2))
                    panel(u0 + 2 + s, i, ps[:, 2 + s, :], xg_hi, xg_lo)
            pe.wait_ge(a_in["w_lo"], 1)
            for g in range(N_SPATIAL):
                if g >= 2:
                    pe.wait_ge(a_in["z"], g - 1)
                for b in range(TB):
                    if g == 0:
                        pe.wait_ge(a_in["v_lo"], b + 1)
                    mm = product(ps[:, 4 + g % 2, b * P:(b + 1) * P],
                                 sg["v_hi"][:, b, g * P:(g + 1) * P], sg["v_lo"][:, b, g * P:(g + 1) * P],
                                 sg["w_hi"][:, g * P:(g + 1) * P], sg["w_lo"][:, g * P:(g + 1) * P], True, True)
                mm.then_inc(a_in["z_done"], 1)
            into_residual("a_out", KC, 0, sg["hi"], sg["lo"], a_in["ready"], lambda k: k + 1,
                          {0: (a_in["v"], 8), 2: (a_in["scaled"], KC), 4: (a_in["z"], N_SPATIAL - 1), 5: (a_in["z"], N_SPATIAL)})

            st = ffn_stages["gu0"]
            hidden("gu0", "ffn0", st, 0)
            into_residual("down0", FC, 2, ffn["hi"], ffn["lo"], st["hid"], lambda k: k + 1,
                          {0: (r_ready, NORM["ffn0"] + 1), 6: (st["scaled"], 2 * FC - 1), 7: (st["scaled"], 2 * FC)})

            u0 = FIRST["kv_v"]
            for u in range(u0, u0 + 4):
                pe.wait_ge(xg_ready, KC * SPLIT["kv"] + max(4, 2 * (u - u0 + 1)))
                values(u0, u, xg_hi, xg_lo, TB, (2, 3, 4, 5), 2)
                if u == u0 + 1:
                    pe.wait_ge(xg_ready, KC * SPLIT["kv"] + 6)
                    square_sums("kv", 6, 7)
            pe.wait_ge(r_ready, NORM["kv"] + 1)
            pe.wait_ge(rows_ready, ROWS["kv"] + 1)
            pe.wait_ge(x_ready, KC * NORM["kv"])
            for u in range(u0 + 4, u0 + KC):
                values(u0 + 4, u, xg_hi, xg_lo, TB, (6, 7, 0, 1), 2)
            qk0 = FIRST["qk"]

            def half_panel(u, i, to, hi, lo, half):
                if half == 0:
                    pe.wait_ge(w_ready, at(u + 1, i, 4))
                for k in range(KC // 2 * half, KC // 2 * (half + 1)):
                    wh, wl = tile(u % 2, k)
                    mm = product(to, wh, wl, hi[:, k, :], lo[:, k, :], k == 0, k == KC - 1)
                if half:
                    mm.then_inc(used, 1)

            def qk_input(p):
                return (da["xb_hi"], da["xb_lo"]) if p % 2 else (xg_hi, xg_lo)

            pe.wait_ge(kv["v"], 4)
            for p in range(EARLY_PANELS):
                if p == 1:
                    pe.wait_ge(kv["xb"], KC)
                for half in range(2):
                    half_panel(qk0 + p, None, ps[:, 2 + p, :], *qk_input(p), half)
            pe.wait_ge(kv["v"], 8)
            pe.wait_ge(kv["qk"], EARLY_PANELS)

            def diff_item(n, c, base):
                def scores(n):
                    s, b = n // TB, n % TB
                    if b == 0:
                        pe.wait_ge(a3["staged"], at(2 * (base // TB + s + 1), c, 4))
                    if c is not None or n + base >= 2:
                        pe.wait_ge(a3["least"], at(2 * (base + n - 1), c, 16))
                    w = P * (b + 1)
                    qh, ql, kh, kl = (at3[f"{p}{s % 2}"] for p in ("qhi", "qlo", "khi", "klo"))
                    block_ = slice(b * P, (b + 1) * P)
                    for k, (q_, k_) in enumerate(((qh, kh), (qh, kl), (ql, kh))):
                        for h in range(2):
                            rows = slice(HD * h, HD * h + HD)
                            mm = nc.tensor.matmul(ps[:, 2 * (n % 2) + h, 0:w], q_[rows, block_], k_[rows, 0:w],
                                                  start=k == 0, stop=k == 2)
                            if k == 2:
                                mm.then_inc(a3["scores"], 1)

                def turn(n):
                    b = n % TB
                    pe.wait_ge(a3["probs"], at(base + n + 1, c, 8))
                    if c is not None or n + base >= 2:
                        pe.wait_ge(a3["pt"], at(base + n - 1, c, 8))
                    for j in range(b + 1):
                        mm = nc.tensor.transpose(ps[:, 4 + n % 2, j * P:(j + 1) * P],
                                                 at3["e"][:, 2 * (n % DIFF_SLOTS), j * P:(j + 1) * P], ident)
                    mm.then_inc(a3["turned"], 1)

                def weigh(n):
                    s, b = n // TB, n % TB
                    pe.wait_ge(a3["pt"], at(base + n + 1, c, 8))
                    if b == 0:
                        pe.wait_ge(a3["v_staged"], at(base // TB + s + 1, c, 2))
                        pe.wait_ge(a3["out"], at(base // TB + s + 1, c, 2))
                    vh, vl = at3[f"vhi{s % 2}"], at3[f"vlo{s % 2}"]
                    for j in range(b + 1):
                        cols = slice(j * P, (j + 1) * P)
                        mm = product(ps[:, 6, b * P:(b + 1) * P], vh[:, cols], vl[:, cols],
                                     at3["pt_hi"][:, n % 2, cols], at3["pt_lo"][:, n % 2, cols], j == 0, j == b)
                    mm.then_inc(a3["pv"], 1)

                if live(n - 4, c, base):
                    turn(n - 4)
                if live(n, c, base):
                    scores(n)
                p = EARLY_PANELS + (base + n) // 2
                if p < 2 * N_DIFF:
                    if n % 2 == 0:
                        pe.wait_ge(kv["qk"], at(p, c, 4))
                    half_panel(qk0 + p, c, ps[:, 7, :], *qk_input(p), n % 2)
                if live(n - 6, c, base):
                    weigh(n - 6)
                if n >= 8:
                    head_sums(n - 8)

            def head_sums(h):
                if h == 0:
                    pe.wait_ge(a3["least"], 8 * N_DIFF - 2)
                pe.wait_ge(a3["sq"], h + 1)
                pick = con[:, CAT["pick"] + N_DIFF - 1 - h:CAT["pick"] + 2 * N_DIFF - 1 - h]
                nc.tensor.matmul(ps[0:N_DIFF, 0, :], pick, squares[:, h % 2, :], start=h == 0,
                                 stop=h == N_DIFF - 1).then_inc(a3["summed"], 1)

            diff_turns(pe, diff_item, 6)
            for h in range(6, N_DIFF):
                head_sums(h)
            pe.wait_ge(a3["least"], 8 * N_DIFF)
            pe.wait_ge(loads["alibi"], 2 * 16)
            pe.wait_ge(a3["rms"], 2)
            for h in range(N_DIFF):
                if h >= 4:
                    pe.wait_ge(a3["normed"], h - 3)
                pick = da["picks"][:, h * P:(h + 1) * P]
                nc.tensor.matmul(ps[:, h % 4, :], pick, da["rms"], start=True, stop=True).then_inc(a3["spread"], 1)
            into_residual("bo", KC, 4, xg_hi, xg_lo, a3["out_lo"], lambda k: k + 1, {0: (a3["out"], N_DIFF + 1), 3: (kv["qk"], 2 * KC), 4: (a3["normed"], N_DIFF)})

            st = ffn_stages["gu1"]
            hidden("gu1", "ffn1", st, 4)
            into_residual("down1", FC, 6, ffn["hi"], ffn["lo"], st["hid"], lambda k: k + 1,
                          {0: (r_ready, NORM["ffn1"] + 1), 6: (st["scaled"], 2 * FC - 1), 7: (st["scaled"], 2 * FC)})
            pe.wait_ge(x_ready, KC * (NORM["final"] - 1) + TB)
            for c in range(0, KC, 2):
                pe.wait_ge(finals["pairs"], c // 2 + 1)
                for b in range(TB):
                    mm = nc.tensor.matmul(ps[:, FINAL_BANKS[b], 0:1], final["squares"][:, c, b * P:(b + 1) * P], ones[:, 0:1],
                                          start=c == 0, stop=c == KC - 2)
            mm.then_inc(sums_ready, 1)
            pe.wait_ge(x_ready, KC * NORM["final"])
            for b in range(TB):
                pe.wait_ge(finals["diagonal"], b + 1)
                mm = nc.tensor.matmul(ps[:, 2, b * P:(b + 1) * P], ones, final["diagonal"][:, b * P:(b + 1) * P],
                                      start=True, stop=True)
            mm.then_inc(finals["spread"], 1)

        @block.scalar
        def _(act):
            def split(u, i=None):
                if u >= N_UNITS:
                    return
                act.wait_ge(w_loaded[u % 2], at(16 * (u // 2 + 1), i, 16))
                if u >= 2:
                    act.wait_ge(used, at(u - 1, i, 2))
                nc.scalar.activation(w_hi[:, u % 2, :], w_raw[:, u % 2, :], ACT.Copy).then_inc(w_hi_ready, 1)

            def norm_input(norm, gain, finals_only=False):
                n = NORM[norm]
                for c in range(KC):
                    if n == 0:
                        if c == 1:
                            split(0)
                        if c == 0:
                            act.wait_ge(loads["input"], 2 * 16)
                        if c == KC // 2:
                            act.wait_ge(loads["rest"], 16)
                    else:
                        act.wait_ge(x_ready, KC * (n - 1) + c + 1)
                    if not finals_only:
                        nc.scalar.activation(xg_hi[:, c, :], x[:, c, :], ACT.Copy, scale=column(gain, c)).then_inc(xg_hi_ready, 1)
                    k = KC * n + c
                    if k >= 2 and not finals_only:
                        act.wait_ge(summed, k - 1)
                    to = final["squares"][:, c, :] if finals_only else squares[:, c % 2, :]
                    nc.scalar.activation(to, x[:, c, :], ACT.Square).then_inc(sq_ready, 1)

            def norm_rms(norm, bank=None, rows_bank=None):
                n = NORM[norm]
                if norm == "a":
                    act.wait_ge(a_in["first"], 4)
                    nc.scalar.activation(first["sums"][:], first["sums"][:], ACT.Sqrt, bias=column("eps"), scale=1.0 / D).then_inc(rms_ready, 1)
                    nc.scalar.activation(first["sums_rows"][:], first["sums_rows"][:], ACT.Sqrt, bias=column("eps"),
                                         scale=1.0 / D).then_inc(rows_rms_ready, 1)
                    return
                act.wait_ge(sums_ready, n + 1)
                if norm == "final":
                    for b in range(0, TB, 2):
                        sums = ps[:, FINAL_BANKS[b]:FINAL_BANKS[b] + 2, 0:1].rearrange("p b n -> p (b n)")
                        nc.scalar.activation(rms_rows[:, b:b + 2], sums, ACT.Sqrt, bias=column("eps"), scale=1.0 / D).then_inc(rms_ready, 1)
                    return
                if rows_bank is not None:
                    act.wait_ge(rows_sums_ready, ROWS[norm] + 1)
                nc.scalar.activation(square_sum[:], ps[:, bank, :], ACT.Sqrt, bias=column("eps"), scale=1.0 / D).then_inc(rms_ready, 1)
                if rows_bank is not None:
                    if ROWS[norm]:
                        act.wait_ge(rows_ready, ROWS[norm])
                    nc.scalar.activation(rms_rows[:], ps[:, rows_bank, 0:TB], ACT.Sqrt, bias=column("eps"),
                                         scale=1.0 / D).then_inc(rows_rms_ready, 1)

            def splits_of(name, n, skip_last=0):
                u0 = FIRST[name]
                with act.Fori(0, n // 2 - 1) as i:
                    split(u0 + 2, i)
                    split(u0 + 3, i)
                split(u0 + n)
                if not skip_last:
                    split(u0 + n + 1)

            def into_residual(name, n, norm, gain):
                splits_of(name, n, 1)
                norm_input(norm, gain, gain is None)
                split(FIRST[name] + n + 1)

            act.wait_ge(loads["input"], 2 * 16)
            act.dma_start(con[:], consts).then_inc(loads["con"], 16)
            norm_input("mix", "g_mix")
            split(1)
            norm_rms("mix", 2, 3)
            u0 = FIRST["w_in"]
            split(u0 + 2)
            act.wait_ge(lams["dots"], 4)
            nc.scalar.activation(lam_exp[:], lam_dot[:], ACT.Exp).then_inc(lams["exps"], 1)
            with act.Fori(0, 4) as i:
                split(u0 + 3, i)
                split(u0 + 4, i)
            act.wait_ge(w_in["evacuated"], 1)
            nc.scalar.activation(rope["g1"][0:N_FORGET, :], mix["proj"][0:N_FORGET, 0, :], ACT.Abs,
                                 bias=column("b_forget", 0, slice(0, N_FORGET))).then_inc(gate["abs"], 1)
            act.wait_ge(gate["abs"], 1)
            nc.scalar.activation(rope["g2"][0:N_FORGET, :], rope["g1"][0:N_FORGET, :], ACT.Exp, scale=-1.0).then_inc(gate["exp"], 1)
            split(u0 + 11)
            split(u0 + 12)
            act.wait_ge(rot["steps"], 11)
            nc.scalar.activation(rope["sin"][:], rope["red"][:], ACT.Sin).then_inc(rot["trig"], 1)
            nc.scalar.activation(rope["cos"][:], rope["ang"][:], ACT.Sin).then_inc(rot["trig"], 1)
            with act.Fori(1, 5) as i:
                split(u0 + 11, i)
                split(u0 + 12, i)
            for c in range(GC):
                act.wait_ge(small["conv"], c + 1)
                nc.scalar.activation(mix["hi"][:, c, :], mix["proj"][:, 1 + c, :], ACT.Copy).then_inc(small["hi"], 1)
            for c in range(GC):
                act.wait_ge(small["product"], c + 1)
                nc.scalar.activation(mix["hi"][:, GC + c, :], ps[:, c, :], ACT.Copy, scale=column("pool_scale", c)).then_inc(small["hi"], 1)
            split(u0 + 21)
            split(u0 + 22)
            act.wait_ge(gate["turned"], 1)
            nc.scalar.activation(mix["nci"][:].rearrange("p b h -> p (b h)"), ps[:, 2, 0:TB * N_FORGET], ACT.Copy,
                                 scale=-1.0).then_inc(gate["rows"], 1)

            def gate_rows(h):
                if h == 0:
                    act.wait_ge(mix_ready, 4)
                act.wait_ge(gate["turned"], h + 2)
                nc.scalar.activation(mix["proj"][:, 1 + h, :], ps[:, 6 + h % 2, :], ACT.Copy).then_inc(gate["rows"], 1)

            act.wait_ge(summed, KC)
            act.wait_ge(r_ready, 1)
            act.wait_ge(gate["c"], 1)
            act.dma_start(squares[:].rearrange("p a t -> p (a t)"), mem_cols[:, 0:4, :].rearrange("p c t -> p (c t)")
                          ).then_inc(loads["mem"], 16)
            act.dma_start(square_sum[:], mem_cols[:, 4:6, :].rearrange("p c t -> p (c t)")).then_inc(loads["mem"], 16)
            act.dma_start(mix["proj"][:, 0, :], mem_cols[:, 6:8, :].rearrange("p c t -> p (c t)")).then_inc(loads["mem"], 16)

            act.wait_ge(rot["done"], 4)
            act.wait_ge(w_in["evacuated"], 17)
            act.wait_ge(w_in["v_ready"], TB)
            act.wait_ge(used, FIRST["w_in"] + 2 * KC + 5)

            def stage_part(g, name, src, scale):
                to = at1[f"{name}{g % 2}"].rearrange("p (a n) -> p a n", a=src.shape[1])
                return nc.scalar.activation(to, src, ACT.Copy, scale=scale).then_inc(a1["staged_hi"], 1)

            def stage_qk(g):
                s, c = g % 2, g // 2
                if g >= 2:
                    act.wait_ge(a1["scores"], 8 * (g - 1))
                stage_part(g, "qhi", mix["proj"][:, 9 + 4 * s + c:10 + 4 * s + c, :], -HD ** -0.5)
                stage_part(g, "khi", mix["proj"][:, 11 + 4 * s + c:12 + 4 * s + c, :], 1.0)

            def stage_v(g):
                s, c = g % 2, g // 2
                if g >= 2:
                    act.wait_ge(a1["pv"], 8 * (g - 1))
                stage_part(g, "vhi", mix["v"][:, :, G * s + c * P:G * s + (c + 1) * P], 1.0)

            def exp(t):
                act.wait_ge(a1["least"], t + 1)
                w = P * (t % 8 // 2 + 1)
                nc.scalar.activation(at1["e"][:, t % 3, 0:w], at1["e"][:, t % 3, 0:w], ACT.Exp, scale=-1.0,
                                     bias=at1["least"][:, t % 3:t % 3 + 1],
                                     accum_out=at1["sums"][:, t % 3:t % 3 + 1]).then_inc(a1["exps"], 1)

            def hi(t):
                act.wait_ge(a1["turned"], t + 1)
                if t >= 2:
                    act.wait_ge(a1["pv"], t - 1)
                w = P * (t % 8 // 2 + 1)
                nc.scalar.activation(at1["pt_hi"][:, t % 2, 0:w], ps[:, 2 + t % 2, 0:w], ACT.Copy).then_inc(a1["pt_hi"], 1)

            def output(g):
                act.wait_ge(a1["pv"], 8 * (g + 1))
                for h in range(2):
                    rows = slice(HD * h, HD * h + HD)
                    nc.scalar.activation(mix["hi"][rows, 4 + g, :], ps[rows, 4 + h, :], ACT.Copy).then_inc(a1["out_hi"], 1)

            def memory_in(c):
                if c == 0:
                    act.wait_ge(loads["mem"], 3 * 16)
                nc.scalar.activation(mem_split(xg_hi, c), mem_input(c), ACT.Copy, scale=column("g_mem", c)).then_inc(mem["hi"], 1)
                if c >= 2:
                    act.wait_ge(mem["summed"], c - 1)
                nc.scalar.activation(memory["sq"][:, c % 2, :], mem_input(c), ACT.Square).then_inc(mem["sq"], 1)

            def memory_out(t):
                if t == 2:
                    act.wait_ge(mem["sums"], 1)
                    nc.scalar.activation(memory["rms"][:], ps[:, 7, 0:M], ACT.Sqrt, bias=column("eps"), scale=1.0 / D).then_inc(mem["rms"], 1)
                    nc.scalar.activation(memory["rms_rows"][:], ps[:, 7, M:M + MB], ACT.Sqrt, bias=column("eps"),
                                         scale=1.0 / D).then_inc(mem["rms"], 1)
                m = t // 2 - 1
                if t % 2 == 0 and 0 <= m < 2 * KC:
                    if m in (KC + 3, KC + 7):
                        h = (m - KC) // 4
                        act.wait_ge(used, FIRST["mem_k"] + m + 1)
                        act.wait_ge(mem["r"], 2)
                        for b in range(MB):
                            nc.scalar.activation(xa["v"][:, b, h * S:(h + 1) * S], ps[:, 6 + b, :], ACT.Copy,
                                                 scale=memory["r_rows"][:, b:b + 1]).then_inc(mem["v_ready"], 1)
                    split(FIRST["mem_k"] + m + 2)

            stage_qk(0)
            stage_v(0)
            for t in range(MIX_ITEMS + 6):
                if 0 <= t - 4 < MIX_ITEMS:
                    hi(t - 4)
                if t % 8 == 5 and t > 8:
                    output(t // 8 - 1)
                if 0 <= t - 1 < MIX_ITEMS:
                    exp(t - 1)
                g = t // 8 + 1
                if t % 8 == 1 and g < 2 * GC:
                    stage_qk(g)
                if t % 8 == 6 and g < 2 * GC:
                    stage_v(g)
                if t < N_FORGET:
                    gate_rows(t)
                if t < KC // 2:
                    memory_in(2 * t)
                    memory_in(2 * t + 1)
                memory_out(t - MEM_LAG)

            u0 = FIRST["w_out"]
            split(u0 + 2)
            split(u0 + 3)
            for u in range(u0 + 4, u0 + KC + 1):
                split(u)
            norm_input("xa", "g_xa")
            split(u0 + KC + 1)
            norm_rms("xa", 6)
            u0 = FIRST["xq"]
            split(u0 + 2)
            split(u0 + 3)

            def stage_part(g, name, src, scale):
                to = at2[f"{name}{g % 2}"][:].rearrange("p (a n) -> p a n", a=src.shape[1])
                nc.scalar.activation(to, src, ACT.Copy, scale=scale).then_inc(a2["staged_hi"], 1)

            def stage_qk(g):
                if g >= 2:
                    act.wait_ge(a2["scores"], TB * (g - 1))
                stage_part(g, "khi", xa["k"][:, XC * g:XC * (g + 1), :], 1.0)
                act.wait_ge(xqs["ready"], XC * (g + 1))
                stage_part(g, "qhi", xa["q"][:, XC * g:XC * (g + 1), :], -(XC * P) ** -0.5)

            def stage_v(g):
                if g >= 2:
                    act.wait_ge(a2["pv"], g - 1)
                stage_part(g, "vhi", xa["v"][:, :, XC * P * g:XC * P * (g + 1)], 1.0)

            def exp(t):
                k = t % 3
                if t >= 3:
                    act.wait_ge(a2["turned"], t - 2)
                act.wait_ge(a2["least"], t + 1)
                nc.scalar.activation(at2["e"][:, k, :], ps[:, t % 2, 0:M], ACT.Exp, scale=-1.0, bias=at2["least"][:, k:k + 1],
                                     accum_out=at2["sums"][:, k:k + 1]).then_inc(a2["exps"], 1)

            def hi(t):
                h, b = t // TB, t % TB
                act.wait_ge(a2["turned"], t + 1)
                if h >= 2 and b == 0:
                    act.wait_ge(a2["pv"], h - 1)
                to = at2["pt_hi"][:, h % 2, :].rearrange("p (j n) -> p j n", j=MB)[:, :, b * P:(b + 1) * P]
                nc.scalar.activation(to, ps[:, 2 + t % 2, 0:M].rearrange("p (j n) -> p j n", j=MB), ACT.Copy).then_inc(a2["pt_hi"], 1)

            def output(h):
                act.wait_ge(a2["pv"], h + 1)
                for d in range(XC):
                    nc.scalar.activation(xa["hi"][:, XC * h + d, :], ps[:, 4 + d, :], ACT.Copy).then_inc(a2["out_hi"], 1)

            act.wait_ge(mem["v_ready"], 2 * MB)
            stage_qk(0)
            stage_v(0)
            split(u0 + 4)
            for t in range(XA_ITEMS + 6):
                if 0 <= t - 4 < XA_ITEMS:
                    hi(t - 4)
                if t % TB == 1 and t > 2 * TB:
                    output(t // TB - 2)
                if 0 <= t - 1 < XA_ITEMS:
                    exp(t - 1)
                if t % TB == 2 and t // TB + 1 < XA_HEADS:
                    stage_qk(t // TB + 1)
                if t % TB == 1 and 0 < t // TB < XA_HEADS:
                    stage_v(t // TB)
                if t % 2 == 0 and 0 < t <= 2 * (KC - XQ_FIRST):
                    split(u0 + XQ_FIRST + t // 2 + 1)
            into_residual("xo", KC, "ffn", "g_ffn")

            st = ffn_stages["up"]
            norm_rms("ffn", 2)

            def conv_gate(i, done):
                act.wait_ge(st["steps"], at(4 * done + 4, i, 4))
                nc.scalar.activation(ffn["gate"][:], ffn["tg"][:], ACT.Silu).then_inc(st["gated"], 1)

            def conv_hidden(i, done):
                act.wait_ge(st["product"], at(done + 1, i, 1))
                nc.scalar.activation(ffn["hi"][:, bass.ds(at(done, i, 1), 1), :].rearrange("p a n -> p (a n)"), ffn["h"][:],
                                     ACT.Copy).then_inc(st["hid_hi"], 1)

            def conv_turn(i, first):
                u = FIRST["up"]
                if not first:
                    conv_gate(i, -1)
                for s, (src, to) in enumerate(((ffn["ua"], ffn["ta"]), (ffn["ug"], ffn["tg"]))):
                    split(u + 2 + s, i)
                    if s == 0 and not first:
                        act.wait_ge(st["product"], at(0, i, 1))
                    act.wait_ge(st["scaled"], at(s + 1, i, 2))
                    nc.scalar.activation(to[:], src[:, 2:S + 2], ACT.Copy,
                                         scale=column("w_ffconv", at(2 * 2 * FC + s * FC, i, 1))).then_inc(st["tapped"], 1)
                    if s == 0 and not first:
                        conv_hidden(i, -1)

            conv_turn(None, True)
            with act.Fori(1, FC) as i:
                conv_turn(i, False)
            conv_gate(None, FC - 1)
            conv_hidden(None, FC - 1)
            act.wait_ge(st["hid"], FC)
            act.dma_start(sg["w"][:], spatial).then_inc(loads["spatial"], 16)
            act.dma_start(sg["b"][:].rearrange("p g t -> p (g t)"), spatial_bias).then_inc(loads["spatial"], 16)
            into_residual("down", FC, "first", "a_gain")

            u0 = FIRST["a_v"]
            for c in range(KC):
                k = KC * NORM["a"] + c
                act.wait_ge(summed, k - 1)
                nc.scalar.activation(squares[:, c % 2, :], x[:, c, :], ACT.Square, scale=column("g_first", c)).then_inc(sq_ready, 1)
                if c == KC // 2:
                    split(u0 + 2)
            split(u0 + 3)
            norm_rms("first", 6, 7)
            split(u0 + 4)
            norm_rms("a")
            split(u0 + 5)
            for h in range(2):
                if h:
                    for u in range(u0 + 6, u0 + KC + 2):
                        split(u)
                act.wait_ge(used, u0 + 4 * h + 4)
                act.wait_ge(rows_ready, ROWS["a"] + 1)
                for b in range(TB):
                    bank = ((2, 3, 4, 5), (6, 7, 0, 1))[h][b]
                    nc.scalar.activation(sg["v"][:, b, h * S:(h + 1) * S], ps[:, bank, :], ACT.Gelu_apprx_tanh,
                                         scale=r_rows[:, b:b + 1], accum_out=sg["v_sum"][:, b, h:h + 1]).then_inc(a_in["v"], 1)
            u0 = FIRST["a_u"]

            def gate_panel(s, i):
                act.wait_ge(a_in["scaled"], at(s + 1, i, 2))
                ut = sg["u"][:, bass.ds(at(s, i, 2), 1), :].rearrange("p a n -> p (a n)")
                nc.scalar.activation(ut, ut, ACT.Gelu_apprx_tanh).then_inc(a_in["u"], 1)
                split(u0 + 2 + s, i)

            for b in range(TB):
                act.wait_ge(a_in["steps"], 2)
                nc.scalar.activation(sg["hi"][:, 2 * b:2 * b + 2, :], sg["v"][:, b, :].rearrange("p (a n) -> p a n", a=2),
                                     ACT.Square, bias=sg["mean"][:, b:b + 1], accum_out=sg["v_sq"][:, b:b + 1]).then_inc(a_in["v_sq"], 1)
            gate_panel(0, None)
            act.wait_ge(a_in["v_sq"], TB)
            nc.scalar.activation(sg["std"][:], sg["v_sq"][:], ACT.Sqrt, bias=column("eps"), scale=1.0 / D).then_inc(a_in["std"], 1)
            act.wait_ge(a_in["w"], 1)
            nc.scalar.activation(sg["w_hi"][:], sg["w"][:], ACT.Copy).then_inc(a_in["w_hi"], 1)
            gate_panel(1, None)
            for p in range(KC - 2):
                if p < TB:
                    act.wait_ge(a_in["normed"], p + 1)
                    nc.scalar.activation(sg["v_hi"][:, p, :], sg["v"][:, p, :], ACT.Copy).then_inc(a_in["v_hi"], 1)
                gate_panel(p % 2, 1 + p // 2)
            for g in range(N_SPATIAL):
                act.wait_ge(a_in["product"], g + 1)
                nc.scalar.activation(sg["hi"][:, g, :], sg["u"][:, g, :], ACT.Copy).then_inc(a_in["hi"], 1)
            into_residual("a_out", KC, "ffn0", "ffn_norm0")

            def swiglu(name, norm, base):
                st = ffn_stages[name]
                norm_rms(norm, (base + 2) % 8)
                with act.Fori(0, FC) as i:
                    act.wait_ge(st["scaled"], at(1, i, 2))
                    nc.scalar.activation(ffn["gate"][:], ffn["tg"][:], ACT.Silu).then_inc(st["gated"], 1)
                    split(FIRST[name] + 2, i)
                    split(FIRST[name] + 3, i)
                    act.wait_ge(st["product"], at(1, i, 1))
                    nc.scalar.activation(ffn["hi"][:, bass.ds(at(0, i, 1), 1), :].rearrange("p a n -> p (a n)"), ffn["h"][:],
                                         ACT.Copy).then_inc(st["hid_hi"], 1)

            swiglu("gu0", "ffn0", 0)
            into_residual("down0", FC, "kv", "kv_norm")

            act.dma_start(da["alibi"][:], alibi_table).then_inc(loads["alibi"], 16)
            u0 = FIRST["kv_v"]
            split(u0 + 2)
            norm_rms("kv", 6, 7)
            for h in range(2):
                for u in range(u0 + 4 * h + (h == 0), u0 + 4 * h + 4):
                    split(u + 2)
                    if h:
                        for c in range(2 * (u - u0 - 4), 2 * (u - u0 - 4) + 2):
                            nc.scalar.activation(da["xb_hi"][:, c, :], x[:, c, :], ACT.Copy,
                                                 scale=column("b_norm", c)).then_inc(kv["xb_hi"], 1)
                act.wait_ge(used, u0 + 4 * h + 4)
                act.wait_ge(rows_ready, ROWS["kv"] + 1)
                for b in range(TB):
                    bank = ((2, 3, 4, 5), (6, 7, 0, 1))[h][b]
                    nc.scalar.activation(da["v"][:, b, h * S:(h + 1) * S], ps[:, bank, :], ACT.Copy,
                                         scale=r_rows[:, b:b + 1]).then_inc(kv["v"], 1)
            qk0 = FIRST["qk"]
            for p in range(EARLY_PANELS):
                split(qk0 + p + 2)

            def diff_item(n, c, base):
                def hi(n):
                    act.wait_ge(a3["turned"], at(base + n + 1, c, 8))
                    if c is not None or n + base >= 2:
                        act.wait_ge(a3["pv"], at(base + n - 1, c, 8))
                    w = P * (n % TB + 1)
                    nc.scalar.activation(at3["pt_hi"][:, n % 2, 0:w], ps[:, 4 + n % 2, 0:w], ACT.Copy).then_inc(a3["pt_hi"], 1)

                def exp(n):
                    w = P * (n % TB + 1)
                    for h in range(2):
                        k = 2 * (n % DIFF_SLOTS) + h
                        act.wait_ge(a3["least"], at(2 * (base + n) + h + 1, c, 16))
                        nc.scalar.activation(at3["e"][:, k, 0:w], at3["e"][:, k, 0:w], ACT.Exp, scale=-1.0,
                                             bias=at3["least"][:, k:k + 1], accum_out=at3["sums"][:, k:k + 1]).then_inc(a3["exps"], 1)

                def second(n):
                    act.wait_ge(a3["second"], at(base + n + 1, c, 8))
                    w = P * (n % TB + 1)
                    k = 2 * (n % DIFF_SLOTS) + 1
                    nc.scalar.activation(at3["e"][:, k, 0:w], at3["e"][:, k, 0:w], ACT.Copy,
                                         scale=at3["second"][:, k:k + 1]).then_inc(a3["weighed"], 1)

                def output(n):
                    s = n // TB
                    act.wait_ge(a3["pv"], at(base + n + 1, c, 8))
                    h = bass.ds(at(base // TB + s, c, 2), 1)
                    nc.scalar.activation(da["o"][:, h, :].rearrange("p a n -> p (a n)"), ps[:, 6, :],
                                         ACT.Copy).then_inc(a3["out"], 1)

                if live(n - 5, c, base):
                    hi(n - 5)
                if n % TB == 2 and live(n - 7, c, base):
                    output(n - 7)
                if live(n - 1, c, base):
                    exp(n - 1)
                if live(n - 2, c, base):
                    second(n - 2)
                if qk_due(n, c, base):
                    split_qk(n, c, base)
                if n >= 8:
                    head_square(n - 8)

            def split_qk(n, c, base):
                u = qk0 + EARLY_PANELS - 1 + (base + n) // 2 + 2
                act.wait_ge(w_loaded[u % 2], at(16 * (u // 2 + 1), c, 32))
                act.wait_ge(used, at(u - 1, c, 4))
                nc.scalar.activation(w_hi[:, u % 2, :], w_raw[:, u % 2, :], ACT.Copy).then_inc(w_hi_ready, 1)

            def head_square(h):
                if h == 0:
                    act.wait_ge(a3["staged"], 2 * N_DIFF)
                act.wait_ge(a3["out"], h + 2)
                if h >= 2:
                    act.wait_ge(a3["summed"], h - 1)
                nc.scalar.activation(squares[:, h % 2, :], da["o"][:, h, :], ACT.Square).then_inc(a3["sq"], 1)

            act.sem_inc(a3["out"], 1)
            diff_turns(act, diff_item, 7)
            act.wait_ge(a3["turned"], 4 * N_DIFF)
            act.dma_start(da["picks"], head_picks).then_inc(loads["alibi"], 16)
            head_square(N_DIFF - 1)
            act.wait_ge(a3["summed"], N_DIFF)
            nc.scalar.activation(da["rms"], ps[0:N_DIFF, 0, :], ACT.Sqrt, bias=column("eps", 0, slice(0, N_DIFF)),
                                 scale=1.0 / P).then_inc(a3["rms"], 1)
            for h in range(N_DIFF):
                act.wait_ge(a3["normed"], h + 1)
                nc.scalar.activation(xg_hi[:, h, :], da["o"][:, h, :], ACT.Copy).then_inc(a3["out_hi"], 1)
            into_residual("bo", KC, "ffn1", "ffn_norm1")
            swiglu("gu1", "ffn1", 4)
            into_residual("down1", FC, "final", None)
            norm_rms("final")

        @block.vector
        def _(dve):
            def split(u, i=None):
                if u >= N_UNITS:
                    return
                dve.wait_ge(w_hi_ready, at(u + 1, i, 2))
                nc.vector.tensor_tensor(w_lo[:, u % 2, :], w_raw[:, u % 2, :], w_hi[:, u % 2, :].bitcast(F32),
                                        ALU.subtract).then_inc(w_ready, 1)

            def gained(norm, gain, c):
                dve.wait_ge(xg_hi_ready, KC * SPLIT[norm] + c + 1)
                nc.vector.scalar_tensor_tensor(out=xg_lo[:, c, :], in0=x[:, c, :], scalar=column(gain, c),
                                               in1=xg_hi[:, c, :].bitcast(F32), op0=ALU.mult,
                                               op1=ALU.subtract).then_inc(xg_ready, 1)

            def norm_r(norm, rows=False):
                n = NORM[norm]
                dve.wait_ge(rms_ready, n + 1)
                nc.vector.reciprocal(r_cols[:], square_sum[:]).then_inc(r_ready, 1)
                if rows:
                    dve.wait_ge(rows_rms_ready, ROWS[norm] + 1)
                    nc.vector.reciprocal(r_rows[:], rms_rows[:]).then_inc(rows_ready, 1)
                dve.wait_ge(r_ready, n + 1)

            def scaled(to, bank, signal, cols=S, r=None):
                return nc.vector.tensor_tensor(to, ps[:, bank, 0:cols], r_cols[:] if r is None else r,
                                               ALU.mult).then_inc(signal, 1)

            def chunk(t, c):
                return t[:, bass.ds(c, 1), :].rearrange("p a n -> p (a n)")

            def splits_of(name, n, skip_last=0):
                u0 = FIRST[name]
                with dve.Fori(0, n // 2 - 1) as i:
                    split(u0 + 2, i)
                    split(u0 + 3, i)
                split(u0 + n)
                if not skip_last:
                    split(u0 + n + 1)

            def into_residual(name, n, norm, gain, bank0, final_splits=True):
                if final_splits:
                    splits_of(name, n, 1)
                done = KC * (NORM[norm] - 1)
                for j in range(KC + 1):
                    if j < KC:
                        if j < KC - 1:
                            dve.wait_ge(proj_sums, (KC - 1) * RESIDUALS.index(name) + j + 1)
                        else:
                            dve.wait_ge(used, FIRST[name] + n)
                        nc.vector.tensor_tensor(x[:, j, :], ps[:, (bank0 + j) % 8, :], x[:, j, :],
                                                ALU.add).then_inc(x_ready, 1)
                    if j and gain is not None:
                        gained(norm, gain, j - 1)
                split(FIRST[name] + n + 1)

            for c in range(KC):
                if c == 0:
                    dve.wait_ge(loads["input"], 2 * 16)
                if c == 1:
                    split(0)
                if c == KC // 2:
                    dve.wait_ge(loads["rest"], 16)
                gained("mix", "g_mix", c)
            split(1)
            dve.wait_ge(loads["early"], 16 * N_EARLY)
            for h in range(2):
                a, b = (lam_in[:, (2 * h + k) * HD:(2 * h + k + 1) * HD] for k in range(2))
                nc.vector.tensor_tensor_reduce(a, a, b, 1.0, 0.0, ALU.mult, ALU.add, lam_dot[:, h:h + 1]).then_inc(lams["dots"], 1)
            nc.vector.tensor_tensor(par[:, AT["a_gain"]:AT["a_gain"] + KC], par[:, AT["g_first"]:AT["g_first"] + KC],
                                    par[:, AT["a_norm"]:AT["a_norm"] + KC], ALU.mult).then_inc(lams["dots"], 1)
            nc.vector.tensor_scalar(subln[:], column("b_subln"), 1.0 - LAMBDA_INIT, None, ALU.mult).then_inc(lams["dots"], 1)
            norm_r("mix", True)
            u0 = FIRST["w_in"]
            dve.wait_ge(used, u0 + 1)
            scaled(mix["proj"][:, 0, :], 0, w_in["evacuated"])
            split(u0 + 2)

            def input_panel(s, i):
                dve.wait_ge(used, at(u0 + 2 + s, i, 2))
                scaled(chunk(mix["proj"], at(1 + s, i, 2)), 1 - s, w_in["evacuated"])
                split(u0 + 3 + s, i)

            counted = [0]

            def step(ins, s):
                counted[0] += 1
                ins.then_inc(s, 1)
                dve.wait_ge(s, counted[0])

            ang, turns, red = rope["ang"][:], rope["turns"][:], rope["red"][:]
            input_panel(0, None)
            step(nc.vector.tensor_copy(ang, rope["pos"][:]), rot["steps"])
            step(nc.vector.tensor_scalar(ang, ang, column("inv_freq"), None, ALU.mult), rot["steps"])
            step(nc.vector.tensor_scalar(turns, ang, 1.0 / TWO_PI, ROUNDER, ALU.mult, ALU.add), rot["steps"])
            step(nc.vector.tensor_scalar(turns, turns, -ROUNDER, None, ALU.add), rot["steps"])
            step(nc.vector.scalar_tensor_tensor(out=red, in0=turns, scalar=-TURN_1, in1=ang, op0=ALU.mult, op1=ALU.add), rot["steps"])
            input_panel(1, None)
            for part in (TURN_2, TURN_3, TURN_4):
                step(nc.vector.scalar_tensor_tensor(out=red, in0=turns, scalar=-part, in1=red, op0=ALU.mult, op1=ALU.add), rot["steps"])
            step(nc.vector.tensor_scalar(red, red, PI_BELOW, -PI_BELOW, ALU.min, ALU.max), rot["steps"])
            step(nc.vector.scalar_tensor_tensor(out=ang, in0=red, scalar=-1.0, in1=red, op0=ALU.mult, op1=ALU.max), rot["steps"])
            step(nc.vector.tensor_scalar(ang, ang, -1.0, math.pi / 2, ALU.mult, ALU.add), rot["steps"])
            with dve.Fori(1, 4) as i:
                for s in range(2):
                    input_panel(s, i)
            dve.wait_ge(lams["exps"], 1)
            nc.vector.tensor_scalar(lam[:], lam_exp[:, 0:1], lam_exp[:, 1:2], LAMBDA_INIT, ALU.subtract,
                                    ALU.add).then_inc(lams["done"], 1)

            counted[0] = 0
            g1, g2, g3, g4 = (t[0:N_FORGET, :] for t in (rope["g1"], rope["g2"], rope["g3"], rope["g4"]))

            def gate_steps(p):
                if p == 0:
                    step(nc.vector.tensor_scalar(g3, g2, 2.0, None, ALU.add), gate["steps"])
                    step(nc.vector.reciprocal(g1, g3), gate["steps"])
                if p == 1:
                    step(nc.vector.tensor_tensor(g3, g2, g1, ALU.mult), gate["steps"])
                    step(nc.vector.tensor_tensor(g4, g3, g3, ALU.mult), gate["steps"])
                if p == 2:
                    step(nc.vector.tensor_scalar(g1, g4, 1.0 / 15, None, ALU.mult), gate["steps"])
                if 2 <= p < 5:
                    for k in (13 - 4 * (p - 2), 11 - 4 * (p - 2)):
                        step(nc.vector.scalar_tensor_tensor(out=g1, in0=g1, scalar=1.0 / k, in1=g4, op0=ALU.add,
                                                            op1=ALU.mult), gate["steps"])
                if p == 5:
                    step(nc.vector.scalar_tensor_tensor(out=g1, in0=g1, scalar=1.0, in1=g3, op0=ALU.add, op1=ALU.mult),
                         gate["steps"])
                    step(nc.vector.tensor_scalar(g2, mix["proj"][0:N_FORGET, 0, :], column("b_forget", 0, slice(0, N_FORGET)),
                                                 0.0, ALU.add, ALU.min), gate["steps"])
                if p == 6:
                    step(nc.vector.scalar_tensor_tensor(out=g2, in0=g1, scalar=-2.0, in1=g2, op0=ALU.mult, op1=ALU.add),
                         gate["steps"])
                    step(nc.vector.memset(g3, 1.0), gate["steps"])
                if p == 7:
                    nc.vector.tensor_tensor_scan(mix["c_rows"][0:N_FORGET, :], g3, g2, 0.0, ALU.mult, ALU.add).then_inc(gate["c"], 1)

            dve.wait_ge(gate["exp"], 1)
            for p in range(8):
                dve.wait_ge(used, u0 + 10 + p)
                scaled(mix["proj"][:, 9 + p, :], 1 - p % 2, w_in["evacuated"])
                split(u0 + 11 + p)
                gate_steps(p)
            dve.wait_ge(rot["trig"], 2)
            for c in range(4):
                if c % 2 == 0:
                    split(u0 + 19 + c // 2)
                pc = mix["proj"][:, 9 + c, :]
                dve.wait_ge(rot["swapped"], c + 1)
                if c:
                    dve.wait_ge(rot["done"], c)
                nc.vector.tensor_tensor(rope["prod"][:], ps[:, 2 + c % 2, :], rope["sin"][:], ALU.mult).then_inc(rot["prod"], 1)
                nc.vector.tensor_tensor(pc, pc, rope["cos"][:], ALU.mult).then_inc(rot["prod_cos"], 1)
                dve.wait_ge(rot["prod_cos"], c + 1)
                dve.wait_ge(rot["prod"], c + 1)
                nc.vector.tensor_tensor(pc, pc, rope["prod"][:], ALU.add).then_inc(rot["done"], 1)
            for c in range(GC):
                dve.wait_ge(small["hi"], c + 1)
                nc.vector.tensor_tensor(mix["lo"][:, c, :], mix["proj"][:, 1 + c, :], mix["hi"][:, c, :].bitcast(F32),
                                        ALU.subtract).then_inc(mix_ready, 1)
            for c in range(GC):
                dve.wait_ge(small["hi"], GC + c + 1)
                nc.vector.scalar_tensor_tensor(out=mix["lo"][:, GC + c, :], in0=ps[:, c, :], scalar=column("pool_scale", c),
                                               in1=mix["hi"][:, GC + c, :].bitcast(F32), op0=ALU.mult,
                                               op1=ALU.subtract).then_inc(mix_ready, 1)
            split(u0 + 21)
            dve.wait_ge(used, u0 + 21)
            for b in range(TB):
                nc.vector.tensor_scalar(mix["v"][:, b, :], ps[:, 4 + b, :], r_rows[:, b:b + 1], None,
                                        ALU.mult).then_inc(w_in["v_ready"], 1)
            split(u0 + 22)

            dve.wait_ge(rot["done"], 4)
            dve.wait_ge(w_in["v_ready"], TB)

            def stage_part(g, n_split, name, src, scale):
                dve.wait_ge(a1["staged_hi"], n_split)
                hi, lo = (at1[f"{name}{half}{g % 2}"].rearrange("p (a n) -> p a n", a=src.shape[1]) for half in ("hi", "lo"))
                if scale is None:
                    return nc.vector.tensor_tensor(lo, src, hi.bitcast(F32), ALU.subtract)
                return nc.vector.scalar_tensor_tensor(out=lo, in0=src, scalar=scale, in1=hi.bitcast(F32), op0=ALU.mult,
                                                      op1=ALU.subtract)

            def stage_qk(g):
                s, c = g % 2, g // 2
                stage_part(g, 3 * g + 1, "q", mix["proj"][:, 9 + 4 * s + c:10 + 4 * s + c, :], -HD ** -0.5)
                stage_part(g, 3 * g + 2, "k", mix["proj"][:, 11 + 4 * s + c:12 + 4 * s + c, :], None).then_inc(a1["staged"], 1)

            def stage_v(g):
                s, c = g % 2, g // 2
                stage_part(g, 3 * g + 3, "v", mix["v"][:, :, G * s + c * P:G * s + (c + 1) * P], None).then_inc(a1["v_staged"], 1)

            def least(t):
                b = t % 8 // 2
                w = P * (b + 1)
                if t >= 3:
                    dve.wait_ge(a1["turned"], t - 2)
                if t // 8 % 2:
                    dve.wait_ge(a1["bias"], t // 16 * 8 + t % 8 + 1)
                    bias = mix["proj"][:, 5 + t % 2, 0:w]
                else:
                    dve.wait_ge(loads["tables"], 16 * N_TABLES)
                    bias = mix["dil"][:, S - P - b * P:S - P - b * P + w]
                dve.wait_ge(a1["scores"], t + 1)
                nc.vector.tensor_tensor_reduce(at1["e"][:, t % 3, 0:w], ps[:, t % 2, 0:w], bias, 1.0, FAR, ALU.add,
                                               ALU.min, at1["least"][:, t % 3:t % 3 + 1]).then_inc(a1["least"], 1)

            def probs(t):
                w = P * (t % 8 // 2 + 1)
                k = t % 3
                dve.wait_ge(a1["exps"], t + 1)
                nc.vector.reciprocal(at1["inv"][:, k:k + 1], at1["sums"][:, k:k + 1]).then_inc(a1["inv"], 1)
                dve.wait_ge(a1["inv"], t + 1)
                nc.vector.tensor_scalar(at1["e"][:, k, 0:w], at1["e"][:, k, 0:w], at1["inv"][:, k:k + 1], None,
                                        ALU.mult).then_inc(a1["probs"], 1)

            def lo(t):
                w = P * (t % 8 // 2 + 1)
                dve.wait_ge(a1["pt_hi"], t + 1)
                nc.vector.tensor_tensor(at1["pt_lo"][:, t % 2, 0:w], ps[:, 2 + t % 2, 0:w],
                                        at1["pt_hi"][:, t % 2, 0:w].bitcast(F32), ALU.subtract).then_inc(a1["pt"], 1)

            def output(g):
                dve.wait_ge(a1["out_hi"], 2 * g + 2)
                for h in range(2):
                    rows = slice(HD * h, HD * h + HD)
                    ins = nc.vector.tensor_tensor(mix["lo"][rows, 4 + g, :], ps[rows, 4 + h, :], mix["hi"][rows, 4 + g, :].bitcast(F32),
                                                  ALU.subtract)
                ins.then_inc(mix_ready, 1)

            def memory_in(c):
                dve.wait_ge(mem["hi"], c + 1)
                nc.vector.scalar_tensor_tensor(out=mem_split(xg_lo, c), in0=mem_input(c), scalar=column("g_mem", c),
                                               in1=mem_split(xg_hi, c).bitcast(F32), op0=ALU.mult,
                                               op1=ALU.subtract).then_inc(mem["lo"], 1)

            def memory_out(t):
                if t == 2:
                    dve.wait_ge(mem["rms"], 2)
                    nc.vector.reciprocal(memory["r_cols"][:], memory["rms"][:]).then_inc(mem["r"], 1)
                    nc.vector.reciprocal(memory["r_rows"][:], memory["rms_rows"][:]).then_inc(mem["r"], 1)
                    dve.wait_ge(mem["r"], 2)
                m = t // 2 - 1
                if t % 2 == 0 and 0 <= m < KC:
                    dve.wait_ge(used, FIRST["mem_k"] + m + 1)
                    scaled(xa["k"][:, m, :], 6 + m % 2, mem["k_ready"], M, memory["r_cols"][:])
                if t % 2 == 0 and 0 <= m < 2 * KC:
                    split(FIRST["mem_k"] + m + 2)

            stage_qk(0)
            stage_v(0)
            for t in range(MIX_ITEMS + 6):
                if t % 8 == 5 and t > 8:
                    output(t // 8 - 1)
                if t < MIX_ITEMS:
                    least(t)
                if 0 <= t - 2 < MIX_ITEMS:
                    probs(t - 2)
                if 0 <= t - 4 < MIX_ITEMS:
                    lo(t - 4)
                g = t // 8 + 1
                if t % 8 == 1 and g < 2 * GC:
                    stage_qk(g)
                if t % 8 == 6 and g < 2 * GC:
                    stage_v(g)
                if t < KC // 2:
                    memory_in(2 * t)
                    memory_in(2 * t + 1)
                memory_out(t - MEM_LAG)

            u0 = FIRST["w_out"]
            for u in range(u0 + 2, u0 + KC + 1):
                split(u)
            into_residual("w_out", KC, "xa", "g_xa", 0, False)
            norm_r("xa")
            u0 = FIRST["xq"]

            def query_panel(p, bank):
                dve.wait_ge(used, u0 + p + 1)
                scaled(xa["q"][:, p, :], bank, xqs["ready"])

            for p in range(XC):
                query_panel(p, p)
                split(u0 + p + 2)

            def stage_part(g, n_split, name, src, scale):
                dve.wait_ge(a2["staged_hi"], n_split)
                hi, lo = (at2[f"{name}{half}{g % 2}"][:].rearrange("p (a n) -> p a n", a=src.shape[1]) for half in ("hi", "lo"))
                if scale is None:
                    return nc.vector.tensor_tensor(lo, src, hi.bitcast(F32), ALU.subtract)
                return nc.vector.scalar_tensor_tensor(out=lo, in0=src, scalar=scale, in1=hi.bitcast(F32), op0=ALU.mult,
                                                      op1=ALU.subtract)

            def stage_qk(g):
                stage_part(g, 3 * g + 1, "k", xa["k"][:, XC * g:XC * (g + 1), :], None)
                stage_part(g, 3 * g + 2, "q", xa["q"][:, XC * g:XC * (g + 1), :], -(XC * P) ** -0.5).then_inc(a2["staged"], 1)

            def stage_v(g):
                stage_part(g, 3 * g + 3, "v", xa["v"][:, :, XC * P * g:XC * P * (g + 1)], None).then_inc(a2["v_staged"], 1)

            def least(t):
                dve.wait_ge(a2["scores"], t + 1)
                nc.vector.tensor_reduce(at2["least"][:, t % 3:t % 3 + 1], ps[:, t % 2, 0:M], AX.X, ALU.min).then_inc(a2["least"], 1)

            def probs(t):
                k = t % 3
                dve.wait_ge(a2["exps"], t + 1)
                nc.vector.reciprocal(at2["inv"][:, k:k + 1], at2["sums"][:, k:k + 1]).then_inc(a2["inv"], 1)
                dve.wait_ge(a2["inv"], t + 1)
                nc.vector.tensor_scalar(at2["e"][:, k, :], at2["e"][:, k, :], at2["inv"][:, k:k + 1], None,
                                        ALU.mult).then_inc(a2["probs"], 1)

            def lo(t):
                h, b = t // TB, t % TB
                dve.wait_ge(a2["pt_hi"], t + 1)
                hi_, lo_ = (at2[name][:, h % 2, :].rearrange("p (j n) -> p j n", j=MB)[:, :, b * P:(b + 1) * P]
                            for name in ("pt_hi", "pt_lo"))
                nc.vector.tensor_tensor(lo_, ps[:, 2 + t % 2, 0:M].rearrange("p (j n) -> p j n", j=MB), hi_.bitcast(F32),
                                        ALU.subtract).then_inc(a2["pt"], 1)

            def output(h):
                for d in range(XC):
                    dve.wait_ge(a2["out_hi"], XC * h + d + 1)
                    nc.vector.tensor_tensor(xa["lo"][:, XC * h + d, :], ps[:, 4 + d, :], xa["hi"][:, XC * h + d, :].bitcast(F32),
                                            ALU.subtract).then_inc(a2["out"], 1)

            stage_qk(0)
            stage_v(0)
            query_panel(XC, XC)
            split(u0 + XC + 2)
            for t in range(XA_ITEMS + 6):
                panel_out = t % 2 == 0 and 0 < t <= 2 * (KC - XQ_FIRST)
                if panel_out:
                    query_panel(XQ_FIRST + t // 2 - 1, 6 + (t // 2 - 1) % 2)
                if t % TB == 1 and t > 2 * TB:
                    output(t // TB - 2)
                if t < XA_ITEMS:
                    least(t)
                if 0 <= t - 2 < XA_ITEMS:
                    probs(t - 2)
                if 0 <= t - 4 < XA_ITEMS:
                    lo(t - 4)
                if t % TB == 2 and t // TB + 1 < XA_HEADS:
                    stage_qk(t // TB + 1)
                if t % TB == 1 and 0 < t // TB < XA_HEADS:
                    stage_v(t // TB)
                if panel_out:
                    split(u0 + XQ_FIRST + t // 2 + 1)
            into_residual("xo", KC, "ffn", "g_ffn", 0)

            st = ffn_stages["up"]
            nc.vector.memset(ffn["ua"][:, 0:2], 0.0).then_inc(st["zero"], 1)
            nc.vector.memset(ffn["ug"][:, 0:2], 0.0).then_inc(st["zero"], 1)
            norm_r("ffn")
            dve.wait_ge(st["zero"], 2)
            def conv_product(i, done):
                dve.wait_ge(st["gated"], at(done + 1, i, 1))
                nc.vector.tensor_tensor(ffn["h"][:], ffn["ta"][:], ffn["gate"][:], ALU.mult).then_inc(st["product"], 1)

            def conv_lo(i, done):
                dve.wait_ge(st["hid_hi"], at(done + 1, i, 1))
                nc.vector.tensor_tensor(chunk(ffn["lo"], at(done, i, 1)), ffn["h"][:],
                                        chunk(ffn["hi"], at(done, i, 1)).bitcast(F32), ALU.subtract).then_inc(st["hid"], 1)

            def conv_taps(i, s, src, to):
                dve.wait_ge(st["tapped"], at(s + 1, i, 2))
                dve.wait_ge(st["scaled"], at(s + 1, i, 2))
                for k in (1, 0):
                    nc.vector.scalar_tensor_tensor(out=to[:], in0=src[:, k:S + k],
                                                   scalar=column("w_ffconv", at(k * 2 * FC + s * FC, i, 1)),
                                                   in1=to[:], op0=ALU.mult, op1=ALU.add).then_inc(st["steps"], 1)
                    dve.wait_ge(st["steps"], at(2 * s + 2 - k, i, 4))

            def conv_turn(i, first):
                u = FIRST["up"]
                dve.wait_ge(used, at(u + 1, i, 2))
                scaled(ffn["ua"][:, 2:S + 2], 0, st["scaled"])
                split(u + 2, i)
                if not first:
                    conv_product(i, -1)
                dve.wait_ge(used, at(u + 2, i, 2))
                scaled(ffn["ug"][:, 2:S + 2], 1, st["scaled"])
                split(u + 3, i)
                conv_taps(i, 0, ffn["ua"], ffn["ta"])
                if not first:
                    conv_lo(i, -1)
                conv_taps(i, 1, ffn["ug"], ffn["tg"])

            conv_turn(None, True)
            with dve.Fori(1, FC) as i:
                conv_turn(i, False)
            conv_product(None, FC - 1)
            conv_lo(None, FC - 1)
            into_residual("down", FC, "first", "a_gain", 2)

            dve.wait_ge(loads["spatial"], 2 * 16)
            for g in range(N_SPATIAL):
                wg = sg["w"][:, g * P:(g + 1) * P]
                ins = nc.vector.tensor_tensor(wg, wg, con[:, CAT["keep"]:CAT["keep"] + P], ALU.mult)
            ins.then_inc(a_in["w"], 1)
            u0 = FIRST["a_v"]
            split(u0 + 2)
            split(u0 + 3)
            dve.wait_ge(rms_ready, NORM["first"] + 1)
            nc.vector.reciprocal(first["r"][:], square_sum[:]).then_inc(r_ready, 1)
            dve.wait_ge(rows_rms_ready, ROWS["first"] + 1)
            nc.vector.reciprocal(first["r_rows"][:], rms_rows[:]).then_inc(rows_ready, 1)
            dve.wait_ge(r_ready, NORM["first"] + 1)
            dve.wait_ge(rows_ready, ROWS["first"] + 1)
            dve.wait_ge(sums_ready, NORM["a"] + 1)
            dve.wait_ge(rows_sums_ready, ROWS["a"] + 1)
            for k, (src, to, to_rows) in enumerate(((ps[:, 0, :], first["sums"], first["sums_rows"]),
                                                    (first["sums"][:], first["sums"], first["sums_rows"]))):
                if k:
                    dve.wait_ge(a_in["first"], 2 * k)
                nc.vector.tensor_tensor(to[:], src, first["r"][:], ALU.mult).then_inc(a_in["first"], 1)
                nc.vector.tensor_tensor(to_rows[:], to_rows[:] if k else ps[:, 1, 0:TB], first["r_rows"][:],
                                        ALU.mult).then_inc(a_in["first"], 1)
            split(u0 + 4)
            dve.wait_ge(rms_ready, NORM["a"] + 1)
            nc.vector.reciprocal(first["sums"][:], first["sums"][:]).then_inc(a_in["first"], 1)
            dve.wait_ge(rows_rms_ready, ROWS["a"] + 1)
            nc.vector.reciprocal(first["sums_rows"][:], first["sums_rows"][:]).then_inc(a_in["first"], 1)
            dve.wait_ge(a_in["first"], 6)
            nc.vector.tensor_tensor(r_cols[:], first["sums"][:], first["r"][:], ALU.mult).then_inc(r_ready, 1)
            nc.vector.tensor_tensor(r_rows[:], first["sums_rows"][:], first["r_rows"][:], ALU.mult).then_inc(rows_ready, 1)
            dve.wait_ge(r_ready, NORM["a"] + 1)
            for u in range(u0 + 5, u0 + KC + 2):
                split(u)
            dve.wait_ge(a_in["v"], 2 * TB)
            nc.vector.tensor_tensor(sg["mean"][:], sg["v_sum"][:, :, 0], sg["v_sum"][:, :, 1], ALU.add).then_inc(a_in["steps"], 1)
            dve.wait_ge(a_in["steps"], 1)
            nc.vector.tensor_scalar(sg["mean"][:], sg["mean"][:], -1.0 / D, None, ALU.mult).then_inc(a_in["steps"], 1)
            u0 = FIRST["a_u"]

            def gate_panel(s, i):
                dve.wait_ge(used, at(u0 + 1 + s, i, 2))
                scaled(chunk(sg["u"], at(s, i, 2)), 2 + s, a_in["scaled"])
                split(u0 + 2 + s, i)

            gate_panel(0, None)
            dve.wait_ge(a_in["std"], 1)
            nc.vector.reciprocal(sg["r"][:], sg["std"][:]).then_inc(a_in["steps"], 1)
            gate_panel(1, None)
            dve.wait_ge(a_in["steps"], 3)

            def normed(b):
                nc.vector.tensor_scalar(sg["v"][:, b, :], sg["v"][:, b, :], sg["mean"][:, b:b + 1], sg["r"][:, b:b + 1], ALU.add,
                                        ALU.mult).then_inc(a_in["normed"], 1)

            def v_lo(b):
                dve.wait_ge(a_in["v_hi"], b + 1)
                nc.vector.tensor_tensor(sg["v_lo"][:, b, :], sg["v"][:, b, :], sg["v_hi"][:, b, :].bitcast(F32),
                                        ALU.subtract).then_inc(a_in["v_lo"], 1)

            normed(0)
            for b in range(TB):
                if b < TB - 1:
                    normed(b + 1)
                gate_panel(b % 2, 1 + b // 2)
                v_lo(b)
            dve.wait_ge(a_in["w_hi"], 1)
            nc.vector.tensor_tensor(sg["w_lo"][:], sg["w"][:], sg["w_hi"][:].bitcast(F32), ALU.subtract).then_inc(a_in["w_lo"], 1)
            for p in range(TB, KC - 2):
                gate_panel(p % 2, 1 + p // 2)
            dve.wait_ge(loads["spatial"], 2 * 16)
            dve.wait_ge(a_in["u"], KC)
            for g in range(N_SPATIAL + 1):
                if g < N_SPATIAL:
                    dve.wait_ge(a_in["z_done"], g + 1)
                    if g:
                        dve.wait_ge(a_in["product"], g)
                    nc.vector.scalar_tensor_tensor(
                        out=sg["z"][:].rearrange("p (b t) -> p b t", b=TB),
                        in0=ps[:, 4 + g % 2, :].rearrange("p (b t) -> p b t", b=TB), scalar=column("a_v_norm", g),
                        in1=sg["b"][:, g, :].unsqueeze(1).to_broadcast([P, TB, P]), op0=ALU.mult, op1=ALU.add).then_inc(a_in["z"], 1)
                    dve.wait_ge(a_in["z"], g + 1)
                    nc.vector.tensor_tensor(sg["u"][:, g, :], sg["u"][:, g, :], sg["z"][:], ALU.mult).then_inc(a_in["product"], 1)
                if g:
                    dve.wait_ge(a_in["hi"], g)
                    nc.vector.tensor_tensor(sg["lo"][:, g - 1, :], sg["u"][:, g - 1, :], sg["hi"][:, g - 1, :].bitcast(F32),
                                            ALU.subtract).then_inc(a_in["ready"], 1)
            for c in range(KC):
                nc.vector.scalar_tensor_tensor(out=x[:, c, :], in0=x[:, c, :], scalar=column("g_first", c), in1=first["r"][:],
                                               op0=ALU.mult, op1=ALU.mult).then_inc(x_ready, 1)
            dve.wait_ge(x_ready, KC * NORM["a"])
            into_residual("a_out", KC, "ffn0", "ffn_norm0", 0)

            def swiglu(name, norm, base):
                st = ffn_stages[name]
                norm_r(norm)
                u0 = FIRST[name]
                with dve.Fori(0, FC) as i:
                    for s, to in enumerate((ffn["tg"], ffn["ta"])):
                        dve.wait_ge(used, at(u0 + 1 + s, i, 2))
                        scaled(to[:], base + s, st["scaled"])
                        split(u0 + 2 + s, i)
                    dve.wait_ge(st["gated"], at(1, i, 1))
                    dve.wait_ge(st["scaled"], at(2, i, 2))
                    nc.vector.tensor_tensor(ffn["h"][:], ffn["ta"][:], ffn["gate"][:], ALU.mult).then_inc(st["product"], 1)
                    dve.wait_ge(st["hid_hi"], at(1, i, 1))
                    nc.vector.tensor_tensor(chunk(ffn["lo"], at(0, i, 1)), ffn["h"][:], chunk(ffn["hi"], at(0, i, 1)).bitcast(F32),
                                            ALU.subtract).then_inc(st["hid"], 1)

            swiglu("gu0", "ffn0", 0)
            into_residual("down0", FC, "kv", "kv_norm", 2)

            nc.vector.memset(da["zero"][:], 0.0).then_inc(kv["zero"], 1)
            u0 = FIRST["kv_v"]
            split(u0 + 2)
            norm_r("kv", True)
            for u in range(u0 + 1, u0 + KC):
                split(u + 2)
                for c in range(2 * (u - u0 - 4), 2 * (u - u0 - 4) + 2):
                    if c >= 0:
                        dve.wait_ge(kv["xb_hi"], c + 1)
                        nc.vector.scalar_tensor_tensor(out=da["xb_lo"][:, c, :], in0=x[:, c, :], scalar=column("b_norm", c),
                                                       in1=da["xb_hi"][:, c, :].bitcast(F32), op0=ALU.mult,
                                                       op1=ALU.subtract).then_inc(kv["xb"], 1)
            qk0 = FIRST["qk"]

            def panel_out(p, i, bank):
                dve.wait_ge(used, at(qk0 + p + 1, i, 4))
                if p >= 2:
                    dve.wait_ge(a3["staged"], at(p - 1, i, 4))
                if p % 2:
                    nc.vector.scalar_tensor_tensor(out=da["q"], in0=ps[:, bank, :], scalar=-HD ** -0.5, in1=r_cols[:],
                                                   op0=ALU.mult, op1=ALU.mult).then_inc(kv["qk"], 1)
                else:
                    scaled(da["k"], bank, kv["qk"])

            for p in range(EARLY_PANELS):
                panel_out(p, None, 2 + p)
                split(qk0 + p + 2)
            dve.wait_ge(lams["done"], 1)

            def diff_item(n, c, base):
                def least(n):
                    s, b = n // TB, n % TB
                    w = P * (b + 1)
                    if c is not None or n + base >= DIFF_SLOTS:
                        dve.wait_ge(a3["turned"], at(base + n + 1 - DIFF_SLOTS, c, 8))
                    if b == 0:
                        dve.wait_ge(a3["bias"], at(base // TB + s + 1, c, 2))
                    for h in range(2):
                        k = 2 * (n % DIFF_SLOTS) + h
                        half = dve.to_reg(at(2 * (base + n) + h + 1, c, 16))
                        dve.wait_ge(loads["alibi"], 16)
                        dve.wait_ge(a3["scores"], half)
                        nc.vector.tensor_tensor_reduce(at3["e"][:, k, 0:w], ps[:, 2 * (n % 2) + h, 0:w],
                                                       da["bias"][:, s % 2, S - P - b * P:S - P - b * P + w], 1.0, FAR,
                                                       ALU.add, ALU.min, at3["least"][:, k:k + 1]).then_inc(a3["least"], 1)

                def inverse(n):
                    k = 2 * (n % DIFF_SLOTS)
                    dve.wait_ge(a3["exps"], at(2 * (base + n) + 2, c, 16))
                    nc.vector.reciprocal(at3["inv"][:, k:k + 2], at3["sums"][:, k:k + 2]).then_inc(a3["inv"], 1)
                    dve.wait_ge(a3["inv"], at(base + n + 1, c, 8))
                    nc.vector.tensor_scalar(at3["second"][:, k + 1:k + 2], at3["inv"][:, k + 1:k + 2], lam[:, 0:1], None,
                                            ALU.mult).then_inc(a3["second"], 1)

                def probs(n):
                    w = P * (n % TB + 1)
                    k = 2 * (n % DIFF_SLOTS)
                    dve.wait_ge(a3["weighed"], at(base + n + 1, c, 8))
                    nc.vector.scalar_tensor_tensor(out=at3["e"][:, k, 0:w], in0=at3["e"][:, k, 0:w],
                                                   scalar=at3["inv"][:, k:k + 1], in1=at3["e"][:, k + 1, 0:w], op0=ALU.mult,
                                                   op1=ALU.subtract).then_inc(a3["probs"], 1)

                def lo(n):
                    w = P * (n % TB + 1)
                    dve.wait_ge(a3["pt_hi"], at(base + n + 1, c, 8))
                    nc.vector.tensor_tensor(at3["pt_lo"][:, n % 2, 0:w], ps[:, 4 + n % 2, 0:w],
                                            at3["pt_hi"][:, n % 2, 0:w].bitcast(F32), ALU.subtract).then_inc(a3["pt"], 1)

                if qk_due(n, c, base):
                    panel_out(EARLY_PANELS - 1 + (base + n) // 2, c, 7)
                if live(n, c, base):
                    least(n)
                if live(n - 2, c, base):
                    inverse(n - 2)
                if live(n - 3, c, base):
                    probs(n - 3)
                if live(n - 5, c, base):
                    lo(n - 5)
                if qk_due(n, c, base):
                    u = qk0 + EARLY_PANELS - 1 + (base + n) // 2 + 2
                    dve.wait_ge(w_hi_ready, at(u + 1, c, 4))
                    nc.vector.tensor_tensor(w_lo[:, u % 2, :], w_raw[:, u % 2, :], w_hi[:, u % 2, :].bitcast(F32),
                                            ALU.subtract).then_inc(w_ready, 1)

            diff_turns(dve, diff_item, 5)
            dve.wait_ge(a3["rms"], 1)
            nc.vector.reciprocal(da["rms"], da["rms"]).then_inc(a3["rms"], 1)
            for h in range(N_DIFF + 1):
                if h < N_DIFF:
                    dve.wait_ge(a3["spread"], h + 1)
                    nc.vector.scalar_tensor_tensor(out=da["o"][:, h, :], in0=da["o"][:, h, :], scalar=subln[:, 0:1],
                                                   in1=ps[:, h % 4, :], op0=ALU.mult, op1=ALU.mult).then_inc(a3["normed"], 1)
                if h:
                    dve.wait_ge(a3["out_hi"], h)
                    nc.vector.tensor_tensor(xg_lo[:, h - 1, :], da["o"][:, h - 1, :], xg_hi[:, h - 1, :].bitcast(F32),
                                            ALU.subtract).then_inc(a3["out_lo"], 1)
            into_residual("bo", KC, "ffn1", "ffn_norm1", 4)
            swiglu("gu1", "ffn1", 4)
            into_residual("down1", FC, "final", None, 6)
            dve.wait_ge(rms_ready, NORM["final"] + TB // 2)
            nc.vector.reciprocal(r_rows[:], rms_rows[:]).then_inc(finals["r_rows"], 1)
            dve.wait_ge(finals["r_rows"], 1)
            for b in range(TB):
                nc.vector.tensor_scalar(final["diagonal"][:, b * P:(b + 1) * P], ident, r_rows[:, b:b + 1], None,
                                        ALU.mult).then_inc(finals["diagonal"], 1)
            dve.wait_ge(finals["spread"], 1)
            for c in range(KC):
                nc.vector.scalar_tensor_tensor(out=result[:, c, :], in0=x[:, c, :], scalar=column("g_final", c), in1=ps[:, 2, :],
                                               op0=ALU.mult, op1=ALU.mult).then_inc(finals["scaled"], 1)

        @block.gpsimd
        def _(pool):
            def sum_squares(norm, sums=square_sum):
                n = NORM[norm]
                for c in range(KC):
                    k = KC * n + c
                    pool.wait_ge(sq_ready, k + 1)
                    if c == 0:
                        nc.gpsimd.tensor_copy(sums[:], squares[:, 0, :]).then_inc(summed, 1)
                    else:
                        pool.wait_ge(summed, k)
                        nc.gpsimd.tensor_tensor(sums[:], sums[:], squares[:, c % 2, :], ALU.add).then_inc(summed, 1)

            pool.wait_ge(loads["input"], 2 * 16)
            pool.dma_start(rope["pos"][:], positions).then_inc(loads["early"], 16)
            pool.dma_start(lam_in[:], lambdas).then_inc(loads["early"], 16)
            pool.dma_start(rope["pool_w"][:], pool_blocks).then_inc(loads["tables"], 16)
            pool.dma_start(rope["heads"][:], head_rows).then_inc(loads["tables"], 16)
            pool.dma_start(mix["dil"][:], dil_table).then_inc(loads["tables"], 16)
            sum_squares("mix")

            counted = [0]

            def step(ins):
                counted[0] += 1
                ins.then_inc(small["steps"], 1)
                pool.wait_ge(small["steps"], counted[0])

            step(nc.gpsimd.memset(rope["pad"][:, 0:16], 0.0))
            u = rope["pad"]
            for c in range(GC):
                pool.wait_ge(w_in["evacuated"], 4 + 3 * c)
                h_, b_, c_ = (mix["proj"][:, 1 + 3 * c + k, :] for k in range(3))
                step(nc.gpsimd.tensor_tensor(u[:, 16:], c_, h_, ALU.mult))
                step(nc.gpsimd.tensor_scalar(rope["win"][:, 0:S], u[:, 16:], column("w_sconv", 2 * GC + c), None, ALU.mult))
                for k in (1, 0):
                    step(nc.gpsimd.tensor_scalar(rope["win2"][:, 0:S], u[:, 14 + k:14 + k + S], column("w_sconv", k * GC + c),
                                                 None, ALU.mult))
                    step(nc.gpsimd.tensor_tensor(rope["win"][:, 0:S], rope["win"][:, 0:S], rope["win2"][:, 0:S], ALU.add))
                counted[0] += 1
                nc.gpsimd.tensor_tensor(mix["proj"][:, 1 + c, :], b_, rope["win"][:, 0:S], ALU.mult).then_inc(small["steps"], 1)
                pool.wait_ge(small["steps"], counted[0])
                pool.sem_inc(small["conv"], 1)
            for c in range(GC):
                pool.wait_ge(w_in["evacuated"], 8 + c)
                s1, s2 = rope["win"], rope["win2"]
                step(nc.gpsimd.tensor_copy(u[:, 16:], mix["proj"][:, 7 + c, :]))
                step(nc.gpsimd.tensor_tensor(s1[:, 1:], u[:, 1:], u[:, 0:S + 15], ALU.add))
                step(nc.gpsimd.tensor_tensor(s2[:, 3:], s1[:, 3:], s1[:, 1:S + 14], ALU.add))
                if c:
                    step(nc.gpsimd.tensor_tensor(s1[:, 7:], s2[:, 7:], s2[:, 3:S + 12], ALU.add))
                    step(nc.gpsimd.tensor_tensor(s2[:, 15:], s1[:, 15:], s1[:, 7:S + 8], ALU.add))
                for h, t in enumerate((s1, s2)):
                    rows = slice(HD * h, HD * h + HD)
                    step(nc.gpsimd.tensor_scalar(rope["z"][rows, c, :], t[rows, 16:], column("inv_window", c, rows), None, ALU.mult))
                    step(nc.gpsimd.tensor_tensor(rope["z"][rows, c, 0:16], t[rows, 16:32],
                                                 con[rows, CAT["inv_count"] + 16 * c:CAT["inv_count"] + 16 * c + 16], ALU.mult))
                counted[0] += 1
                nc.gpsimd.tensor_tensor(rope["z"][:, c, :], rope["z"][:, c, :], u[:, 16:], ALU.subtract).then_inc(small["steps"], 1)
                pool.wait_ge(small["steps"], counted[0])
                pool.sem_inc(small["pooled"], 1)

            for c in range(KC):
                pool.wait_ge(mem["sq"], c + 1)
                if c == 0:
                    nc.gpsimd.tensor_copy(memory["acc"][:], memory["sq"][:, 0, :]).then_inc(mem["summed"], 1)
                else:
                    pool.wait_ge(mem["summed"], c)
                    nc.gpsimd.tensor_tensor(memory["acc"][:], memory["acc"][:], memory["sq"][:, c % 2, :], ALU.add).then_inc(mem["summed"], 1)
            pool.wait_ge(gate["rows"], 1 + N_FORGET)
            with pool.Fori(0, GC) as c:
                for m in range(8):
                    b, h = m // 2, m % 2
                    w = P * (b + 1)
                    pool.wait_ge(a1["least"], at(8 + m - 1 if m >= 2 else 1, c, 16))
                    to = mix["proj"][:, 5 + m % 2, 0:w]
                    nc.gpsimd.tensor_tensor(to, mix["proj"][:, bass.ds(1 + h + c * 2, 1), 0:w].rearrange("p a n -> p (a n)"),
                                            mix["nci"][:, b, bass.ds(h + c * 2, 1)].to_broadcast([P, w]), ALU.add).then_inc(a1["bias_steps"], 1)
                    pool.wait_ge(a1["bias_steps"], at(m + 1, c, 8))
                    to = mix["proj"][:, 5 + m % 2, w - P:w]
                    nc.gpsimd.tensor_tensor(to, to, causal, ALU.add).then_inc(a1["bias"], 1)

            sum_squares("xa")
            for norm in ("ffn", "first", "ffn0", "kv"):
                sum_squares(norm)
                if norm == "first":
                    sum_squares("a", first["sums"])
            pool.wait_ge(loads["alibi"], 16)
            pool.wait_ge(kv["zero"], 1)
            pool.wait_ge(kv["v"], 8)

            def parts_of(set_, n_split, c, *parts):
                for k, (name, src) in enumerate(parts):
                    n = src.shape[1]
                    hi, lo = (at3[f"{name}{half}{set_}"][:].rearrange("p (a n) -> p a n", a=n) for half in ("hi", "lo"))
                    nc.gpsimd.tensor_tensor(hi, src, da["zero"][:].unsqueeze(2).to_broadcast(src.shape),
                                            ALU.add).then_inc(a3["staged_hi"], 1)
                    split_ = pool.to_reg(at(n_split + k + 1, c, 6))
                    pool.wait_ge(kv["zero"], 1)
                    pool.wait_ge(a3["staged_hi"], split_)
                    ins = nc.gpsimd.tensor_tensor(lo, src, hi.bitcast(F32), ALU.subtract)
                return ins

            def stage_qk(s, c):
                first_pair = c is None
                if not first_pair:
                    pool.wait_ge(a3["scores"], at(8 * (s - 1), c, 16))
                for k, name in enumerate(("k", "q")):
                    pool.wait_ge(kv["qk"], at(2 * s + k + 1, c, 4))
                    parts_of(s, (2 * s if first_pair else 3 * s - 1) + k, c,
                             (name, da[name].unsqueeze(1))).then_inc(a3["staged"], 1)
                if not first_pair:
                    pool.wait_ge(a3["least"], at(8 * (s - 1), c, 16))
                nc.gpsimd.tensor_tensor(da["bias"][:, s, :], da["alibi"][:], column("slopes", at(s, c, 2)).to_broadcast([P, BAND]),
                                        ALU.mult).then_inc(a3["bias"], 1)

            def stage_v(s, c, base, n_split):
                if c is not None or base + s >= 2:
                    pool.wait_ge(a3["pv"], at(TB * (base + s - 1) + (s < 0), c, 2 * TB))
                cols = bass.ds(at((base + s) * P, c, 2 * P), P)
                parts_of(s % 2, n_split, c, ("v", da["v"][:, :, cols])).then_inc(a3["v_staged"], 1)

            stage_qk(0, None)
            stage_qk(1, None)
            stage_v(0, None, 0, 4)
            with pool.Fori(1, N_DIFF // 2) as c:
                for s in range(2):
                    stage_qk(s, c)
                    stage_v(s - 1, c, 0, 3 * s + 1)
            stage_v(1, None, N_DIFF - 2, 3 * N_DIFF - 1)
            sum_squares("ffn1")
            for c in range(0, KC, 2):
                pool.wait_ge(sq_ready, KC * NORM["final"] + c + 2)
                pair = final["squares"][:, c, :]
                nc.gpsimd.tensor_tensor(pair, pair, final["squares"][:, c + 1, :], ALU.add).then_inc(finals["pairs"], 1)

    return nc


def _tiles(w):
    k, n = w.shape
    return w.reshape(k // P, P, n // P, P).transpose(2, 1, 0, 3).reshape(n // P, P, -1)


def _rows(w, per_unit):
    k, n = w.shape
    return w.reshape(k // P // per_unit, per_unit, P, n).transpose(0, 2, 1, 3).reshape(-1, P, per_unit * n)


def _halves(w):
    return [_rows(w[:, h * S:(h + 1) * S], 2) for h in range(w.shape[1] // S)]


def _chunks(a):
    t, n = a.shape
    return a.T.reshape(n // P, P, t).transpose(1, 0, 2)


def _pairs(a, b):
    return np.stack([_tiles(a), _tiles(b)], 1).reshape(-1, P, a.shape[0])


def _columns(v):
    return v.reshape(-1, P).T


def _constants():
    con = np.zeros((P, N_CONSTS), np.float32)
    eye = np.eye(P, dtype=np.float32)
    con[:, CAT["ident"]:CAT["ident"] + P] = eye
    con[:, CAT["ones"]:CAT["ones"] + P] = 1.0
    perm = np.zeros((P, P), np.float32)
    half = ROPE_DIM // 2
    for h in range(P // HD):
        for f in range(half):
            perm[h * HD + f + half, h * HD + f] = -1.0
            perm[h * HD + f, h * HD + f + half] = 1.0
    con[:, CAT["rope_perm"]:CAT["rope_perm"] + P] = perm
    p, j = np.arange(P)[:, None], np.arange(P)[None, :]
    con[:, CAT["causal"]:CAT["causal"] + P] = np.where(j <= p, 0.0, MASKED)
    con[:, CAT["keep"]:CAT["keep"] + P] = p <= j
    for c in range(GC):
        for h in range(2):
            w = POOL_WINDOWS[2 * c + h]
            con[HD * h:HD * h + HD, CAT["inv_count"] + 16 * c:CAT["inv_count"] + 16 * c + 16] = \
                np.float32(1.0) / np.minimum(np.arange(16) + 1, w).astype(np.float32)
    con[:, CAT["pick"] + N_DIFF - 1] = 1.0
    dist = p + (S - P) - np.arange(BAND)[None, :]
    count = sum(((dist % d == 0) & (dist <= w)).astype(np.float64) for w, d in DILATED)
    count = np.where(dist >= 0, count, 0.0)
    dil = np.where(count > 0, -np.log(np.maximum(count, 1.0)), MASKED).astype(np.float32)
    alibi = np.where(dist >= 0, dist, MASKED).astype(np.float32)
    heads = np.zeros((P, N_FORGET, P), np.float32)
    for h in range(N_FORGET):
        heads[h, h, :] = 1.0
    picks = np.zeros((N_DIFF, N_DIFF, P), np.float32)
    for h in range(N_DIFF):
        picks[h, h, :] = 1.0
    return con, dil, alibi, heads.reshape(P, -1), picks.reshape(N_DIFF, -1)


def _lay_out(i):
    a = {n: np.asarray(v) for n, v in i.items()}
    w_in = a["w_in"][0]
    g3 = 3 * G
    gate0 = 9 * G
    gate = np.zeros((D, P), np.float32)
    gate[:, :N_FORGET] = w_in[:, gate0:gate0 + N_FORGET]
    conv = [w_in[:, k * G + c * P:k * G + (c + 1) * P] for c in range(GC) for k in range(3)]
    qk = [w_in[:, g3:g3 + 2 * G], w_in[:, 2 * g3:2 * g3 + 2 * G]]
    panels = np.concatenate([gate] + conv + [w_in[:, gate0 + N_FORGET:]] + qk, 1)
    values = np.concatenate([w_in[:, g3 + 2 * G:2 * g3], w_in[:, 2 * g3 + 2 * G:3 * g3]], 1)
    order = [0, 1, 6, 7, 2, 4, 3, 5]
    w_out = a["w_out"][0].reshape(KC, P, D)[order].reshape(D, D)
    up, xkv, kv, a_in = a["w_up"][0], a["w_xkv"][0], a["kv_w_2"], a["a_w_in_2"][0]
    gu, dn = a["ffn_w_gu_2"], a["ffn_w_down_2"]
    stream = [_tiles(panels), *_halves(values), _tiles(xkv[:, :D]), *_halves(xkv[:, D:]), _rows(w_out, 1),
              _tiles(a["w_xq"][0]), _rows(a["w_xo"][0], 1), _pairs(up[:, :FF], up[:, FF:]), _rows(a["w_down"][0], 1),
              *_halves(a_in[:, D:]), _tiles(a_in[:, :D]), _rows(a["a_w_out_2"][0], 1),
              _pairs(gu[0][:, :FF], gu[0][:, FF:]), _rows(dn[0], 1),
              *_halves(kv[:, D:]), _pairs(kv[:, :D], a["b_w_q_2"][0]), _rows(a["b_w_o_2"][0], 1),
              _pairs(gu[1][:, :FF], gu[1][:, FF:]), _rows(dn[1], 1)]
    weights = np.concatenate(stream, 0)
    par = np.zeros((P, N_PARAMS), np.float32)

    def put(name, cols):
        par[:cols.shape[0], AT[name]:AT[name] + cols.shape[1]] = cols

    for name, v in (("g_mix", a["g_mix"]), ("g_xa", a["g_xa"]), ("g_mem", a["g_mem"]), ("g_ffn", a["g_ffn"]),
                    ("a_norm", a["a_norm_2"]), ("ffn_norm0", a["ffn_norm_2"][0]), ("kv_norm", a["kv_norm_2"]),
                    ("b_norm", a["b_norm_2"]), ("ffn_norm1", a["ffn_norm_2"][1]), ("g_first", a["g_final"]), ("g_final", a["final_norm_2"]),
                    ("a_v_norm", a["a_v_norm_2"]), ("w_sconv", a["w_sconv"][0]), ("pool_scale", a["pool_scale"]),
                    ("w_ffconv", a["w_ffconv"][0]), ("b_subln", a["b_subln_2"])):
        put(name, _columns(v))
    put("b_forget", a["b_forget"].reshape(N_FORGET, 1))
    par[:, AT["eps"]] = EPS
    half = ROPE_DIM // 2
    freq = np.float32(ROPE_THETA) ** (-np.arange(0, ROPE_DIM, 2, dtype=np.float32) / np.float32(ROPE_DIM))
    for h in range(P // HD):
        for k in range(2):
            par[h * HD + k * half:h * HD + (k + 1) * half, AT["inv_freq"]] = freq
        for c in range(GC):
            par[HD * h:HD * h + HD, AT["inv_window"] + c] = 1.0 / POOL_WINDOWS[2 * c + h]
    par[:, AT["slopes"]:AT["slopes"] + N_DIFF] = 2.0 ** (-8.0 * (np.arange(N_DIFF) + 1) / N_DIFF)
    con, dil, alibi, heads, picks = _constants()
    blocks = np.zeros((P, GC, P), np.float32)
    for c in range(GC):
        for h in range(2):
            blocks[HD * h:HD * h + HD, c, HD * h:HD * h + HD] = a["w_pool"][0][2 * c + h]
    return {
        "weights": weights, "x_cols": _chunks(a["x"][0]), "mem_cols": _chunks(a["mem"][0]),
        "positions": np.broadcast_to(a["positions"], (P, S)), "params": par, "consts": con,
        "dil_table": dil, "head_rows": heads, "alibi_table": alibi, "head_picks": picks, "pool_blocks": blocks,
        "spatial": a["a_w_sp_2"][0].transpose(2, 0, 1).reshape(P, -1),
        "spatial_bias": np.broadcast_to(a["a_b_sp_2"][0].reshape(1, -1), (P, N_SPATIAL * P)),
        "lambdas": np.broadcast_to(a["b_lambda_2"][0].reshape(1, -1), (P, 4 * HD)),
    }


def kernel(**inputs):
    import concourse.bacc as bacc
    from concourse.bass_utils import run_bass_kernel_spmd as run

    nc = bacc.Bacc("TRN2", target_bir_lowering=False, num_devices=1)
    arrays, args = {}, {}
    for name, a in _lay_out(inputs).items():
        a = np.ascontiguousarray(a)
        arrays[f"in_{name}"] = a
        args[name] = nc.dram_tensor(f"in_{name}", a.shape, mybir.dt.from_np(a.dtype), kind="ExternalInput").ap()
    out = nc.dram_tensor("out_cols", (P, KC, S), F32, kind="ExternalOutput").ap()
    bass_two_blocks(nc, out=out, **args)
    got = run(nc, [arrays], core_ids=[0]).results[0]["out_cols"]
    return np.ascontiguousarray(got.transpose(2, 1, 0)).reshape(1, S, D)
```
